# Optimizing a Trainium2 kernel written in Bass

```python
import jax, jax.numpy as jnp
from jax import lax
import numpy as np
import math

D_MODEL = 1024
BATCH = 1
SEQ = 256
DEPTH = 2

CHUNK = 64
N_A_LAYERS = DEPTH // 2
N_B_LAYERS = DEPTH - N_A_LAYERS
MIX_WIDTH = D_MODEL
MEM_TOKENS = 256
MEM_HEADS = 4
MEM_WIDTH = D_MODEL // 4
MEM_HEAD_DIM = MEM_WIDTH // MEM_HEADS
A_WIDTH = MIX_WIDTH - MEM_WIDTH
A_HEADS = 4
A_HEAD_DIM = A_WIDTH // A_HEADS
A_CONV = 4
B_HEAD_DIM = 64
B_HEADS = A_WIDTH // B_HEAD_DIM
B_WIDTH = B_HEADS * B_HEAD_DIM
BAND_CHUNKS = 9
BAND = BAND_CHUNKS * CHUNK
KV_PAD = BAND - CHUNK
MAX_REL = 128
REL_SIZE = MAX_REL + CHUNK
D_FF = ((8 * D_MODEL // 3 + 127) // 128) * 128
FFN_CONV = 3
A_IN = 4 * A_WIDTH + 2 * A_HEADS + MEM_WIDTH
B_IN = B_WIDTH + MEM_WIDTH
EPS = 1e-6


def rmsnorm(x, g):
    x32 = x.astype(jnp.float32)
    y = x32 * lax.rsqrt(jnp.mean(x32 * x32, axis=-1, keepdims=True) + EPS)
    return (y * g.astype(jnp.float32)).astype(x.dtype)

def causal_dwconv(x, w, b):
    k = w.shape[0]
    s = x.shape[1]
    xp = jnp.pad(x, ((0, 0), (k - 1, 0), (0, 0)))
    y = xp[:, 0:s] * w[0]
    for j in range(1, k):
        y = y + xp[:, j:j + s] * w[j]
    return y + b

def mlstm_chunkwise(q, k, v, ig, logf):
    bsz, seq, nh, dh = q.shape
    nc = seq // CHUNK
    f32 = jnp.float32

    def to_chunks(t):
        t = t.astype(f32).reshape((bsz, nc, CHUNK) + t.shape[2:])
        perm = (1, 0, 3, 2) + tuple(range(4, t.ndim))
        return t.transpose(perm)

    qc, kc, vc = to_chunks(q), to_chunks(k * (dh ** -0.5)), to_chunks(v)
    igc, lfc = to_chunks(ig), to_chunks(logf)
    tril = jnp.tril(jnp.ones((CHUNK, CHUNK), dtype=bool))

    def step(carry, inp):
        c_st, n_st, m_st = carry
        qq, kk, vv, ii, lf = inp
        b = jnp.cumsum(lf, axis=-1)
        d = b[..., :, None] - b[..., None, :] + ii[..., None, :]
        d = jnp.where(tril, d, -jnp.inf)
        m_inter = b + m_st[..., None]
        m_t = jnp.maximum(m_inter, jnp.max(d, axis=-1))
        inter = jnp.exp(m_inter - m_t)
        s = jnp.einsum('bhtd,bhsd->bhts', qq, kk) * jnp.exp(d - m_t[..., None])
        num = jnp.einsum('bhts,bhse->bhte', s, vv) + inter[..., None] * jnp.einsum('bhtd,bhde->bhte', qq, c_st)
        den = jnp.sum(s, axis=-1) + inter * jnp.einsum('bhtd,bhd->bht', qq, n_st)
        h = num / jnp.maximum(jnp.abs(den), jnp.exp(-m_t))[..., None]
        b_last = b[..., -1]
        w = b_last[..., None] - b + ii
        m_new = jnp.maximum(b_last + m_st, jnp.max(w, axis=-1))
        w_exp = jnp.exp(w - m_new[..., None])
        decay = jnp.exp(b_last + m_st - m_new)
        c_new = decay[..., None, None] * c_st + jnp.einsum('bhs,bhsd,bhse->bhde', w_exp, kk, vv)
        n_new = decay[..., None] * n_st + jnp.einsum('bhs,bhsd->bhd', w_exp, kk)
        return (c_new, n_new, m_new), h

    init = (jnp.zeros((bsz, nh, dh, dh), f32), jnp.zeros((bsz, nh, dh), f32), jnp.zeros((bsz, nh), f32))
    _, h = lax.scan(step, init, (qc, kc, vc, igc, lfc))
    return h.transpose(1, 0, 3, 2, 4).reshape(bsz, seq, nh, dh)

def band_attention(q, k_pad, v_pad, rel_table):
    bsz, seq, _ = q.shape
    nc = seq // CHUNK
    q = q.reshape(bsz, seq, B_HEADS, B_HEAD_DIM)
    qi = jnp.arange(CHUNK)
    kj = jnp.arange(BAND)
    rel = KV_PAD + qi[:, None] - kj[None, :]
    idx = jnp.clip(rel, -(CHUNK - 1), MAX_REL) + (CHUNK - 1)
    bias = rel_table.astype(jnp.float32)[:, idx]
    scale = B_HEAD_DIM ** -0.5

    def one_chunk(c):
        start = c * CHUNK
        qc = lax.dynamic_slice_in_dim(q, start, CHUNK, axis=1)
        kc = lax.dynamic_slice_in_dim(k_pad, start, BAND, axis=1)
        vc = lax.dynamic_slice_in_dim(v_pad, start, BAND, axis=1)
        s = jnp.einsum('bqhd,bkhd->bhqk', qc, kc).astype(jnp.float32) * scale + bias
        valid = (start - KV_PAD + kj) >= 0
        s = jnp.where(valid, s, -jnp.inf)
        p = jax.nn.softmax(s, axis=-1).astype(vc.dtype)
        return jnp.einsum('bhqk,bkhd->bqhd', p, vc)

    out = lax.map(one_chunk, jnp.arange(nc))
    return out.transpose(1, 0, 2, 3, 4).reshape(bsz, seq, B_WIDTH)

def memory_attention(q, mem, w_kv):
    bsz, seq, _ = q.shape
    q = q.reshape(bsz, seq, MEM_HEADS, MEM_HEAD_DIM)
    mk, mv = jnp.split(mem @ w_kv, 2, axis=-1)
    mk = mk.reshape(bsz, -1, MEM_HEADS, MEM_HEAD_DIM)
    mv = mv.reshape(bsz, -1, MEM_HEADS, MEM_HEAD_DIM)
    s = jnp.einsum('bshd,bmhd->bhsm', q, mk).astype(jnp.float32) * (MEM_HEAD_DIM ** -0.5)
    p = jax.nn.softmax(s, axis=-1).astype(mv.dtype)
    return jnp.einsum('bhsm,bmhd->bshd', p, mv).reshape(bsz, seq, MEM_WIDTH)

def conv_ffn(h, w_up, conv_w, conv_b, w_down):
    u, g = jnp.split(h @ w_up, 2, axis=-1)
    g = causal_dwconv(g, conv_w, conv_b)
    return (jax.nn.silu(g) * u) @ w_down

def first_inputs(seed: int = 0) -> dict:
    key = jax.random.key(seed)
    ks = jax.random.split(key, 24)
    f32 = jnp.float32

    def nrm(k, shape, scale):
        return jax.random.normal(k, shape, f32) * scale

    gate_b = jnp.concatenate([
        nrm(ks[5], (N_A_LAYERS, A_HEADS), 0.1),
        jnp.linspace(3.0, 6.0, A_HEADS, dtype=f32)[None, :] + nrm(ks[6], (N_A_LAYERS, A_HEADS), 0.1),
    ], axis=-1)
    return {
        "x": nrm(ks[0], (BATCH, SEQ, D_MODEL), 1.0),
        "mem": nrm(ks[1], (BATCH, MEM_TOKENS, D_MODEL), 1.0),
        "norm_mix_g": 1.0 + nrm(ks[2], (DEPTH, D_MODEL), 0.1),
        "norm_ffn_g": 1.0 + nrm(ks[3], (DEPTH, D_MODEL), 0.1),
        "a_w_in": nrm(ks[4], (N_A_LAYERS, D_MODEL, A_IN), D_MODEL ** -0.5),
        "a_gate_b": gate_b,
        "a_conv_w": nrm(ks[7], (N_A_LAYERS, A_CONV, 2 * A_WIDTH), A_CONV ** -0.5),
        "a_conv_b": nrm(ks[8], (N_A_LAYERS, 2 * A_WIDTH), 0.02),
        "a_head_g": 1.0 + nrm(ks[9], (N_A_LAYERS, A_WIDTH), 0.1),
        "a_w_out": nrm(ks[10], (N_A_LAYERS, MIX_WIDTH, D_MODEL), MIX_WIDTH ** -0.5),
        "kv_norm_g": 1.0 + nrm(ks[11], (D_MODEL,), 0.1),
        "w_kv": nrm(ks[12], (D_MODEL, 2 * B_WIDTH), D_MODEL ** -0.5),
        "b_w_in": nrm(ks[13], (N_B_LAYERS, D_MODEL, B_IN), D_MODEL ** -0.5),
        "b_rel_bias": nrm(ks[14], (N_B_LAYERS, B_HEADS, REL_SIZE), 0.5),
        "b_w_out": nrm(ks[15], (N_B_LAYERS, MIX_WIDTH, D_MODEL), MIX_WIDTH ** -0.5),
        "mem_w_kv": nrm(ks[16], (DEPTH, D_MODEL, 2 * MEM_WIDTH), D_MODEL ** -0.5),
        "ffn_w_up": nrm(ks[17], (DEPTH, D_MODEL, 2 * D_FF), D_MODEL ** -0.5),
        "ffn_conv_w": nrm(ks[18], (DEPTH, FFN_CONV, D_FF), FFN_CONV ** -0.5),
        "ffn_conv_b": nrm(ks[19], (DEPTH, D_FF), 0.02),
        "ffn_w_down": nrm(ks[20], (DEPTH, D_FF, D_MODEL), D_FF ** -0.5),
        "final_g": 1.0 + nrm(ks[21], (D_MODEL,), 0.1),
    }

def first_block(x, mem, norm_mix_g, norm_ffn_g, a_w_in, a_gate_b, a_conv_w, a_conv_b, a_head_g, a_w_out,
              kv_norm_g, w_kv, b_w_in, b_rel_bias, b_w_out, mem_w_kv, ffn_w_up, ffn_conv_w, ffn_conv_b,
              ffn_w_down, final_g):
    bsz, seq, _ = x.shape
    k_pad = None
    v_pad = None
    for l in range(DEPTH):
        h = rmsnorm(x, norm_mix_g[l])
        if l < N_A_LAYERS:
            a = l
            proj = h @ a_w_in[a]
            qk, v, o, gates, q_mem = jnp.split(
                proj, [2 * A_WIDTH, 3 * A_WIDTH, 4 * A_WIDTH, 4 * A_WIDTH + 2 * A_HEADS], axis=-1)
            qk = jax.nn.silu(causal_dwconv(qk, a_conv_w[a], a_conv_b[a]))
            q, k = jnp.split(qk, 2, axis=-1)
            gates = gates.astype(jnp.float32) + a_gate_b[a].astype(jnp.float32)
            ig, fg = jnp.split(gates, 2, axis=-1)
            hm = mlstm_chunkwise(q.reshape(bsz, seq, A_HEADS, A_HEAD_DIM),
                                 k.reshape(bsz, seq, A_HEADS, A_HEAD_DIM),
                                 v.reshape(bsz, seq, A_HEADS, A_HEAD_DIM),
                                 ig, jax.nn.log_sigmoid(fg))
            hm = hm * lax.rsqrt(jnp.mean(hm * hm, axis=-1, keepdims=True) + EPS)
            hm = hm.reshape(bsz, seq, A_WIDTH) * a_head_g[a].astype(jnp.float32)
            mix_out = (hm * jax.nn.sigmoid(o.astype(jnp.float32))).astype(x.dtype)
            w_out = a_w_out[a]
        else:
            bl = l - N_A_LAYERS
            proj = h @ b_w_in[bl]
            q, q_mem = jnp.split(proj, [B_WIDTH], axis=-1)
            mix_out = band_attention(q, k_pad, v_pad, b_rel_bias[bl])
            w_out = b_w_out[bl]
        mem_out = memory_attention(q_mem, mem, mem_w_kv[l])
        x = x + jnp.concatenate([mix_out, mem_out], axis=-1) @ w_out
        x = x + conv_ffn(rmsnorm(x, norm_ffn_g[l]), ffn_w_up[l], ffn_conv_w[l], ffn_conv_b[l], ffn_w_down[l])
        if l == N_A_LAYERS - 1:
            ks_, vs_ = jnp.split(rmsnorm(x, kv_norm_g) @ w_kv, 2, axis=-1)
            pad = ((0, 0), (KV_PAD, 0), (0, 0), (0, 0))
            k_pad = jnp.pad(ks_.reshape(bsz, seq, B_HEADS, B_HEAD_DIM), pad)
            v_pad = jnp.pad(vs_.reshape(bsz, seq, B_HEADS, B_HEAD_DIM), pad)
    return rmsnorm(x, final_g)


D_FF_2 = 2816
N_NORMS = 6
HEAD_DIM = 64
CONV_CH = 512
CONV_K = 31
SWA_HQ = 8
SWA_HKV = 2
SWA_G = SWA_HQ // SWA_HKV
WINDOW = 128
BLK = 128
FOX_H = 16
AB_IN = 2 * CONV_CH + SWA_HQ * HEAD_DIM + 2 * SWA_HKV * HEAD_DIM
AB_OUT = CONV_CH + SWA_HQ * HEAD_DIM
FOX_IN = 3 * FOX_H * HEAD_DIM + FOX_H
FOX_OUT = FOX_H * HEAD_DIM
NEG = -1e30


def _rmsnorm(x, g):
    xf = x.astype(jnp.float32)
    y = xf * lax.rsqrt(jnp.mean(xf * xf, axis=-1, keepdims=True) + EPS)
    return (y * g.astype(jnp.float32)).astype(x.dtype)

def _swiglu(x, wg, wu, wd):
    return (jax.nn.silu(x @ wg) * (x @ wu)) @ wd

def _alibi_slopes(n):
    return jnp.asarray([2.0 ** (-8.0 * (i + 1) / n) for i in range(n)], dtype=jnp.float32)

def _conv_module(u, gate, w, b, ln_g, ln_b):
    a = u * jax.nn.sigmoid(gate)
    y = lax.conv_general_dilated(
        a, w.reshape(CONV_K, 1, CONV_CH).astype(a.dtype),
        window_strides=(1,), padding=[(CONV_K - 1, 0)],
        dimension_numbers=("NWC", "WIO", "NWC"),
        feature_group_count=CONV_CH) + b
    yf = y.astype(jnp.float32)
    mu = jnp.mean(yf, axis=-1, keepdims=True)
    var = jnp.mean(jnp.square(yf - mu), axis=-1, keepdims=True)
    yf = (yf - mu) * lax.rsqrt(var + EPS) * ln_g.astype(jnp.float32) + ln_b.astype(jnp.float32)
    return jax.nn.silu(yf).astype(u.dtype)

def _swa_sinks(q, k, v, sinks):
    b, s, _, dh = q.shape
    nb = s // BLK
    qb = q.reshape(b, nb, BLK, SWA_HKV, SWA_G, dh)
    kb = k.reshape(b, nb, BLK, SWA_HKV, dh)
    vb = v.reshape(b, nb, BLK, SWA_HKV, dh)
    pad = ((0, 0), (1, 0), (0, 0), (0, 0), (0, 0))
    kk = jnp.concatenate([jnp.pad(kb, pad)[:, :-1], kb], axis=2)
    vv = jnp.concatenate([jnp.pad(vb, pad)[:, :-1], vb], axis=2)
    sc = jnp.einsum("bnqhgd,bnkhd->bnhgqk", qb, kk).astype(jnp.float32) / math.sqrt(dh)
    t_loc = jnp.arange(BLK)[:, None]
    s_loc = jnp.arange(2 * BLK)[None, :]
    dist = t_loc + BLK - s_loc
    valid = (dist >= 0) & (dist < WINDOW)
    mask = valid[None] & ((jnp.arange(nb)[:, None, None] > 0) | (s_loc >= BLK)[None])
    slopes = _alibi_slopes(SWA_HQ).reshape(SWA_HKV, SWA_G)
    sc = sc - slopes[:, :, None, None] * dist.astype(jnp.float32)
    sc = jnp.where(mask[None, :, None, None], sc, NEG)
    sink = jnp.broadcast_to(sinks.astype(jnp.float32).reshape(SWA_HKV, SWA_G)[None, None, :, :, None, None],
                            sc.shape[:-1] + (1,))
    p = jax.nn.softmax(jnp.concatenate([sc, sink], axis=-1), axis=-1)[..., :-1]
    o = jnp.einsum("bnhgqk,bnkhd->bnqhgd", p.astype(v.dtype), vv)
    return o.reshape(b, s, SWA_HQ * dh)

def _fox_attention(q, k, v, zf, b_f):
    b, s, h, dh = q.shape
    nb = s // BLK
    qh = q.transpose(0, 2, 1, 3)
    kh = k.transpose(0, 2, 1, 3)
    vh = v.transpose(0, 2, 1, 3)
    logf = jax.nn.log_sigmoid(zf.astype(jnp.float32) + b_f.astype(jnp.float32))
    c = jnp.cumsum(logf.transpose(0, 2, 1), axis=-1)
    key_pos = jnp.arange(s)

    def one_block(i):
        start = i * BLK
        qs = lax.dynamic_slice_in_dim(qh, start, BLK, axis=2)
        cs = lax.dynamic_slice_in_dim(c, start, BLK, axis=2)
        sc = jnp.einsum("bhqd,bhkd->bhqk", qs, kh).astype(jnp.float32) / math.sqrt(dh)
        sc = sc + cs[..., :, None] - c[..., None, :]
        tpos = start + jnp.arange(BLK)
        sc = jnp.where(tpos[:, None] >= key_pos[None, :], sc, NEG)
        p = jax.nn.softmax(sc, axis=-1)
        return jnp.einsum("bhqk,bhkd->bhqd", p.astype(vh.dtype), vh)

    o = lax.map(one_block, jnp.arange(nb))
    return o.transpose(1, 0, 3, 2, 4).reshape(b, s, h * dh)

def _mixer_even(h, w_in, conv_w, conv_b, ln_g, ln_b, sinks, w_out):
    b, s, _ = h.shape
    z = h @ w_in
    o0 = CONV_CH
    o1 = o0 + CONV_CH
    o2 = o1 + SWA_HQ * HEAD_DIM
    o3 = o2 + SWA_HKV * HEAD_DIM
    u, gate = z[..., :o0], z[..., o0:o1]
    q = z[..., o1:o2].reshape(b, s, SWA_HQ, HEAD_DIM)
    k = z[..., o2:o3].reshape(b, s, SWA_HKV, HEAD_DIM)
    v = z[..., o3:].reshape(b, s, SWA_HKV, HEAD_DIM)
    a_out = _conv_module(u, gate, conv_w, conv_b, ln_g, ln_b)
    b_out = _swa_sinks(q, k, v, sinks)
    return jnp.concatenate([a_out, b_out], axis=-1) @ w_out

def _mixer_odd(h, w_in, b_f, w_out):
    b, s, _ = h.shape
    z = h @ w_in
    hd = FOX_H * HEAD_DIM
    q = z[..., :hd].reshape(b, s, FOX_H, HEAD_DIM)
    k = z[..., hd:2 * hd].reshape(b, s, FOX_H, HEAD_DIM)
    v = z[..., 2 * hd:3 * hd].reshape(b, s, FOX_H, HEAD_DIM)
    zf = z[..., 3 * hd:]
    return _fox_attention(q, k, v, zf, b_f) @ w_out

def second_inputs(seed: int = 0) -> dict:
    key = jax.random.key(seed)
    ks = jax.random.split(key, 16)
    n_even = (DEPTH + 1) // 2
    n_odd = DEPTH // 2
    f32 = jnp.float32
    nrm = lambda k, shp, fan: jax.random.normal(k, shp, f32) * fan ** -0.5
    return {
        "x": jax.random.normal(ks[0], (BATCH, SEQ, D_MODEL), f32),
        "norm_g": 1.0 + 0.05 * jax.random.normal(ks[1], (DEPTH, N_NORMS, D_MODEL), f32),
        "ffn_w_gate": nrm(ks[2], (DEPTH, 2, D_MODEL, D_FF_2), D_MODEL),
        "ffn_w_up": nrm(ks[3], (DEPTH, 2, D_MODEL, D_FF_2), D_MODEL),
        "ffn_w_down": nrm(ks[4], (DEPTH, 2, D_FF_2, D_MODEL), D_FF_2),
        "ab_w_in": nrm(ks[5], (n_even, D_MODEL, AB_IN), D_MODEL),
        "conv_w": nrm(ks[6], (n_even, CONV_K, CONV_CH), CONV_K),
        "conv_b": 0.02 * jax.random.normal(ks[7], (n_even, CONV_CH), f32),
        "conv_ln_g": 1.0 + 0.05 * jax.random.normal(ks[8], (n_even, CONV_CH), f32),
        "conv_ln_b": 0.02 * jax.random.normal(ks[9], (n_even, CONV_CH), f32),
        "swa_sinks": 0.5 * jax.random.normal(ks[10], (n_even, SWA_HQ), f32),
        "ab_w_out": nrm(ks[11], (n_even, AB_OUT, D_MODEL), AB_OUT),
        "fox_w_in": nrm(ks[12], (n_odd, D_MODEL, FOX_IN), D_MODEL),
        "fox_b_f": jax.random.uniform(ks[13], (n_odd, FOX_H), f32, 1.0, 6.0),
        "fox_w_out": nrm(ks[14], (n_odd, FOX_OUT, D_MODEL), FOX_OUT),
    }

def second_block(x, norm_g, ffn_w_gate, ffn_w_up, ffn_w_down, ab_w_in, conv_w, conv_b,
              conv_ln_g, conv_ln_b, swa_sinks, ab_w_out, fox_w_in, fox_b_f, fox_w_out):
    for l in range(DEPTH):
        g = norm_g[l]
        h = _swiglu(_rmsnorm(x, g[0]), ffn_w_gate[l, 0], ffn_w_up[l, 0], ffn_w_down[l, 0])
        x = x + 0.5 * _rmsnorm(h, g[1])
        h = _rmsnorm(x, g[2])
        if l % 2 == 0:
            i = l // 2
            h = _mixer_even(h, ab_w_in[i], conv_w[i], conv_b[i], conv_ln_g[i], conv_ln_b[i],
                            swa_sinks[i], ab_w_out[i])
        else:
            i = l // 2
            h = _mixer_odd(h, fox_w_in[i], fox_b_f[i], fox_w_out[i])
        x = x + _rmsnorm(h, g[3])
        h = _swiglu(_rmsnorm(x, g[4]), ffn_w_gate[l, 1], ffn_w_up[l, 1], ffn_w_down[l, 1])
        x = x + 0.5 * _rmsnorm(h, g[5])
    return x


def setup_inputs(seed=0):
    out = dict(first_inputs(seed))
    for name, value in second_inputs(seed + 1).items():
        if name != "x":
            out[name + "_2"] = value
    return out


def reference(
    x, mem, norm_mix_g, norm_ffn_g, a_w_in, a_gate_b, a_conv_w, a_conv_b, a_head_g, a_w_out,
    kv_norm_g, w_kv, b_w_in, b_rel_bias, b_w_out, mem_w_kv, ffn_w_up, ffn_conv_w, ffn_conv_b,
    ffn_w_down, final_g, norm_g_2, ffn_w_gate_2, ffn_w_up_2, ffn_w_down_2, ab_w_in_2, conv_w_2,
    conv_b_2, conv_ln_g_2, conv_ln_b_2, swa_sinks_2, ab_w_out_2, fox_w_in_2, fox_b_f_2,
    fox_w_out_2,
):
    x = first_block(
        x, mem, norm_mix_g, norm_ffn_g, a_w_in, a_gate_b, a_conv_w, a_conv_b, a_head_g, a_w_out,
        kv_norm_g, w_kv, b_w_in, b_rel_bias, b_w_out, mem_w_kv, ffn_w_up, ffn_conv_w,
        ffn_conv_b, ffn_w_down, final_g,
    )
    return second_block(
        x, norm_g_2, ffn_w_gate_2, ffn_w_up_2, ffn_w_down_2, ab_w_in_2, conv_w_2, conv_b_2,
        conv_ln_g_2, conv_ln_b_2, swa_sinks_2, ab_w_out_2, fox_w_in_2, fox_b_f_2, fox_w_out_2,
    )


_drawn_inputs = setup_inputs


def setup_inputs(seed=0):
    import zlib

    import numpy as np

    out = dict(_drawn_inputs(seed))
    spreads = {}
    factors = {'a_conv_b': 5.126, 'ffn_conv_b': 3.146, 'conv_ln_b_2': 3.628}
    for name, (base, spread) in spreads.items():
        noise = np.random.default_rng([zlib.crc32(name.encode()), seed]).standard_normal(out[name].shape)
        drawn = base * np.exp(spread * noise) if base else spread * noise
        out[name] = __import__('jax').numpy.asarray(drawn.astype(out[name].dtype))
    for name, factor in factors.items():
        out[name] = (out[name] * factor).astype(out[name].dtype)
    return out
```

```python
from contextlib import ExitStack

import concourse.bass as bass
from concourse import mybir

F32 = mybir.dt.float32
F32R = mybir.dt.float32r
BF16 = mybir.dt.bfloat16
ALU = mybir.AluOpType
ACT = mybir.ActivationFunctionType
AXX = mybir.AxisListType.X

P = 128
D = 1024
NCH = D // P
SEQ = 256
NTB = SEQ // P
COLS = 256
RING = 3
SLOTW = NCH * COLS
EPS = 1e-6

DFF = 2816
STEPS = DFF // COLS
FCH = DFF // P

A_WIDTH = 768
A_HEADS = 4
A_DH = A_WIDTH // A_HEADS
A_CONV = 4
ACH = A_WIDTH // P
VA = A_DH + 1
DH = 64
B_HEADS = 12
REL = 192
MAX_REL = 128
CHUNK = 64
MEM_HEADS = 4
MCH = 2
CONV_K = 31
CCH = 4
SWA_HQ = 8
FOX_H = 16
WINDOW = 128
NEG = -1e30
CAUSAL = 3 * P

T_MEM = 0
T_AQK = T_MEM + 4
T_AV = T_AQK + 6
T_AO = T_AV + 3
T_AQM = T_AO + 3
T_AOUT = T_AQM + 1
T_FF0 = T_AOUT + 4
FFN_SLOTS = 3 * STEPS
T_KV = T_FF0 + FFN_SLOTS
T_BIN = T_KV + 6
T_BOUT = T_BIN + 4
T_FF1 = T_BOUT + 4
T_FF2 = T_FF1 + FFN_SLOTS
T_AB = T_FF2 + FFN_SLOTS
T_ABOUT = T_AB + 7
T_FF3 = T_ABOUT + 4
T_FF4 = T_FF3 + FFN_SLOTS
T_FOX = T_FF4 + FFN_SLOTS
T_FOXOUT = T_FOX + 12
T_FF5 = T_FOXOUT + 4
SLOTS = T_FF5 + FFN_SLOTS
FFN_AT = [T_FF0, T_FF1, T_FF2, T_FF3, T_FF4, T_FF5]

PARAM_TILES = 5
C_MIX, C_FFN, C_KV, C_FINAL, C_ACW, C_ACB, C_AHG = 0, 16, 32, 40, 48, 96, 108
C_NG2, C_LNG, C_LNB = 128, 224, 228
C_FCW = [256, 384]
C_FCB = [256 + 66, 384 + 66]
C_CW, C_CB = 512, 636


def a_head_rows(h):
    at, left, out = h * A_DH, A_DH, []
    while left:
        n = min(left, P - at % P)
        out.append((at // P, at % P, n))
        at, left = at + n, left - n
    return out


def softmax_heads():
    return {
        "a_mem": [("mem0", h, 6 + h // 2) for h in range(MEM_HEADS)],
        "band": [("band", h, h // 2) for h in range(B_HEADS)] + [("mem1", h, 6 + h // 2) for h in range(MEM_HEADS)],
        "swa": [("swa", h, 4 + h // 2) for h in range(SWA_HQ)],
        "fox": [("fox", h, h // 2) for h in range(FOX_H)],
    }


HEADS = softmax_heads()
HEAD0 = {"a_mem": 0, "band": 4, "swa": 20, "fox": 28}


def build(nc, x, mem, norm_mix_g, norm_ffn_g, a_w_in, a_gate_b, a_conv_w, a_conv_b, a_head_g, a_w_out,
          kv_norm_g, w_kv, b_w_in, b_rel_bias, b_w_out, mem_w_kv, ffn_w_up, ffn_conv_w, ffn_conv_b,
          ffn_w_down, final_g, norm_g_2, ffn_w_gate_2, ffn_w_up_2, ffn_w_down_2, ab_w_in_2, conv_w_2,
          conv_b_2, conv_ln_g_2, conv_ln_b_2, swa_sinks_2, ab_w_out_2, fox_w_in_2, fox_b_f_2,
          fox_w_out_2, out):
    ctx = ExitStack()
    with ctx:
        def sb(name, shape, dt=F32):
            return ctx.enter_context(nc.sbuf_tensor(name, shape, dt))

        def sem(name):
            return ctx.enter_context(nc.semaphore(name))

        raw = sb("raw", [P, RING, SLOTW])
        w_hi = sb("w_hi", [P, RING, SLOTW], F32R)
        w_lo = sb("w_lo", [P, RING, SLOTW], F32R)
        xT = sb("xT", [P, NCH, SEQ])
        act_hi = sb("act_hi", [P, NCH, SEQ], F32R)
        act_lo = sb("act_lo", [P, NCH, SEQ], F32R)
        nrm = sb("nrm", [P, NCH, SEQ])
        rstd = sb("rstd", [P, SEQ])
        gate_acc = sb("gate_acc", [P, 2, SEQ])
        gate_act = sb("gate_act", [P, 2, SEQ])
        hid = sb("hid", [P, 2, SEQ])
        hid_hi = sb("hid_hi", [P, 2, SEQ], F32R)
        hid_lo = sb("hid_lo", [P, 2, SEQ], F32R)
        qk = sb("qk", [P, 16, SEQ])
        vals = sb("vals", [P, NTB * D])
        qm = sb("qm", [P, MCH, SEQ])
        mk = sb("mk", [P, 2, MCH, SEQ])
        mv = sb("mv", [P, 2, NTB, MCH * P])
        aux = sb("aux", [P, B_HEADS * CAUSAL])
        s_sb = sb("s_sb", [P, 2, 512])
        p_sb = sb("p_sb", [P, 2, 512])
        pt_sb = sb("pt_sb", [P, 2, 512])
        sel = sb("sel", [FOX_H, FOX_H, P])
        ident = sb("ident", [P, P])
        mean_w = sb("mean_w", [P, P])
        mean_c = sb("mean_c", [P, P])
        turn8 = sb("turn8", [P, P])
        tri = sb("tri", [P, 2 * P])
        causal = sb("causal", [P, CAUSAL])
        dist = sb("dist", [P, CAUSAL])
        eps = sb("eps", [P, 1])
        zero = sb("zero", [P, 512], BF16)
        par = sb("par", [P, PARAM_TILES * P])
        gate_b = sb("gate_b", [P, 2 * A_HEADS])
        fox_b = sb("fox_b", [P, FOX_H])
        sink = sb("sink", [P, SWA_HQ])
        nsink8 = sb("nsink8", [P, SWA_HQ])
        gw = sb("gw", [P, NCH, FOX_H])
        gw_hi = sb("gw_hi", [P, NCH, FOX_H], F32R)
        gw_lo = sb("gw_lo", [P, NCH, FOX_H], F32R)
        z_sb = sb("z_sb", [P, NTB, FOX_H])
        za_sb = sb("za_sb", [P, NTB, FOX_H])
        lf_sb = sb("lf_sb", [P, NTB, FOX_H])
        c_sb = sb("c_sb", [P, NTB, FOX_H])
        rowc = sb("rowc", [FOX_H, SEQ])
        cum = sb("cum", [A_HEADS, 2, P + SEQ])
        a_tok = sb("a_tok", [P, NTB, A_HEADS])
        emm = sb("emm", [P, NTB, A_HEADS])
        small = sb("small", [P, 2, 8])
        tab = sb("tab", [B_HEADS, REL])
        tabr = sb("tabr", [B_HEADS, 512])
        tab_dram = nc.dram_tensor("tab_dram", [B_HEADS, 512], F32, kind="Internal").ap()

        oT = aux[:, 0:ACH * SEQ].rearrange("p (c t) -> p c t", c=ACH)
        hm = aux[:, ACH * SEQ:ACH * SEQ + NTB * A_WIDTH].rearrange("p (b f) -> p b f", b=NTB)
        relb = aux[:, :].rearrange("p (h k) -> p h k", h=B_HEADS)
        PADW = CONV_K - 1 + SEQ
        apad = aux[:, 0:CCH * PADW].rearrange("p (c t) -> p c t", c=CCH)
        cv = aux[:, CCH * PADW:CCH * PADW + CCH * SEQ].rearrange("p (c t) -> p c t", c=CCH)
        csg = aux[:, CCH * (PADW + SEQ):CCH * (PADW + 2 * SEQ)].rearrange("p (c t) -> p c t", c=CCH)
        prow = aux[:, 0:PARAM_TILES * P].rearrange("p (n q) -> p n q", n=PARAM_TILES)
        kswap = gate_acc[:, 0, :]
        vaug = vals[:, 0:NTB * A_HEADS * VA].rearrange("p (b h e) -> p b h e", b=NTB, h=A_HEADS)
        vtok = vals[:, :].rearrange("p (b f) -> p b f", b=NTB)

        acc = [ctx.enter_context(nc.psum_tensor(f"acc{j}", [P, 512], F32)) for j in range(4)]
        pj = [ctx.enter_context(nc.psum_tensor(f"pj{j}", [P, 512], F32)) for j in range(RING)]
        st = ctx.enter_context(nc.psum_tensor("st", [P, 512], F32))

        raw_landed = [sem(f"raw_landed{r}") for r in range(RING)]
        hi_done = sem("hi_done")
        lo_done = sem("lo_done")
        w_used = sem("w_used")
        evac_act = sem("evac_act")
        evac_dve = sem("evac_dve")
        params_in = sem("params_in")
        tokens_in = [sem("mem_in"), sem("x_in")]
        small_in = sem("small_in")
        gw_in = sem("gw_in")
        consts = sem("consts")
        vec_const = sem("vec_const")
        in_t = sem("in_t")
        mem_hi = sem("mem_hi")
        mem_lo = sem("mem_lo")
        par_ready = sem("par_ready")
        x_ready = sem("x_ready")
        sq_done = sem("sq_done")
        stat = sem("stat")
        std_done = sem("std_done")
        xn_done = sem("xn_done")
        act_hi_done = sem("act_hi_done")
        act_lo_done = sem("act_lo_done")
        ff_gate = sem("ff_gate")
        ff_tap = sem("ff_tap")
        ff_conv = sem("ff_conv")
        ff_act = sem("ff_act")
        ff_hid = sem("ff_hid")
        ff_hi = sem("ff_hi")
        ff_lo = sem("ff_lo")
        qk_tap = sem("qk_tap")
        qk_conv = sem("qk_conv")
        qk_act = sem("qk_act")
        h_s = sem("h_s")
        h_max = sem("h_max")
        h_exp = sem("h_exp")
        h_p = sem("h_p")
        h_pt = sem("h_pt")
        h_ptc = sem("h_ptc")
        h_o = sem("h_o")
        h_ohi = sem("h_ohi")
        h_olo = sem("h_olo")
        dve_step = sem("dve_step")
        gates_ps = sem("gates_ps")
        gw_split = sem("gw_split")
        gates_z = sem("gates_z")
        gates_e = sem("gates_e")
        gates_lf = sem("gates_lf")
        gates_c = sem("gates_c")
        gates_a = sem("gates_a")
        gates_t = sem("gates_t")
        gates_m = sem("gates_m")
        gates_mt = sem("gates_mt")
        gates_mm = sem("gates_mm")
        gates_em = sem("gates_em")
        ml_bc = sem("ml_bc")
        ml_x = sem("ml_x")
        ml_e = sem("ml_e")
        ml_mask = sem("ml_mask")
        ml_s = sem("ml_s")
        ml_p = sem("ml_p")
        ml_num = sem("ml_num")
        ml_h = sem("ml_h")
        ml_ss = sem("ml_ss")
        ml_std = sem("ml_std")
        ml_hn = sem("ml_hn")
        ml_t = sem("ml_t")
        ml_y = sem("ml_y")
        ml_yhi = sem("ml_yhi")
        ml_ylo = sem("ml_ylo")
        tabr_ready = sem("tabr_ready")
        tab_out = sem("tab_out")
        relb_in = sem("relb_in")
        kswap_in = sem("kswap_in")
        k_ready = sem("k_ready")
        cv_sg = sem("cv_sg")
        cv_pad = sem("cv_pad")
        cv_y = sem("cv_y")
        cv_mu = sem("cv_mu")
        cv_c = sem("cv_c")
        cv_sq = sem("cv_sq")
        cv_var = sem("cv_var")
        cv_std = sem("cv_std")
        cv_z = sem("cv_z")
        cv_silu = sem("cv_silu")
        cv_hi = sem("cv_hi")
        cv_lo = sem("cv_lo")
        v_ones = sem("v_ones")
        out_t = sem("out_t")
        out_sb = sem("out_sb")
        stored = sem("stored")

        block = ctx.enter_context(nc.Block())

        def cols(c0, c=0, n=1):
            return par[:, c0 + c:c0 + c + n]

        evac_of = {}
        counts = {"A": 0, "D": 0}
        parts = [(T_MEM, 4, "D"), (T_AQK, 6, "D"), (T_AV, 3, "D"), (T_AO, 3, "A"), (T_AQM, 1, "D"),
                 (T_KV, 6, "D"), (T_BIN, 4, "D"), (T_AB, 2, "A"), (T_AB + 2, 5, "D"), (T_FOX, 12, "D")]
        for first, n, who in parts:
            for t in range(first, first + n):
                counts[who] += 1
                evac_of[t] = (who, counts[who])

        def evacuated(eng, t):
            who, n = evac_of[t]
            eng.wait_ge(evac_act if who == "A" else evac_dve, n)

        def up_view(w):
            return w.rearrange("(c p) n -> p c n", p=P)

        @block.sync
        def _(sp):
            def load(base, src, i=0):
                r = base % RING
                if base >= RING:
                    sp.wait_ge(lo_done, base + RING * i - RING + 1)
                dst = raw[:, r, :].rearrange("p (c n) -> p c n", c=src.shape[1])
                sp.dma_start(dst, src).then_inc(raw_landed[r], 16)

            def project(first, w, starts):
                v = up_view(w)
                for j, n0 in enumerate(starts):
                    load(first + j, v[:, :, n0:n0 + COLS])

            def ffn(t0, w_gate, g0, w_up, u0, w_down):
                gv, uv = up_view(w_gate), up_view(w_up)
                dv = w_down.rearrange("(s c p) n -> s p c n", c=2, p=P)
                load(t0, gv[:, :, g0:g0 + COLS])
                load(t0 + 1, uv[:, :, u0:u0 + COLS])
                g_rest, u_rest = gv[:, :, g0 + COLS:g0 + DFF], uv[:, :, u0 + COLS:u0 + DFF]
                with sp.Fori(1, STEPS) as i:
                    load(t0 - 1, g_rest[:, :, bass.ds((i - 1) * COLS, COLS)], i)
                    load(t0, u_rest[:, :, bass.ds((i - 1) * COLS, COLS)], i)
                    load(t0 + 1, w_down[bass.ds((i - 1) * COLS, COLS), :].rearrange("(c p) n -> p c n", p=P), i)
                load(t0 + RING * STEPS - 1, dv[STEPS - 1])

            def even(n, start=0, step=COLS):
                return [start + step * j for j in range(n)]

            sp.dma_start(qk[:, 0:8, :].rearrange("p (b c) t -> p b (c t)", b=NTB),
                         mem[0].rearrange("(b p) d -> p b d", p=P)).then_inc(tokens_in[0], 16)
            project(T_MEM, mem_w_kv[0], even(2))
            load(T_MEM + 2, up_view(mem_w_kv[1])[:, :, 0:COLS])
            sp.dma_start(qk[:, 8:16, :].rearrange("p (b c) t -> p b (c t)", b=NTB),
                         x[0].rearrange("(b p) d -> p b d", p=P)).then_inc(tokens_in[1], 16)
            load(T_MEM + 3, up_view(mem_w_kv[1])[:, :, COLS:2 * COLS])
            sp.dma_start(gw[:, :, 0:8], up_view(a_w_in[0])[:, :, 3072:3080]).then_inc(gw_in, 16)
            project(T_AQK, a_w_in[0], even(6 + 3 + 3) + [4 * A_WIDTH + 2 * A_HEADS])
            sp.wait_ge(tabr_ready, 1)
            sp.dma_start(tab_dram, tabr[:, :]).then_inc(tab_out, 16)
            project(T_AOUT, a_w_out[0], even(4))
            ffn(T_FF0, ffn_w_up[0], DFF, ffn_w_up[0], 0, ffn_w_down[0])
            sp.wait_ge(x_ready, 2 * NCH)
            sp.wait_ge(tab_out, 16)
            sp.dma_start(relb[:, :, 0:P],
                         bass.AP(tensor=tab_dram.tensor, offset=P, ap=[[1, P], [512, B_HEADS], [1, P]])).then_inc(relb_in, 16)
            sp.dma_start(relb[:, :, P:CAUSAL],
                         bass.AP(tensor=tab_dram.tensor, offset=0, ap=[[1, P], [512, B_HEADS], [1, 2 * P]])).then_inc(relb_in, 16)
            sp.dma_start(gw[:, :, :], up_view(fox_w_in_2[0])[:, :, 3072:3088]).then_inc(gw_in, 16)
            project(T_KV, w_kv, even(6))
            project(T_BIN, b_w_in[0], even(4))
            project(T_BOUT, b_w_out[0], even(4))
            ffn(T_FF1, ffn_w_up[1], DFF, ffn_w_up[1], 0, ffn_w_down[1])
            ffn(T_FF2, ffn_w_gate_2[0, 0], 0, ffn_w_up_2[0, 0], 0, ffn_w_down_2[0, 0])
            project(T_AB, ab_w_in_2[0], [512, 768, 0, 256, 1024, 1280, 1536])
            load(T_ABOUT, up_view(ab_w_out_2[0])[:, :, 0:COLS])
            load(T_ABOUT + 1, up_view(ab_w_out_2[0])[:, :, COLS:2 * COLS])
            sp.wait_ge(k_ready, 1)
            sp.dma_start(kswap[0:64, :], qk[64:128, 4, :]).then_inc(kswap_in, 16)
            sp.dma_start(kswap[64:128, :], qk[0:64, 4, :]).then_inc(kswap_in, 16)
            load(T_ABOUT + 2, up_view(ab_w_out_2[0])[:, :, 2 * COLS:3 * COLS])
            load(T_ABOUT + 3, up_view(ab_w_out_2[0])[:, :, 3 * COLS:4 * COLS])
            ffn(T_FF3, ffn_w_gate_2[0, 1], 0, ffn_w_up_2[0, 1], 0, ffn_w_down_2[0, 1])
            ffn(T_FF4, ffn_w_gate_2[1, 0], 0, ffn_w_up_2[1, 0], 0, ffn_w_down_2[1, 0])
            project(T_FOX, fox_w_in_2[0], even(12))
            project(T_FOXOUT, fox_w_out_2[0], even(4))
            ffn(T_FF5, ffn_w_gate_2[1, 1], 0, ffn_w_up_2[1, 1], 0, ffn_w_down_2[1, 1])
            for b in range(NTB):
                sp.wait_ge(out_sb, 2 * (b + 1))
                sp.dma_start(out[0, b * P:(b + 1) * P, :],
                             qk[:, 4 * b:4 * b + 4, :].rearrange("p c t -> p (c t)")).then_inc(stored, 16)
            sp.wait_ge(stored, 16 * NTB)

        @block.gpsimd
        def _(pool):
            rows = [(norm_mix_g, 0, 0, 16), (norm_ffn_g, 0, 16, 16), (kv_norm_g, 0, 32, 8), (final_g, 0, 40, 8),
                    (a_conv_w, 0, 48, 48), (a_conv_b, 0, 96, 12), (a_head_g, 0, 108, 6),
                    (norm_g_2, 1, 0, 96), (conv_ln_g_2, 1, 96, 4), (conv_ln_b_2, 1, 100, 4),
                    (ffn_conv_w[0], 2, 0, 66), (ffn_conv_b[0], 2, 66, 22),
                    (ffn_conv_w[1], 3, 0, 66), (ffn_conv_b[1], 3, 66, 22),
                    (conv_w_2, 4, 0, 124), (conv_b_2, 4, 124, 4)]
            nc.gpsimd.memset(prow[:, :, :], 0.0).then_inc(consts, 1)
            nc.gpsimd.memset(ident[:, :], 0.0).then_inc(consts, 1)
            nc.gpsimd.memset(mean_w[:, :], 1.0 / D)
            nc.gpsimd.memset(mean_c[:, :], 1.0 / (CCH * P))
            nc.gpsimd.memset(tri[:, :], 1.0)
            nc.gpsimd.memset(causal[:, :], 0.0)
            nc.gpsimd.memset(sel[:, :, :], 0.0)
            nc.gpsimd.memset(turn8[:, :], 0.0)
            nc.gpsimd.memset(zero[:, :], 0.0)
            nc.gpsimd.memset(eps[:, :], EPS)
            nc.gpsimd.memset(cum[:, :, :], 0.0)
            nc.gpsimd.memset(vaug[:, :, :, A_DH:VA], 1.0)
            nc.gpsimd.iota(dist[:, 0:P], [[-1, P]], base=0, channel_multiplier=1, allow_small_or_imprecise_dtypes=True)
            nc.gpsimd.iota(dist[:, P:CAUSAL], [[-1, 2 * P]], base=P, channel_multiplier=1,
                           allow_small_or_imprecise_dtypes=True).then_inc(consts, 1)
            pool.wait_ge(consts, 3)
            for src, tile, at, n in rows:
                dims = "abc"[:len(src.shape) - 1]
                v = src.rearrange(f"{' '.join(dims)} (r q) -> ({' '.join(dims)} r) q".replace("()", ""), q=P) if dims else \
                    src.rearrange("(r q) -> r q", q=P)
                pool.dma_start(prow[at:at + n, tile, :], v).then_inc(params_in, 16)

            def spread(vec, n):
                return bass.AP(tensor=vec.tensor, offset=vec.offset, ap=[[0, P], [1, n]])

            pool.dma_start(gate_b[:, :], spread(a_gate_b, 8)).then_inc(small_in, 16)
            pool.dma_start(fox_b[:, :], spread(fox_b_f_2, FOX_H)).then_inc(small_in, 16)
            pool.dma_start(sink[:, :], spread(swa_sinks_2, SWA_HQ)).then_inc(small_in, 16)
            pool.dma_start(tab[:, :], b_rel_bias[0]).then_inc(small_in, 16)
            nc.gpsimd.affine_select(out=ident[:, :], in_=ident[:, :], compare_op=ALU.not_equal, fill=1.0,
                                    base=0, pattern=[[-1, P]], channel_multiplier=1).then_inc(consts, 1)
            nc.gpsimd.affine_select(out=turn8[:, :], in_=turn8[:, :], compare_op=ALU.not_equal, fill=DH ** 0.5,
                                    base=1 - P, pattern=[[1, P]], channel_multiplier=1).then_inc(consts, 1)
            nc.gpsimd.affine_select(out=tri[:, 0:P], in_=tri[:, 0:P], compare_op=ALU.is_ge, fill=0.0,
                                    base=0, pattern=[[1, P]], channel_multiplier=-1).then_inc(consts, 1)
            nc.gpsimd.affine_select(out=sel[:, :, :], in_=sel[:, :, :], compare_op=ALU.not_equal, fill=1.0,
                                    base=0, pattern=[[-1, FOX_H], [0, P]], channel_multiplier=1).then_inc(consts, 1)
            nc.gpsimd.affine_select(out=causal[:, :].rearrange("p (a k) -> p a k", a=3)[:, 0:3:2, :],
                                    in_=causal[:, :].rearrange("p (a k) -> p a k", a=3)[:, 0:3:2, :],
                                    compare_op=ALU.is_ge, fill=NEG, base=0, pattern=[[0, 2], [-1, P]],
                                    channel_multiplier=1).then_inc(consts, 1)
            dv = dist[:, :].rearrange("p (a k) -> p a k", a=3)[:, 0:3:2, :]
            nc.gpsimd.affine_select(out=dv, in_=dv, compare_op=ALU.is_ge, fill=-NEG, base=0,
                                    pattern=[[0, 2], [-1, P]], channel_multiplier=1).then_inc(consts, 1)
            nc.gpsimd.affine_select(out=dist[:, P:2 * P], in_=dist[:, P:2 * P], compare_op=ALU.is_gt, fill=-NEG,
                                    base=0, pattern=[[1, P]], channel_multiplier=-1).then_inc(consts, 1)
            for h in range(A_HEADS):
                pool.wait_ge(ml_e, h + 1)
                ev = s_sb[:, h % 2, 0:CAUSAL].rearrange("p (a k) -> p a k", a=3)[:, 0:3:2, :]
                nc.gpsimd.affine_select(out=ev, in_=ev, compare_op=ALU.is_ge, fill=0.0, base=0,
                                        pattern=[[0, 2], [1, P]], channel_multiplier=-1).then_inc(ml_mask, 1)
            pool.wait_ge(relb_in, 32)
            for half in (0, 2):
                v = relb[CHUNK:P, :, half * P + CHUNK:(half + 1) * P]
                ins = nc.gpsimd.memset(v, NEG)
            ins.then_inc(vec_const, 1)
            pool.wait_ge(x_ready, 4 * NCH)
            nc.gpsimd.memset(apad[:, :, 0:CONV_K - 1], 0.0).then_inc(vec_const, 1)

        @block.scalar
        def _(act):
            def split_hi(base, i=0):
                if isinstance(i, int) and base + RING * i >= SLOTS:
                    return
                r = base % RING
                act.wait_ge(raw_landed[r], 16 * (base // RING + i) + 16)
                if base >= RING:
                    act.wait_ge(w_used, base + RING * i - RING + 1)
                nc.scalar.copy(w_hi[:, r, :], raw[:, r, :]).then_inc(hi_done, 1)

            def deviation(n):
                act.wait_ge(stat, n + 1)
                nc.scalar.activation(rstd[:, :], st[:, 0:SEQ], ACT.Sqrt, bias=eps[:, :]).then_inc(std_done, 1)

            def squares(n, u):
                for c in range(NCH):
                    act.wait_ge(x_ready, NCH * u + c + 1)
                    nc.scalar.activation(nrm[:, c, :], xT[:, c, :], ACT.Square).then_inc(sq_done, 1)
                deviation(n)

            def post_squares(n, t_last):
                act.wait_ge(w_used, t_last + 1)
                for j in range(4):
                    nc.scalar.activation(nrm[:, 2 * j:2 * j + 2, :], acc[j][:, :], ACT.Square).then_inc(sq_done, 2)
                deviation(n)

            def apply_hi(a):
                for c in range(NCH):
                    act.wait_ge(xn_done, NCH * a + c + 1)
                    nc.scalar.copy(act_hi[:, c, :], nrm[:, c, :]).then_inc(act_hi_done, 1)

            def ffn(f, conv):
                t0 = FFN_AT[f]

                def gate(t, s, i=0):
                    split_hi(t + 2, i)
                    bank = pj[t % RING]
                    act.wait_ge(w_used, t + RING * i + 1)
                    if conv:
                        act.wait_ge(ff_act, STEPS * f + s) if f or not isinstance(s, int) else act.wait_ge(qk_act, ACH)
                        for j in range(2):
                            w2 = par[:, bass.ds(C_FCW[f] + 2 * FCH + 2 * s + j, 1)]
                            bb = par[:, bass.ds(C_FCB[f] + 2 * s + j, 1)]
                            nc.scalar.activation(gate_acc[:, j, :], bank[:, j * SEQ:(j + 1) * SEQ], ACT.Identity,
                                                 bias=bb, scale=w2).then_inc(ff_gate, 1)
                        act.wait_ge(ff_conv, STEPS * f + s + 1)
                    if f or not isinstance(s, int):
                        act.wait_ge(ff_hid, STEPS * f + s)
                    src = gate_acc[:, :, :] if conv else bank[:, :].rearrange("p (j t) -> p j t", j=2)
                    nc.scalar.activation(gate_act[:, :, :], src, ACT.Silu).then_inc(ff_act, 1)

                def up_hi(s):
                    act.wait_ge(ff_hid, STEPS * f + s + 1)
                    nc.scalar.copy(hid_hi[:, :, :], hid[:, :, :]).then_inc(ff_hi, 1)

                gate(t0, 0)
                split_hi(t0 + 3)
                up_hi(0)

                def one(i):
                    gate(t0 - 1, i, i)
                    split_hi(t0 + 2, i)
                    split_hi(t0 + 3, i)
                    act.wait_ge(w_used, t0 + 2 + RING * i)
                    up_hi(i)

                alone = t0 + FFN_SLOTS == SLOTS
                with act.Fori(1, STEPS - alone) as i:
                    one(i)
                if alone:
                    one(STEPS - 1)
                split_hi(t0 + RING * STEPS + 1)

            def projection(first, n, take=None):
                for t in range(first, first + n):
                    split_hi(t + 2)
                    if take:
                        act.wait_ge(w_used, t + 1)
                        take(t, t - first)

            def exps(phase, n):
                kind, h, _ = HEADS[phase][n]
                g = HEAD0[phase] + n
                src = pj[g % 2] if kind[:3] in ("mem", "ban") else s_sb[:, g % 2, :]
                act.wait_ge(h_max, g + 1)
                if g >= 2:
                    act.wait_ge(h_pt, g - 1)
                cuts = [(0, 256), (256, 512)] if kind.startswith("mem") else [(0, 128), (128, 384)]
                for b, (lo, hi) in enumerate(cuts):
                    ins = nc.scalar.activation(p_sb[:, g % 2, lo:hi], src[:, lo:hi], ACT.Exp, bias=small[:, g % 2, b:b + 1],
                                               scale=DH ** -0.5, accum_out=small[:, g % 2, 2 + b:3 + b])
                if kind == "swa":
                    ins = nc.scalar.activation(small[:, g % 2, 4:6], small[:, g % 2, 0:2], ACT.Exp, bias=sink[:, h:h + 1])
                ins.then_inc(h_exp, 1)

            def pt_copy(phase, n):
                kind, h, _ = HEADS[phase][n]
                g = HEAD0[phase] + n
                width = 512 if kind.startswith("mem") else CAUSAL
                act.wait_ge(h_pt, g + 1)
                if g >= 2:
                    act.wait_ge(h_o, g - 1)
                nc.scalar.copy(pt_sb[:, g % 2, 0:width], acc[g % 2][:, 0:width]).then_inc(h_ptc, 1)

            def o_hi(phase, n):
                g = HEAD0[phase] + n
                if n % 2 == 1:
                    c = HEADS[phase][n][2]
                    act.wait_ge(h_o, g + 1)
                    nc.scalar.copy(act_hi[:, c, :], acc[2 + g // 2 % 2][:, 0:SEQ]).then_inc(h_ohi, 1)

            def attention(phase):
                heads = len(HEADS[phase])
                for n in range(heads + 3):
                    if n < heads:
                        exps(phase, n)
                    if 1 <= n <= heads:
                        pt_copy(phase, n - 1)
                    if 2 <= n < heads + 2:
                        o_hi(phase, n - 2)

            def log_sigmoid(n, k):
                act.wait_ge(gates_z, n)
                nc.scalar.activation(lf_sb[:, :, 0:k], za_sb[:, :, 0:k], ACT.Exp, scale=-1.0).then_inc(gates_e, 1)
                act.wait_ge(gates_e, 2 * n - 1)
                nc.scalar.activation(za_sb[:, :, 0:k], lf_sb[:, :, 0:k], ACT.Ln, bias=1.0).then_inc(gates_e, 1)

            split_hi(0)
            split_hi(1)
            for j in range(4):
                act.wait_ge(in_t, j + 1)
                nc.scalar.copy(act_hi[:, 2 * j:2 * j + 2, :], acc[j][:, :]).then_inc(mem_hi, 1)
            projection(T_MEM, 4)
            act.wait_ge(gw_in, 16)
            nc.scalar.copy(gw_hi[:, :, 0:8], gw[:, :, 0:8]).then_inc(gw_split, 1)
            squares(0, 0)
            act.wait_ge(w_used, T_MEM + 4)
            apply_hi(0)

            def take_qk(t, j):
                if j:
                    act.wait_ge(qk_act, j)
                for m in range(2):
                    c = 2 * j + m
                    nc.scalar.activation(gate_acc[:, m, :], pj[t % RING][:, m * SEQ:(m + 1) * SEQ], ACT.Identity,
                                         bias=cols(C_ACB, c), scale=cols(C_ACW + 3 * 12, c)).then_inc(qk_tap, 1)
                act.wait_ge(qk_conv, j + 1)
                nc.scalar.activation(qk[:, 2 * j:2 * j + 2, :], gate_acc[:, :, :], ACT.Silu).then_inc(qk_act, 1)

            def take_o(t, j):
                nc.scalar.activation(oT[:, 2 * j:2 * j + 2, :], pj[t % RING][:, :], ACT.Sigmoid).then_inc(evac_act, 1)

            projection(T_AQK, 6, take_qk)
            projection(T_AV, 3)
            projection(T_AO, 3, take_o)
            projection(T_AQM, 1)
            log_sigmoid(1, 4)
            act.wait_ge(gates_mm, 1)
            nc.scalar.activation(emm[:, :, :], emm[:, :, :], ACT.Exp, scale=-1.0).then_inc(gates_em, 1)
            for h in range(A_HEADS):
                act.wait_ge(ml_x, h + 1)
                nc.scalar.activation(s_sb[:, h % 2, 0:CAUSAL], p_sb[:, h % 2, 0:CAUSAL], ACT.Exp).then_inc(ml_e, 1)
            for h in range(A_HEADS):
                act.wait_ge(ml_h, h + 1)
                for b in range(NTB):
                    ins = nc.scalar.activation(nrm[:, 2 * h + b, 0:A_DH], hm[:, b, h * A_DH:(h + 1) * A_DH], ACT.Square,
                                               accum_out=small[:, 0, 2 * h + b:2 * h + b + 1])
                ins.then_inc(ml_ss, 1)
            act.wait_ge(ml_ss, A_HEADS)
            nc.scalar.activation(small[:, 1, :], small[:, 0, :], ACT.Sqrt, bias=eps[:, :], scale=1.0 / A_DH).then_inc(ml_std, 1)
            for c in range(ACH):
                act.wait_ge(ml_y, c + 1)
                nc.scalar.copy(act_hi[:, c, :], nrm[:, c, :]).then_inc(ml_yhi, 1)
            attention("a_mem")
            projection(T_AOUT, 4)
            squares(1, 1)
            apply_hi(1)
            ffn(0, True)

            squares(2, 2)
            apply_hi(2)
            projection(T_KV, 6)
            act.wait_ge(w_used, T_KV + 6)
            apply_hi(3)
            projection(T_BIN, 4)
            attention("band")
            projection(T_BOUT, 4)
            squares(3, 3)
            apply_hi(4)
            ffn(1, True)

            squares(4, 4)
            squares(5, 5)
            apply_hi(5)
            ffn(2, False)
            post_squares(6, T_FF2 + FFN_SLOTS - 1)
            squares(7, 6)
            apply_hi(6)

            def take_gate(t, j):
                nc.scalar.activation(csg[:, 2 * j:2 * j + 2, :], pj[t % RING][:, :], ACT.Sigmoid).then_inc(evac_act, 1)
                if j == 1:
                    pass

            projection(T_AB, 2, take_gate)
            projection(T_AB + 2, 5)
            attention("swa")
            act.wait_ge(cv_c, 1)
            for c in range(CCH):
                nc.scalar.activation(nrm[:, c, :], cv[:, c, :], ACT.Square).then_inc(cv_sq, 1)
            act.wait_ge(cv_var, 1)
            nc.scalar.activation(rstd[:, :], st[:, SEQ:2 * SEQ], ACT.Sqrt, bias=eps[:, :]).then_inc(cv_std, 1)
            for c in range(CCH):
                act.wait_ge(cv_z, 1)
                nc.scalar.activation(nrm[:, c, :], cv[:, c, :], ACT.Silu, bias=cols(C_LNB, c),
                                     scale=cols(C_LNG, c)).then_inc(cv_silu, 1)
                act.wait_ge(cv_silu, c + 1)
                nc.scalar.copy(act_hi[:, c, :], nrm[:, c, :]).then_inc(cv_hi, 1)
            projection(T_ABOUT, 4)
            post_squares(8, T_ABOUT + 3)
            squares(9, 7)
            apply_hi(7)
            ffn(3, False)
            post_squares(10, T_FF3 + FFN_SLOTS - 1)
            squares(11, 8)
            apply_hi(8)
            ffn(4, False)
            post_squares(12, T_FF4 + FFN_SLOTS - 1)
            squares(13, 9)
            apply_hi(9)

            act.wait_ge(gw_in, 32)
            nc.scalar.copy(gw_hi[:, :, :], gw[:, :, :]).then_inc(gw_split, 1)
            projection(T_FOX, 12)
            log_sigmoid(2, FOX_H)
            attention("fox")
            projection(T_FOXOUT, 4)
            post_squares(14, T_FOXOUT + 3)
            squares(15, 10)
            apply_hi(10)
            ffn(5, False)
            post_squares(16, T_FF5 + FFN_SLOTS - 1)
            for b in range(NTB):
                for q in range(2):
                    act.wait_ge(out_t, 2 * b + q + 1)
                    nc.scalar.copy(qk[:, 4 * b + 2 * q:4 * b + 2 * q + 2, :], acc[2 * b + q][:, :]).then_inc(out_sb, 1)

        @block.vector
        def _(dve):
            chain = [0]

            def step(ins):
                chain[0] += 1
                ins.then_inc(dve_step, 1)
                dve.wait_ge(dve_step, chain[0])

            def split_lo(base, i=0):
                if isinstance(i, int) and base + RING * i >= SLOTS:
                    return
                r = base % RING
                dve.wait_ge(hi_done, base + RING * i + 1)
                nc.vector.tensor_tensor(w_lo[:, r, :], raw[:, r, :], w_hi[:, r, :], ALU.subtract).then_inc(lo_done, 1)

            def deviation(n):
                dve.wait_ge(std_done, n + 1)
                step(nc.vector.reciprocal(rstd[:, :], rstd[:, :]))

            def apply(a, col):
                for c in range(NCH + 1):
                    if c < NCH:
                        nc.vector.scalar_tensor_tensor(out=nrm[:, c, :], in0=xT[:, c, :], scalar=cols(col, c),
                                                       in1=rstd[:, :], op0=ALU.mult, op1=ALU.mult).then_inc(xn_done, 1)
                    if c >= 1:
                        dve.wait_ge(act_hi_done, NCH * a + c)
                        nc.vector.tensor_tensor(act_lo[:, c - 1, :], nrm[:, c - 1, :], act_hi[:, c - 1, :],
                                                ALU.subtract).then_inc(act_lo_done, 1)

            def residual(t_last):
                dve.wait_ge(w_used, t_last + 1)
                for j in range(4):
                    xs = xT[:, 2 * j:2 * j + 2, :].rearrange("p c t -> p (c t)")
                    nc.vector.tensor_tensor(xs, acc[j][:, :], xs, ALU.add).then_inc(x_ready, 2)

            def post(n, t_last, col, factor):
                deviation(n)
                for c in range(NCH):
                    ins = nc.vector.scalar_tensor_tensor(
                        out=nrm[:, c, :], in0=acc[c // 2][:, c % 2 * SEQ:(c % 2 + 1) * SEQ], scalar=cols(col, c),
                        in1=rstd[:, :], op0=ALU.mult, op1=ALU.mult)
                    if c % 2:
                        step(ins)
                        xs = xT[:, c - 1:c + 1, :]
                        nc.vector.scalar_tensor_tensor(out=xs, in0=nrm[:, c - 1:c + 1, :], scalar=factor, in1=xs,
                                                       op0=ALU.mult, op1=ALU.add).then_inc(x_ready, 2)

            def ffn(f, conv):
                t0 = FFN_AT[f]

                def gate(t, s, i=0):
                    split_lo(t + 2, i)
                    if conv:
                        bank = pj[t % RING]
                        dve.wait_ge(ff_gate, 2 * STEPS * f + 2 * s + 2)
                        for back in (1, 2):
                            if back == 2:
                                dve.wait_ge(ff_tap, STEPS * f + s + 1)
                            for j in range(2):
                                wt = par[:, bass.ds(C_FCW[f] + (2 - back) * FCH + 2 * s + j, 1)]
                                ins = nc.vector.scalar_tensor_tensor(
                                    out=gate_acc[:, j, back:SEQ], in0=bank[:, j * SEQ:(j + 1) * SEQ - back], scalar=wt,
                                    in1=gate_acc[:, j, back:SEQ], op0=ALU.mult, op1=ALU.add)
                            ins.then_inc(ff_tap if back == 1 else ff_conv, 1)

                def up(t, s, i=0):
                    if f or not isinstance(s, int):
                        dve.wait_ge(ff_lo, STEPS * f + s)
                    dve.wait_ge(ff_act, STEPS * f + s + 1)
                    dve.wait_ge(w_used, t + RING * i + 1)
                    nc.vector.tensor_tensor(hid[:, :, :], gate_act[:, :, :],
                                            pj[t % RING][:, :].rearrange("p (j t) -> p j t", j=2), ALU.mult).then_inc(ff_hid, 1)

                def hid_part(s):
                    dve.wait_ge(ff_hi, STEPS * f + s + 1)
                    nc.vector.tensor_tensor(hid_lo[:, :, :], hid[:, :, :], hid_hi[:, :, :], ALU.subtract).then_inc(ff_lo, 1)

                gate(t0, 0)
                split_lo(t0 + 3)
                up(t0 + 1, 0)
                hid_part(0)

                def one(i):
                    gate(t0 - 1, i, i)
                    split_lo(t0 + 2, i)
                    up(t0, i, i)
                    split_lo(t0 + 3, i)
                    hid_part(i)

                alone = t0 + FFN_SLOTS == SLOTS
                with dve.Fori(1, STEPS - alone) as i:
                    one(i)
                if alone:
                    one(STEPS - 1)
                split_lo(t0 + RING * STEPS + 1)

            def projection(first, n, take=None):
                for t in range(first, first + n):
                    split_lo(t + 2)
                    if take:
                        dve.wait_ge(w_used, t + 1)
                        take(t, t - first)

            def copy_out(dst):
                def take(t, j):
                    nc.vector.tensor_copy(dst(j), pj[t % RING][:, :].rearrange("p (a n) -> p a n", a=2)).then_inc(evac_dve, 1)
                return take

            def scores(phase, n):
                kind, h, _ = HEADS[phase][n]
                g = HEAD0[phase] + n
                dve.wait_ge(h_s, g + 1)
                sm, ps = small[:, g % 2, :], pj[g % 2]
                if g >= 2:
                    dve.wait_ge(h_exp, g - 1)
                if kind.startswith("mem"):
                    step(nc.vector.tensor_reduce(sm[:, 0:2], ps[:, :].rearrange("p (b k) -> p b k", b=2), AXX, ALU.max,
                                                 negate=True))
                else:
                    ss = ps if kind == "band" else s_sb[:, g % 2, :]
                    if kind == "band":
                        pass
                    elif kind == "swa":
                        slope = 2.0 ** (-8.0 * (h + 1) / SWA_HQ)
                        step(nc.vector.scalar_tensor_tensor(out=ss[:, 0:CAUSAL], in0=dist[:, :], scalar=-slope * DH ** 0.5,
                                                            in1=ps[:, 0:CAUSAL], op0=ALU.mult, op1=ALU.add))
                    else:
                        for b, (lo, hi) in enumerate([(0, P), (P, CAUSAL)]):
                            ins = nc.vector.scalar_tensor_tensor(out=ss[:, lo:hi], in0=ps[:, lo:hi], scalar=c_sb[:, b, h:h + 1],
                                                                 in1=causal[:, lo:hi], op0=ALU.add, op1=ALU.add)
                        step(ins)
                    nc.vector.tensor_reduce(sm[:, 0:1], ss[:, 0:P], AXX, ALU.max, negate=True)
                    step(nc.vector.tensor_reduce(sm[:, 1:2], ss[:, P:CAUSAL], AXX, ALU.max, negate=True))
                if kind == "swa":
                    nc.vector.tensor_scalar(sm[:, 0:2], sm[:, 0:2], nsink8[:, h:h + 1], DH ** -0.5, ALU.min,
                                            ALU.mult).then_inc(h_max, 1)
                else:
                    nc.vector.tensor_scalar(sm[:, 0:2], sm[:, 0:2], DH ** -0.5, None, ALU.mult).then_inc(h_max, 1)

            def probs(phase, n):
                kind, h, _ = HEADS[phase][n]
                g = HEAD0[phase] + n
                dve.wait_ge(h_exp, g + 1)
                sm = small[:, g % 2, :]
                if kind == "swa":
                    step(nc.vector.tensor_tensor(sm[:, 2:4], sm[:, 2:4], sm[:, 4:6], ALU.add))
                step(nc.vector.reciprocal(sm[:, 2:4], sm[:, 2:4]))
                cuts = [(0, 256), (256, 512)] if kind.startswith("mem") else [(0, 128), (128, 384)]
                for b, (lo, hi) in enumerate(cuts):
                    ins = nc.vector.tensor_scalar(p_sb[:, g % 2, lo:hi], p_sb[:, g % 2, lo:hi], sm[:, 2 + b:3 + b], None,
                                                  ALU.mult)
                ins.then_inc(h_p, 1)

            def o_lo(phase, n):
                g = HEAD0[phase] + n
                if n % 2 == 1:
                    c = HEADS[phase][n][2]
                    dve.wait_ge(h_ohi, (g + 1) // 2)
                    nc.vector.tensor_tensor(act_lo[:, c, :], acc[2 + g // 2 % 2][:, 0:SEQ], act_hi[:, c, :],
                                            ALU.subtract).then_inc(h_olo, 1)

            def attention(phase, between=None):
                heads = len(HEADS[phase])
                for n in range(heads + 3):
                    if n < heads:
                        scores(phase, n)
                    if 1 <= n <= heads:
                        probs(phase, n - 1)
                    if 3 <= n < heads + 3:
                        o_lo(phase, n - 3)
                    if between:
                        between(n)

            def log_sigmoid(n, k, bias, zcol):
                dve.wait_ge(gates_ps, n)
                width = zcol + k
                zv = z_sb[:, :, 0:width]
                step(nc.vector.tensor_tensor(zv, st[:, 0:NTB * width].rearrange("p (b w) -> p b w", b=NTB),
                                             bias.rearrange("p (a w) -> p a w", a=1).to_broadcast([P, NTB, width]), ALU.add))
                zk = z_sb[:, :, zcol:width]
                nc.vector.scalar_tensor_tensor(out=za_sb[:, :, 0:k], in0=zk, scalar=-1.0, in1=zk, op0=ALU.mult,
                                               op1=ALU.max).then_inc(gates_z, 1)
                dve.wait_ge(gates_e, 2 * n)
                nc.vector.scalar_tensor_tensor(out=lf_sb[:, :, 0:k], in0=z_sb[:, :, zcol:width], scalar=0.0,
                                               in1=za_sb[:, :, 0:k], op0=ALU.min, op1=ALU.subtract).then_inc(gates_lf, 1)

            dve.wait_ge(small_in, 64)
            nc.vector.tensor_scalar(nsink8[:, :], sink[:, :], -(DH ** 0.5), None, ALU.mult)
            nc.vector.tensor_copy(tabr[:, 127:127 + REL], tab[:, ::-1])
            nc.vector.tensor_copy(tabr[:, 0:127], tab[:, REL - 1:REL].to_broadcast([B_HEADS, 127]))
            nc.vector.tensor_copy(tabr[:, 127 + REL:512], tab[:, 0:1].to_broadcast([B_HEADS, 512 - 127 - REL])).then_inc(tabr_ready, 1)
            split_lo(0)
            split_lo(1)
            for j in range(4):
                dve.wait_ge(mem_hi, j + 1)
                nc.vector.tensor_tensor(act_lo[:, 2 * j:2 * j + 2, :], acc[j][:, :].rearrange("p (c t) -> p c t", c=2),
                                        act_hi[:, 2 * j:2 * j + 2, :], ALU.subtract).then_inc(mem_lo, 1)
            dve.wait_ge(in_t, 5)
            nc.vector.tensor_copy(par[:, 0:512], pj[0][:, :])
            dve.wait_ge(in_t, 6)
            nc.vector.tensor_copy(par[:, 512:640], pj[1][:, 0:P]).then_inc(par_ready, 1)
            for j in range(4):
                dve.wait_ge(in_t, 7 + j)
                nc.vector.tensor_copy(xT[:, 2 * j:2 * j + 2, :], acc[j][:, :].rearrange("p (c t) -> p c t", c=2)).then_inc(x_ready, 2)

            def take_mem(t, j):
                dst = mv[:, j // 2, :, :] if j % 2 else mk[:, j // 2, :, :]
                nc.vector.tensor_copy(dst, pj[t % RING][:, :].rearrange("p (a n) -> p a n", a=2)).then_inc(evac_dve, 1)

            projection(T_MEM, 4, take_mem)
            dve.wait_ge(gw_split, 1)
            nc.vector.tensor_tensor(gw_lo[:, :, 0:8], gw[:, :, 0:8], gw_hi[:, :, 0:8], ALU.subtract).then_inc(gw_split, 1)
            dve.wait_ge(par_ready, 1)
            deviation(0)
            apply(0, C_MIX)

            def take_qk(t, j):
                dve.wait_ge(qk_tap, 2 * j + 2)
                for back in (1, 2, 3):
                    for m in range(2):
                        c = 2 * j + m
                        ins = nc.vector.scalar_tensor_tensor(
                            out=gate_acc[:, m, back:SEQ], in0=pj[t % RING][:, m * SEQ:(m + 1) * SEQ - back],
                            scalar=cols(C_ACW + (3 - back) * 12, c), in1=gate_acc[:, m, back:SEQ], op0=ALU.mult, op1=ALU.add)
                    if back < 3:
                        step(ins)
                ins.then_inc(qk_conv, 1)
                dve.wait_ge(qk_conv, j + 1)
                dve.sem_inc(evac_dve, 1)

            def take_v(t, j):
                at, left = j * COLS, COLS
                while left:
                    h, e = at // A_DH, at % A_DH
                    n = min(left, A_DH - e)
                    off = at - j * COLS
                    ins = nc.vector.tensor_copy(vaug[:, :, h, e:e + n],
                                                pj[t % RING][:, :].rearrange("p (a n) -> p a n", a=2)[:, :, off:off + n])
                    at, left = at + n, left - n
                ins.then_inc(evac_dve, 1)

            projection(T_AQK, 6, take_qk)
            projection(T_AV, 3, take_v)
            projection(T_AO, 3)
            projection(T_AQM, 1, copy_out(lambda j: qm[:, :, :]))
            log_sigmoid(1, A_HEADS, gate_b[:, :], A_HEADS)
            dve.wait_ge(gates_c, 1)
            nc.vector.tensor_copy(c_sb[:, :, 0:4], st[:, 64:72].rearrange("p (b h) -> p b h", b=2))
            nc.vector.tensor_tensor(a_tok[:, :, :], z_sb[:, :, 0:4], st[:, 64:72].rearrange("p (b h) -> p b h", b=2),
                                    ALU.subtract).then_inc(gates_a, 1)
            dve.wait_ge(gates_t, 1)
            step(nc.vector.tensor_scalar(cum[:, 0, P:], pj[2][0:A_HEADS, 0:SEQ], 0.0, None, ALU.max))
            for k in range(8):
                s, d, back = k % 2, (k + 1) % 2, 1 << k
                step(nc.vector.tensor_tensor(cum[:, d, P:], cum[:, s, P:], cum[:, s, P - back:P + SEQ - back], ALU.max))
            nc.vector.tensor_scalar(rowc[0:A_HEADS, :], cum[:, 0, P:], -1.0, None, ALU.mult).then_inc(gates_m, 1)
            dve.wait_ge(gates_mt, 1)
            dve.wait_ge(gates_a, 1)
            nc.vector.tensor_tensor(emm[:, :, :], c_sb[:, :, 0:4], pj[2][:, 256:264].rearrange("p (b h) -> p b h", b=2),
                                    ALU.add).then_inc(gates_mm, 1)

            def decays(h):
                dve.wait_ge(ml_bc, h + 1)
                if h >= 2:
                    dve.wait_ge(ml_e, h - 1)
                bc = pj[h % 2]
                nc.vector.tensor_scalar(p_sb[:, h % 2, 0:SEQ], bc[:, 0:SEQ], a_tok[:, 0, h:h + 1], 0.0, ALU.add, ALU.min)
                nc.vector.tensor_scalar(p_sb[:, h % 2, SEQ:CAUSAL], bc[:, P:SEQ], a_tok[:, 1, h:h + 1], 0.0, ALU.add,
                                        ALU.min).then_inc(ml_x, 1)

            def weigh(h):
                dve.wait_ge(ml_mask, h + 1)
                dve.wait_ge(ml_s, h + 1)
                if h >= 2:
                    dve.wait_ge(ml_num, h - 1)
                nc.vector.scalar_tensor_tensor(out=pt_sb[:, h % 2, 0:CAUSAL], in0=acc[h % 2][:, 0:CAUSAL], scalar=A_DH ** -0.5,
                                               in1=s_sb[:, h % 2, 0:CAUSAL], op0=ALU.mult, op1=ALU.mult).then_inc(ml_p, 1)

            def divide(h):
                dve.wait_ge(ml_num, h + 1)
                num = acc[2 + h % 2][:, 0:2 * VA].rearrange("p (b e) -> p b e", b=2)
                den = small[:, 1, 2 * h:2 * h + 2]
                ps = num[:, :, A_DH:VA].rearrange("p b e -> p (b e)")
                step(nc.vector.scalar_tensor_tensor(out=den, in0=ps, scalar=-1.0, in1=emm[:, :, h:h + 1].rearrange("p b e -> p (b e)"),
                                                    op0=ALU.mult, op1=ALU.max))
                step(nc.vector.tensor_tensor(den, ps, den, ALU.max))
                step(nc.vector.reciprocal(den, den))
                for b in range(NTB):
                    ins = nc.vector.tensor_scalar(hm[:, b, h * A_DH:(h + 1) * A_DH], num[:, b, 0:A_DH], den[:, b:b + 1], None,
                                                  ALU.mult)
                ins.then_inc(ml_h, 1)

            dve.wait_ge(gates_em, 1)
            for n in range(A_HEADS + 2):
                if n < A_HEADS:
                    decays(n)
                if 1 <= n <= A_HEADS:
                    weigh(n - 1)
                if n >= 2:
                    divide(n - 2)
            dve.wait_ge(ml_std, 1)
            step(nc.vector.reciprocal(small[:, 1, :], small[:, 1, :]))
            dve.wait_ge(ml_h, A_HEADS)
            for h in range(A_HEADS):
                for b in range(NTB):
                    hs = hm[:, b, h * A_DH:(h + 1) * A_DH]
                    ins = nc.vector.tensor_scalar(hs, hs, small[:, 1, 2 * h + b:2 * h + b + 1], None, ALU.mult)
            ins.then_inc(ml_hn, 1)
            for c in range(ACH + 1):
                if c < ACH:
                    dve.wait_ge(ml_t, c + 1)
                    if c == 0:
                        dve.wait_ge(evac_act, 3)
                    nc.vector.scalar_tensor_tensor(out=nrm[:, c, :], in0=pj[c % 2][:, 0:SEQ], scalar=cols(C_AHG, c),
                                                   in1=oT[:, c, :], op0=ALU.mult, op1=ALU.mult).then_inc(ml_y, 1)
                if c >= 1:
                    dve.wait_ge(ml_yhi, c)
                    nc.vector.tensor_tensor(act_lo[:, c - 1, :], nrm[:, c - 1, :], act_hi[:, c - 1, :],
                                            ALU.subtract).then_inc(ml_ylo, 1)
            attention("a_mem")
            projection(T_AOUT, 4)
            residual(T_AOUT + 3)
            deviation(1)
            apply(1, C_FFN)
            ffn(0, True)
            residual(T_FF0 + FFN_SLOTS - 1)

            deviation(2)
            apply(2, C_KV)
            projection(T_KV, 3, copy_out(lambda j: qk[:, 6 + 2 * j:8 + 2 * j, :]))
            projection(T_KV + 3, 3, copy_out(lambda j: vtok[:, :, j * COLS:(j + 1) * COLS]))
            apply(3, C_MIX + 8)
            projection(T_BIN, 3, copy_out(lambda j: qk[:, 2 * j:2 * j + 2, :]))
            projection(T_BIN + 3, 1, copy_out(lambda j: qm[:, :, :]))
            attention("band")
            projection(T_BOUT, 4)
            residual(T_BOUT + 3)
            deviation(3)
            apply(4, C_FFN + 8)
            ffn(1, True)
            residual(T_FF1 + FFN_SLOTS - 1)

            deviation(4)
            for c in range(NCH):
                nc.vector.scalar_tensor_tensor(out=xT[:, c, :], in0=xT[:, c, :], scalar=cols(C_FINAL, c), in1=rstd[:, :],
                                               op0=ALU.mult, op1=ALU.mult).then_inc(x_ready, 1)
            deviation(5)
            apply(5, C_NG2)
            ffn(2, False)
            post(6, T_FF2 + FFN_SLOTS - 1, C_NG2 + 8, 0.5)
            deviation(7)
            apply(6, C_NG2 + 16)

            def take_u(t, j):
                if j == 0:
                    dve.wait_ge(evac_act, 5)
                nc.vector.tensor_tensor(apad[:, 2 * j:2 * j + 2, CONV_K - 1:], pj[t % RING][:, :].rearrange("p (a n) -> p a n", a=2),
                                        csg[:, 2 * j:2 * j + 2, :], ALU.mult).then_inc(evac_dve, 1)

            def take_kv(t, j):
                nc.vector.tensor_copy(qk[:, 4, :], pj[t % RING][:, 0:SEQ]).then_inc(k_ready, 1)
                nc.vector.tensor_copy(vtok[:, :, 0:P], pj[t % RING][:, SEQ:].rearrange("p (a n) -> p a n", a=2)).then_inc(evac_dve, 1)

            projection(T_AB, 2)
            projection(T_AB + 2, 2, take_u)
            projection(T_AB + 4, 2, copy_out(lambda j: qk[:, 2 * j:2 * j + 2, :]))
            projection(T_AB + 6, 1, take_kv)
            dve.wait_ge(vec_const, 2)

            taps = [(c, j) for j in range(CONV_K) for c in range(CCH)]

            def tap(c, j):
                src = apad[:, c, j:j + SEQ]
                if j == 0:
                    nc.vector.tensor_scalar(cv[:, c, :], src, cols(C_CW, c), cols(C_CB, c), ALU.mult, ALU.add).then_inc(cv_y, 1)
                else:
                    dve.wait_ge(cv_y, CCH * (j - 1) + c + 1)
                    nc.vector.scalar_tensor_tensor(out=cv[:, c, :], in0=src, scalar=cols(C_CW, 4 * j + c), in1=cv[:, c, :],
                                                   op0=ALU.mult, op1=ALU.add).then_inc(cv_y, 1)

            def some_taps(n):
                for _ in range(2):
                    if taps:
                        tap(*taps.pop(0))

            attention("swa", some_taps)
            while taps:
                tap(*taps.pop(0))
            dve.wait_ge(cv_mu, 1)
            for c in range(CCH):
                ins = nc.vector.tensor_tensor(cv[:, c, :], cv[:, c, :], st[:, 0:SEQ], ALU.subtract)
            ins.then_inc(cv_c, 1)
            dve.wait_ge(cv_std, 1)
            step(nc.vector.reciprocal(rstd[:, :], rstd[:, :]))
            dve.wait_ge(cv_c, 1)
            for c in range(CCH):
                ins = nc.vector.tensor_tensor(cv[:, c, :], cv[:, c, :], rstd[:, :], ALU.mult)
            ins.then_inc(cv_z, 1)
            for c in range(CCH):
                dve.wait_ge(cv_hi, c + 1)
                nc.vector.tensor_tensor(act_lo[:, c, :], nrm[:, c, :], act_hi[:, c, :], ALU.subtract).then_inc(cv_lo, 1)
            projection(T_ABOUT, 4)
            post(8, T_ABOUT + 3, C_NG2 + 24, 1.0)
            deviation(9)
            apply(7, C_NG2 + 32)
            ffn(3, False)
            post(10, T_FF3 + FFN_SLOTS - 1, C_NG2 + 40, 0.5)
            deviation(11)
            apply(8, C_NG2 + 48)
            ffn(4, False)
            post(12, T_FF4 + FFN_SLOTS - 1, C_NG2 + 56, 0.5)
            deviation(13)
            apply(9, C_NG2 + 64)

            dve.wait_ge(gw_split, 3)
            nc.vector.tensor_tensor(gw_lo[:, :, :], gw[:, :, :], gw_hi[:, :, :], ALU.subtract).then_inc(gw_split, 1)
            projection(T_FOX, 8, copy_out(lambda j: qk[:, 2 * j:2 * j + 2, :]))
            projection(T_FOX + 8, 4, copy_out(lambda j: vtok[:, :, j * COLS:(j + 1) * COLS]))
            log_sigmoid(2, FOX_H, fox_b[:, :], 0)
            dve.wait_ge(gates_c, 2)
            nc.vector.tensor_scalar(c_sb[:, :, :], st[:, 64:64 + NTB * FOX_H].rearrange("p (b h) -> p b h", b=2), DH ** 0.5,
                                    None, ALU.mult).then_inc(gates_a, 1)
            dve.wait_ge(gates_t, 2)
            nc.vector.tensor_scalar(rowc[:, :], pj[2][0:FOX_H, 0:SEQ], -1.0, None, ALU.mult).then_inc(gates_m, 1)
            attention("fox")
            projection(T_FOXOUT, 4)
            post(14, T_FOXOUT + 3, C_NG2 + 72, 1.0)
            deviation(15)
            apply(10, C_NG2 + 80)
            ffn(5, False)
            post(16, T_FF5 + FFN_SLOTS - 1, C_NG2 + 88, 0.5)

        @block.tensor
        def _(pe):
            def three(dst, w, a, start, stop):
                nc.tensor.matmul(dst, w[0], a[0], start=start, stop=False, skip_group_check=True)
                nc.tensor.matmul(dst, w[0], a[1], start=False, stop=False, skip_group_check=True)
                return nc.tensor.matmul(dst, w[1], a[0], start=False, stop=stop, skip_group_check=True)

            def weights(base, lo, n=P):
                r = base % RING
                return w_hi[:, r, lo:lo + n], w_lo[:, r, lo:lo + n]

            def acts(k, lo=0, n=SEQ):
                return act_hi[:, k, lo:lo + n], act_lo[:, k, lo:lo + n]

            def slot_ready(base, i=0):
                pe.wait_ge(lo_done, base + RING * i + 1)

            def feature_major(base, bank, i=0, first_use=None, widths=2):
                slot_ready(base, i)
                for m in range(widths):
                    for k in range(NCH):
                        if m == 0 and first_use:
                            first_use(k)
                        ins = three(bank[:, m * SEQ:(m + 1) * SEQ], weights(base, k * COLS + m * P), acts(k),
                                    start=k == 0, stop=k == NCH - 1)
                return ins

            def token_major(base, bank, i=0, first_use=None, lo=0, n=COLS, at=0, ready=True):
                if ready:
                    slot_ready(base, i)
                for b in range(NTB):
                    for k in range(NCH):
                        if b == 0 and first_use:
                            first_use(k)
                        ins = three(bank[:, at + b * n:at + (b + 1) * n], acts(k, b * P, P), weights(base, k * COLS + lo, n),
                                    start=k == 0, stop=k == NCH - 1)
                return ins

            def down(base, i=0):
                slot_ready(base, i)
                for k in range(2):
                    for c in range(NCH):
                        ins = three(acc[c // 2][:, c % 2 * SEQ:(c % 2 + 1) * SEQ], weights(base, k * D + c * P),
                                    (hid_hi[:, k, :], hid_lo[:, k, :]), start=False, stop=False)
                ins.then_inc(w_used, 1)

            def statistics(n, w=mean_w):
                for c in range(NCH):
                    pe.wait_ge(sq_done, NCH * n + c + 1)
                    ins = nc.tensor.matmul(st[:, 0:SEQ], w[:, :], nrm[:, c, :], start=c == 0, stop=c == NCH - 1)
                ins.then_inc(stat, 1)

            def applied(a):
                return lambda k: pe.wait_ge(act_lo_done, NCH * a + k + 1)

            def ffn(f, a, u):
                t0 = FFN_AT[f]
                pe.wait_ge(x_ready, NCH * (u + 1))
                for j in range(4):
                    nc.tensor.matmul(acc[j][:, :], zero[:, 0:P], zero[:, :], start=True, stop=True)

                feature_major(t0, pj[t0 % RING], first_use=applied(a)).then_inc(w_used, 1)
                feature_major(t0 + 1, pj[(t0 + 1) % RING]).then_inc(w_used, 1)
                with pe.Fori(1, STEPS) as i:
                    pe.wait_ge(ff_act, STEPS * f + i)
                    feature_major(t0 - 1, pj[(t0 - 1) % RING], i).then_inc(w_used, 1)
                    pe.wait_ge(ff_hid, STEPS * f + i)
                    feature_major(t0, pj[t0 % RING], i).then_inc(w_used, 1)
                    pe.wait_ge(ff_lo, STEPS * f + i)
                    down(t0 + 1, i)
                pe.wait_ge(ff_lo, STEPS * (f + 1))
                down(t0 + RING * STEPS - 1)

            def project(first, n, form, first_use=None):
                for t in range(first, first + n):
                    if t - RING in evac_of:
                        evacuated(pe, t - RING)
                    form(t, pj[t % RING], first_use=first_use if t == first else None).then_inc(w_used, 1)

            def project_out(first):
                for j in range(4):
                    feature_major(first + j, acc[j]).then_inc(w_used, 1)

            def head_qk(kind, h):
                rows = slice(DH * (h % 2), DH * (h % 2) + DH)
                if kind == "band":
                    return qk[rows, h // 2, :], qk[rows, 6 + h // 2, :]
                if kind == "fox":
                    return qk[rows, h // 2, :], qk[rows, 8 + h // 2, :]
                if kind == "swa":
                    keys = qk[rows, 4, :] if h // 4 == h % 2 else kswap[rows, :]
                    return qk[rows, h // 2, :], keys
                return qm[rows, h // 2, :], mk[rows, int(kind[3]), h // 2, :]

            def head_v(kind, h, b):
                if kind.startswith("mem"):
                    return mv[:, int(kind[3]), b, h * DH:(h + 1) * DH]
                if kind == "swa":
                    h = h // 4
                return vtok[:, b, h * DH:(h + 1) * DH]

            def scores(phase, n):
                kind, h, _ = HEADS[phase][n]
                g = HEAD0[phase] + n
                q, k = head_qk(kind, h)
                bank = pj[g % 2]
                if n >= 2:
                    pe.wait_ge(h_exp, g - 1)
                for b in range(NTB):
                    lo, keys = (b * SEQ, SEQ) if kind.startswith("mem") else (b * P, P * (b + 1))
                    ins = nc.tensor.matmul(bank[:, lo:lo + keys], q[:, b * P:(b + 1) * P], k[:, 0:keys], start=True,
                                           stop=kind not in ("fox", "band"), skip_group_check=True)
                    if kind == "band":
                        ins = nc.tensor.matmul(bank[:, lo:lo + keys], turn8[:, :], relb[:, h, lo:lo + keys], start=False,
                                               stop=True, skip_group_check=True)
                    if kind == "fox":
                        ins = nc.tensor.matmul(bank[:, lo:lo + keys], sel[:, h, :], rowc[:, 0:keys], start=False, stop=True,
                                               skip_group_check=True)
                ins.then_inc(h_s, 1)

            def turns(phase, n):
                kind, h, _ = HEADS[phase][n]
                g = HEAD0[phase] + n
                pe.wait_ge(h_p, g + 1)
                if n >= 2:
                    pe.wait_ge(h_ptc, g - 1)
                blocks = [(0, 0), (256, 128), (128, 256), (384, 384)] if kind.startswith("mem") else \
                    [(0, 0), (128, 128), (256, 256)]
                for src, dst in blocks:
                    ins = nc.tensor.transpose(acc[g % 2][:, dst:dst + P], p_sb[:, g % 2, src:src + P], ident[:, :])
                ins.then_inc(h_pt, 1)

            def values(phase, n):
                kind, h, _ = HEADS[phase][n]
                g = HEAD0[phase] + n
                pe.wait_ge(h_ptc, g + 1)
                if n % 2 == 0 and n >= 4:
                    pe.wait_ge(h_olo, g // 2 - 1)
                rows = slice(DH * (n % 2), DH * (n % 2) + DH)
                dst = acc[2 + g // 2 % 2][rows, :]
                nc.tensor.matmul(dst[:, 0:SEQ], head_v(kind, h, 0), pt_sb[:, g % 2, 0:SEQ], start=True, stop=False,
                                 skip_group_check=True)
                if kind.startswith("mem"):
                    ins = nc.tensor.matmul(dst[:, 0:SEQ], head_v(kind, h, 1), pt_sb[:, g % 2, SEQ:2 * SEQ], start=False,
                                           stop=True, skip_group_check=True)
                else:
                    ins = nc.tensor.matmul(dst[:, P:SEQ], head_v(kind, h, 1), pt_sb[:, g % 2, SEQ:CAUSAL], start=False,
                                           stop=True, skip_group_check=True)
                ins.then_inc(h_o, 1)

            def attention(phase):
                heads = len(HEADS[phase])
                for n in range(heads + 2):
                    if n < heads:
                        scores(phase, n)
                    if 1 <= n <= heads:
                        turns(phase, n - 1)
                    if n >= 2:
                        values(phase, n - 2)
                pe.wait_ge(h_olo, (HEAD0[phase] + heads) // 2)

            def narrow(width):
                for b in range(NTB):
                    for k in range(NCH):
                        ins = three(st[:, b * width:(b + 1) * width], acts(k, b * P, P),
                                    (gw_hi[:, k, 0:width], gw_lo[:, k, 0:width]), start=k == 0, stop=k == NCH - 1)
                ins.then_inc(gates_ps, 1)

            def cumulate(n, k):
                pe.wait_ge(gates_lf, n)
                nc.tensor.matmul(st[:, 64:64 + k], tri[:, 0:P], lf_sb[:, 0, 0:k], start=True, stop=True)
                nc.tensor.matmul(st[:, 64 + k:64 + 2 * k], tri[:, P:2 * P], lf_sb[:, 0, 0:k], start=True, stop=False)
                nc.tensor.matmul(st[:, 64 + k:64 + 2 * k], tri[:, 0:P], lf_sb[:, 1, 0:k], start=False, stop=True).then_inc(gates_c, 1)

            pe.wait_ge(consts, 10)
            pe.wait_ge(tokens_in[0], 16)
            tok = [qk[:, 0:8, :].rearrange("p (b c) t -> p b (c t)", b=NTB), qk[:, 8:16, :].rearrange("p (b c) t -> p b (c t)", b=NTB)]

            def turn_tokens(src, waits):
                for j in range(4):
                    if waits:
                        pe.wait_ge(mem_lo, j + 1)
                    for c in range(2):
                        for b in range(NTB):
                            ins = nc.tensor.transpose(acc[j][:, c * SEQ + b * P:c * SEQ + (b + 1) * P],
                                                      src[:, b, (2 * j + c) * P:(2 * j + c + 1) * P], ident[:, :])
                    ins.then_inc(in_t, 1)

            turn_tokens(tok[0], False)
            pe.wait_ge(params_in, 16 * 16)
            for n in range(PARAM_TILES):
                ins = nc.tensor.transpose(pj[n // 4][:, n % 4 * P:(n % 4 + 1) * P], prow[:, n, :], ident[:, :])
                if n in (3, 4):
                    ins.then_inc(in_t, 1)
            pe.wait_ge(tokens_in[1], 16)
            turn_tokens(tok[1], True)
            pe.wait_ge(par_ready, 1)
            for l in range(2):
                for part, form in enumerate((feature_major, token_major)):
                    t = T_MEM + 2 * l + part
                    if t >= RING:
                        evacuated(pe, t - RING)
                    form(t, pj[t % RING]).then_inc(w_used, 1)
            statistics(0)

            project(T_AQK, 6, feature_major, applied(0))
            project(T_AV, 3, token_major)
            project(T_AO, 3, feature_major)
            project(T_AQM, 1, feature_major)
            pe.wait_ge(gw_split, 2)
            narrow(8)
            cumulate(1, 4)
            pe.wait_ge(gates_a, 1)
            evacuated(pe, T_AO + 2)
            evacuated(pe, T_AQM)
            for b in range(NTB):
                ins = nc.tensor.transpose(pj[2][0:A_HEADS, b * P:(b + 1) * P], a_tok[:, b, :], ident[:, :])
            ins.then_inc(gates_t, 1)
            pe.wait_ge(gates_m, 1)
            for b in range(NTB):
                ins = nc.tensor.matmul(pj[2][:, 256 + 4 * b:260 + 4 * b], cum[:, 0, P + b * P:P + (b + 1) * P],
                                       ident[0:A_HEADS, 0:A_HEADS], start=True, stop=True, skip_group_check=True)
            ins.then_inc(gates_mt, 1)

            def spread(h):
                if h >= 2:
                    pe.wait_ge(ml_x, h - 1)
                nc.tensor.matmul(pj[h % 2][:, 0:SEQ], sel[0:A_HEADS, h, :], rowc[0:A_HEADS, :], start=True, stop=True).then_inc(ml_bc, 1)

            def keys_queries(h):
                if h >= 2:
                    pe.wait_ge(ml_p, h - 1)
                pieces = a_head_rows(h)
                for lo, n, s0, t0 in ((0, SEQ, 0, 0), (SEQ, P, P, P)):
                    for i, (c, r0, rows) in enumerate(pieces):
                        rs = slice(r0, r0 + rows)
                        ins = nc.tensor.matmul(acc[h % 2][:, lo:lo + n], qk[rs, ACH + c, s0:s0 + P], qk[rs, c, t0:t0 + n],
                                               start=i == 0, stop=i == len(pieces) - 1, skip_group_check=True)
                ins.then_inc(ml_s, 1)

            def numerator(h):
                pe.wait_ge(ml_p, h + 1)
                if h >= 2:
                    pe.wait_ge(ml_h, h - 1)
                bank = acc[2 + h % 2]
                nc.tensor.matmul(bank[:, 0:VA], pt_sb[:, h % 2, 0:P], vaug[:, 0, h, :], start=True, stop=True, skip_group_check=True)
                nc.tensor.matmul(bank[:, VA:2 * VA], pt_sb[:, h % 2, P:2 * P], vaug[:, 0, h, :], start=True, stop=False, skip_group_check=True)
                nc.tensor.matmul(bank[:, VA:2 * VA], pt_sb[:, h % 2, 2 * P:3 * P], vaug[:, 1, h, :], start=False, stop=True,
                                 skip_group_check=True).then_inc(ml_num, 1)

            pe.wait_ge(qk_act, 6)
            for n in range(A_HEADS + 1):
                if n < A_HEADS:
                    spread(n)
                    keys_queries(n)
                if n >= 1:
                    numerator(n - 1)
            pe.wait_ge(ml_hn, 1)
            for c in range(ACH):
                if c >= 2:
                    pe.wait_ge(ml_y, c - 1)
                for b in range(NTB):
                    ins = nc.tensor.transpose(pj[c % 2][:, b * P:(b + 1) * P], hm[:, b, c * P:(c + 1) * P], ident[:, :])
                ins.then_inc(ml_t, 1)
            pe.wait_ge(ml_ylo, ACH)
            attention("a_mem")
            project_out(T_AOUT)
            statistics(1)
            ffn(0, 1, 1)

            statistics(2)
            project(T_KV, 3, feature_major, applied(2))
            project(T_KV + 3, 3, token_major)
            project(T_BIN, 4, feature_major, applied(3))
            evacuated(pe, T_BIN + 3)
            pe.wait_ge(vec_const, 1)
            attention("band")
            project_out(T_BOUT)
            statistics(3)
            ffn(1, 4, 3)
            statistics(4)
            statistics(5)
            ffn(2, 5, 5)
            statistics(6)
            statistics(7)

            def keys_values(base, bank, first_use=None):
                feature_major(base, bank, widths=1)
                return token_major(base, bank, lo=P, n=P, at=SEQ, ready=False)

            project(T_AB, 6, feature_major, applied(6))
            project(T_AB + 6, 1, keys_values)
            evacuated(pe, T_AB + 6)
            pe.wait_ge(kswap_in, 32)
            attention("swa")
            pe.wait_ge(cv_y, CCH * CONV_K)
            for c in range(CCH):
                ins = nc.tensor.matmul(st[:, 0:SEQ], mean_c[:, :], cv[:, c, :], start=c == 0, stop=c == CCH - 1)
            ins.then_inc(cv_mu, 1)
            for c in range(CCH):
                pe.wait_ge(cv_sq, c + 1)
                ins = nc.tensor.matmul(st[:, SEQ:2 * SEQ], mean_c[:, :], nrm[:, c, :], start=c == 0, stop=c == CCH - 1)
            ins.then_inc(cv_var, 1)
            pe.wait_ge(cv_lo, CCH)
            project_out(T_ABOUT)
            statistics(8)
            statistics(9)
            ffn(3, 7, 7)
            statistics(10)
            statistics(11)
            ffn(4, 8, 8)
            statistics(12)
            statistics(13)

            project(T_FOX, 8, feature_major, applied(9))
            project(T_FOX + 8, 4, token_major)
            pe.wait_ge(gw_split, 4)
            narrow(FOX_H)
            cumulate(2, FOX_H)
            pe.wait_ge(gates_a, 2)
            evacuated(pe, T_FOX + 11)
            for b in range(NTB):
                ins = nc.tensor.transpose(pj[2][0:FOX_H, b * P:(b + 1) * P], c_sb[:, b, :], ident[:, :])
            ins.then_inc(gates_t, 1)
            pe.wait_ge(gates_m, 2)
            attention("fox")
            project_out(T_FOXOUT)
            statistics(14)
            statistics(15)
            ffn(5, 10, 10)
            statistics(16)
            for b in range(NTB):
                for q in range(2):
                    pe.wait_ge(x_ready, NCH * 12)
                    for c in range(4):
                        ins = nc.tensor.transpose(acc[2 * b + q][:, c * P:(c + 1) * P], xT[:, 4 * q + c, b * P:(b + 1) * P], ident[:, :])
                    ins.then_inc(out_t, 1)


INPUTS = ["x", "mem", "norm_mix_g", "norm_ffn_g", "a_w_in", "a_gate_b", "a_conv_w", "a_conv_b", "a_head_g", "a_w_out",
          "kv_norm_g", "w_kv", "b_w_in", "b_rel_bias", "b_w_out", "mem_w_kv", "ffn_w_up", "ffn_conv_w", "ffn_conv_b",
          "ffn_w_down", "final_g", "norm_g_2", "ffn_w_gate_2", "ffn_w_up_2", "ffn_w_down_2", "ab_w_in_2", "conv_w_2",
          "conv_b_2", "conv_ln_g_2", "conv_ln_b_2", "swa_sinks_2", "ab_w_out_2", "fox_w_in_2", "fox_b_f_2", "fox_w_out_2"]


def kernel(**inputs):
    import numpy as np
    import concourse.bacc as bacc
    from concourse.bass_utils import run_bass_kernel_spmd

    nc = bacc.Bacc("TRN2", target_bir_lowering=False, num_devices=1)
    arrays, args = {}, []
    for name in INPUTS:
        a = np.ascontiguousarray(inputs[name])
        arrays[f"in_{name}"] = a
        args.append(nc.dram_tensor(f"in_{name}", a.shape, mybir.dt.from_np(a.dtype), kind="ExternalInput").ap())
    args.append(nc.dram_tensor("out_x", (1, SEQ, D), F32, kind="ExternalOutput").ap())
    build(nc, *args)
    r = run_bass_kernel_spmd(nc, [arrays], core_ids=[0])
    return r.results[0]["out_x"]
```

```python
from contextlib import ExitStack

import concourse.bass as bass
from concourse import mybir

F32 = mybir.dt.float32
F32R = mybir.dt.float32r
BF16 = mybir.dt.bfloat16
ALU = mybir.AluOpType
ACT = mybir.ActivationFunctionType
AXX = mybir.AxisListType.X

P = 128
D = 1024
NCH = D // P
SEQ = 256
NTB = SEQ // P
COLS = 256
RING = 3
SLOTW = NCH * COLS
EPS = 1e-6

DFF = 2816
STEPS = DFF // COLS
FCH = DFF // P

A_WIDTH = 768
A_HEADS = 4
A_DH = A_WIDTH // A_HEADS
A_CONV = 4
ACH = A_WIDTH // P
VA = A_DH + 1
DH = 64
B_HEADS = 12
REL = 192
MAX_REL = 128
CHUNK = 64
MEM_HEADS = 4
MCH = 2
CONV_K = 31
CCH = 4
DVE_CHUNKS = 2
POOL_CHUNK = 2
PE_CHUNK = 3
SWA_HQ = 8
FOX_H = 16
WINDOW = 128
NEG = -1e30
CAUSAL = 3 * P

T_MEM = 0
T_AQK = T_MEM + 4
T_AV = T_AQK + 6
T_AO = T_AV + 3
T_AQM = T_AO + 3
T_AOUT = T_AQM + 1
T_FF0 = T_AOUT + 4
FFN_SLOTS = 3 * STEPS
T_KV = T_FF0 + FFN_SLOTS
T_BIN = T_KV + 6
T_BOUT = T_BIN + 4
T_FF1 = T_BOUT + 4
T_FF2 = T_FF1 + FFN_SLOTS
T_AB = T_FF2 + FFN_SLOTS
T_ABOUT = T_AB + 7
T_FF3 = T_ABOUT + 4
T_FF4 = T_FF3 + FFN_SLOTS
T_FOX = T_FF4 + FFN_SLOTS
T_FOXOUT = T_FOX + 12
T_FF5 = T_FOXOUT + 4
SLOTS = T_FF5 + FFN_SLOTS
FFN_AT = [T_FF0, T_FF1, T_FF2, T_FF3, T_FF4, T_FF5]

PARAM_TILES = 5
C_MIX, C_FFN, C_KV, C_FINAL, C_ACW, C_ACB, C_AHG = 0, 16, 32, 40, 48, 96, 108
C_NG2, C_LNG, C_LNB = 128, 224, 228
C_FCW = [256, 384]
C_FCB = [256 + 66, 384 + 66]
C_CW, C_CB = 512, 636


def a_head_rows(h):
    at, left, out = h * A_DH, A_DH, []
    while left:
        n = min(left, P - at % P)
        out.append((at // P, at % P, n))
        at, left = at + n, left - n
    return out


def pairs(kind, heads, chunk):
    return [(kind, 2 * j, chunk + j) for j in range(heads // 2)]


PAIRS = {"a_mem": pairs("mem0", MEM_HEADS, 6),
         "band": pairs("band", B_HEADS, 0) + pairs("mem1", MEM_HEADS, 6),
         "swa": pairs("swa", SWA_HQ, 4),
         "fox": pairs("fox", FOX_H, 0)}
PAIR0 = {"a_mem": 0, "band": 2, "swa": 10, "fox": 14}


def width(kind):
    return 512 if kind.startswith("mem") else CAUSAL


def cuts(kind):
    return [(0, 256), (256, 512)] if kind.startswith("mem") else [(0, P), (P, CAUSAL)]


def build(nc, x, mem, norm_mix_g, norm_ffn_g, a_w_in, a_gate_b, a_conv_w, a_conv_b, a_head_g, a_w_out,
          kv_norm_g, w_kv, b_w_in, b_rel_bias, b_w_out, mem_w_kv, ffn_w_up, ffn_conv_w, ffn_conv_b,
          ffn_w_down, final_g, norm_g_2, ffn_w_gate_2, ffn_w_up_2, ffn_w_down_2, ab_w_in_2, conv_w_2,
          conv_b_2, conv_ln_g_2, conv_ln_b_2, swa_sinks_2, ab_w_out_2, fox_w_in_2, fox_b_f_2,
          fox_w_out_2, out):
    ctx = ExitStack()
    with ctx:
        def sb(name, shape, dt=F32):
            return ctx.enter_context(nc.sbuf_tensor(name, shape, dt))

        def sem(name):
            return ctx.enter_context(nc.semaphore(name))

        raw = sb("raw", [P, RING, SLOTW])
        w_hi = sb("w_hi", [P, RING, SLOTW], F32R)
        w_lo = sb("w_lo", [P, RING, SLOTW], F32R)
        xT = sb("xT", [P, NCH, SEQ])
        act_hi = sb("act_hi", [P, NCH, SEQ], F32R)
        act_lo = sb("act_lo", [P, NCH, SEQ], F32R)
        nrm = sb("nrm", [P, NCH, SEQ])
        rstd = sb("rstd", [P, SEQ])
        rstd2 = rstd[:, :].rearrange("p (a t) -> p a t", a=1).to_broadcast([P, 2, SEQ])
        work = sb("work", [P, 5 * 2 * SEQ])
        gate_acc, gate_act, hid, gate_cv, up_sc = (
            work[:, j * 2 * SEQ:(j + 1) * 2 * SEQ].rearrange("p (m t) -> p m t", m=2) for j in range(5))
        rtok = sb("rtok", [P, NTB])
        hid_hi = sb("hid_hi", [P, 2, SEQ], F32R)
        hid_lo = sb("hid_lo", [P, 2, SEQ], F32R)
        qk = sb("qk", [P, 16, SEQ])
        vals = sb("vals", [P, NTB * D])
        qm = sb("qm", [P, MCH, SEQ])
        mk = sb("mk", [P, 2, MCH, SEQ])
        mv = sb("mv", [P, 2, NTB, MCH * P])
        aux = sb("aux", [P, B_HEADS * CAUSAL])
        p_sb = sb("p_sb", [P, 2, 2 * 512])
        ident = sb("ident", [P, P])
        mean_w = sb("mean_w", [P, P])
        mean_c = sb("mean_c", [P, P])
        turn8 = sb("turn8", [P, P])
        tri = sb("tri", [P, 2 * P])
        causal = sb("causal", [P, CAUSAL])
        dist = sb("dist", [P, CAUSAL])
        eps = sb("eps", [P, 1])
        zero = sb("zero", [P, 512], BF16)
        par = sb("par", [P, PARAM_TILES * P])
        gate_b = sb("gate_b", [P, 2 * A_HEADS])
        fox_b = sb("fox_b", [P, FOX_H])
        sink = sb("sink", [P, SWA_HQ])
        sink8 = sb("sink8", [P, SWA_HQ])
        gw = sb("gw", [P, NCH, FOX_H])
        gw_hi = sb("gw_hi", [P, NCH, FOX_H], F32R)
        gw_lo = sb("gw_lo", [P, NCH, FOX_H], F32R)
        z_sb = sb("z_sb", [P, NTB, FOX_H])
        za_sb = sb("za_sb", [P, NTB, FOX_H])
        lf_sb = sb("lf_sb", [P, NTB, FOX_H])
        c_sb = sb("c_sb", [P, NTB, FOX_H])
        rowc = sb("rowc", [FOX_H, SEQ])
        cum = sb("cum", [A_HEADS, 2, P + SEQ])
        a_tok = sb("a_tok", [P, NTB, A_HEADS])
        emm = sb("emm", [P, NTB, A_HEADS])
        small = sb("small", [P, 2, 12])
        swab = sb("swab", [P, 2, 2 * CAUSAL])
        tab = sb("tab", [B_HEADS, REL])
        tabr = sb("tabr", [B_HEADS, 512])
        tab_dram = nc.dram_tensor("tab_dram", [B_HEADS, 512], F32, kind="Internal").ap()

        oT = aux[:, 0:ACH * SEQ].rearrange("p (c t) -> p c t", c=ACH)
        hm = aux[:, ACH * SEQ:ACH * SEQ + NTB * A_WIDTH].rearrange("p (b f) -> p b f", b=NTB)
        relb = aux[:, :].rearrange("p (h k) -> p h k", h=B_HEADS)
        PADW = CONV_K - 1 + SEQ
        apad = aux[:, 0:CCH * PADW].rearrange("p (c t) -> p c t", c=CCH)
        cv = aux[:, CCH * PADW:CCH * PADW + CCH * SEQ].rearrange("p (c t) -> p c t", c=CCH)
        csg = aux[:, CCH * (PADW + SEQ):CCH * (PADW + 2 * SEQ)].rearrange("p (c t) -> p c t", c=CCH)
        prow = aux[:, 0:PARAM_TILES * P].rearrange("p (n q) -> p n q", n=PARAM_TILES)
        pool_prod = work[:, 2048 + SEQ:2048 + 2 * SEQ]
        kswap = work[:, 2048:2048 + SEQ]
        hg = qk[:, 0:NCH, :]
        out_rows = qk[:, 8:16, :].rearrange("p (b c) t -> p b (c t)", b=NTB)
        s_sb = nrm[:, :, :].rearrange("p (g c) t -> p g (c t)", g=2)
        pt_sb = work[:, 0:2048].rearrange("p (g n) -> p g n", g=2)
        DIAG_QK = 11 * SEQ // P
        diag_qk = qk[:, 5:16, :].rearrange("p c (a q) -> p (c a) q", a=2)
        diag_aux = aux[:, CCH * (PADW + 2 * SEQ):CCH * (PADW + 2 * SEQ) + (CONV_K - DIAG_QK) * P].rearrange(
            "p (n q) -> p n q", q=P)

        def diag(j):
            return diag_qk[:, j, :] if j < DIAG_QK else diag_aux[:, j - DIAG_QK, :]

        vaug = vals[:, 0:NTB * A_HEADS * VA].rearrange("p (b h e) -> p b h e", b=NTB, h=A_HEADS)
        vtok = vals[:, :].rearrange("p (b f) -> p b f", b=NTB)

        two = [ctx.enter_context(nc.psum_tensor(f"two{j}", [P, 1024], F32)) for j in range(4)]
        bank = [two[j // 2][:, j % 2 * 512:(j % 2 + 1) * 512] for j in range(8)]
        acc, pj, st = bank[0:4], bank[4:7], bank[7]

        raw_landed = [sem(f"raw_landed{r}") for r in range(RING)]
        hi_done = sem("hi_done")
        lo_done = sem("lo_done")
        w_used = sem("w_used")
        evac_act = sem("evac_act")
        evac_dve = sem("evac_dve")
        params_in = sem("params_in")
        tokens_in = [sem("mem_in"), sem("x_in")]
        small_in = sem("small_in")
        gw_in = sem("gw_in")
        consts = sem("consts")
        vec_const = sem("vec_const")
        in_t = sem("in_t")
        mem_hi = sem("mem_hi")
        mem_lo = sem("mem_lo")
        par_ready = sem("par_ready")
        x_ready = sem("x_ready")
        sq_done = sem("sq_done")
        stat = sem("stat")
        sq_sum = sem("sq_sum")
        rstd_ready = sem("rstd_ready")
        tok_ps = sem("tok_ps")
        tok_ready = sem("tok_ready")
        acc_done = sem("acc_done")
        pre_sig = sem("pre_sig")
        hg_done = sem("hg_done")
        std_done = sem("std_done")
        act_hi_done = sem("act_hi_done")
        act_lo_done = sem("act_lo_done")
        ff_raw = sem("ff_raw")
        ff_up = sem("ff_up")
        ff_gate = sem("ff_gate")
        ff_tap = sem("ff_tap")
        ff_conv = sem("ff_conv")
        ff_act = sem("ff_act")
        ff_hid = sem("ff_hid")
        ff_hi = sem("ff_hi")
        ff_lo = sem("ff_lo")
        qk_raw = sem("qk_raw")
        qk_tap = sem("qk_tap")
        qk_conv = sem("qk_conv")
        qk_act = sem("qk_act")
        h_s = sem("h_s")
        h_max = sem("h_max")
        h_exp = sem("h_exp")
        h_p = sem("h_p")
        h_pt = sem("h_pt")
        h_ptc = sem("h_ptc")
        h_o = sem("h_o")
        h_ohi = sem("h_ohi")
        h_olo = sem("h_olo")
        dve_step = sem("dve_step")
        gates_ps = sem("gates_ps")
        gw_split = sem("gw_split")
        gates_z = sem("gates_z")
        gates_e = sem("gates_e")
        gates_lf = sem("gates_lf")
        gates_c = sem("gates_c")
        gates_a = sem("gates_a")
        gates_t = sem("gates_t")
        gates_m = sem("gates_m")
        gates_mt = sem("gates_mt")
        gates_mm = sem("gates_mm")
        gates_em = sem("gates_em")
        ml_bc = sem("ml_bc")
        ml_x = sem("ml_x")
        ml_e = sem("ml_e")
        ml_mask = sem("ml_mask")
        ml_s = sem("ml_s")
        ml_p = sem("ml_p")
        ml_num = sem("ml_num")
        ml_h = sem("ml_h")
        ml_ss = sem("ml_ss")
        ml_std = sem("ml_std")
        ml_hn = sem("ml_hn")
        ml_t = sem("ml_t")
        ml_y = sem("ml_y")
        ml_yhi = sem("ml_yhi")
        ml_ylo = sem("ml_ylo")
        tabr_ready = sem("tabr_ready")
        tab_out = sem("tab_out")
        relb_in = sem("relb_in")
        kswap_in = sem("kswap_in")
        k_ready = sem("k_ready")
        cv_sg = sem("cv_sg")
        cv_pad = sem("cv_pad")
        cv_y = sem("cv_y")
        cv_mu = sem("cv_mu")
        cv_c = sem("cv_c")
        cv_sq = sem("cv_sq")
        cv_var = sem("cv_var")
        cv_std = sem("cv_std")
        cv_z = sem("cv_z")
        cv_silu = sem("cv_silu")
        cv_hi = sem("cv_hi")
        cv_lo = sem("cv_lo")
        swab_ready = sem("swab_ready")
        diags = sem("diags")
        cv_pool = sem("cv_pool")
        cv_prod = sem("cv_prod")
        cv_pe = sem("cv_pe")
        cv_pe_out = sem("cv_pe_out")
        out_t = sem("out_t")
        out_sb = sem("out_sb")
        stored = sem("stored")

        block = ctx.enter_context(nc.Block())

        def cols(c0, c=0, n=1):
            return par[:, c0 + c:c0 + c + n]

        LIGHT = [0, 1, 2, 3, 5, 7, 9, 11, 13, 15]

        def bank_ready(eng, last, j, f):
            if f is None:
                eng.wait_ge(w_used, last - 3 + j + 1)
            elif j < 3:
                eng.wait_ge(acc_done, 3 * f + j + 1)
            else:
                eng.wait_ge(w_used, last + 1)

        evac_of = {}
        counts = {"A": 0, "D": 0}
        parts = [(T_MEM, 4, "D"), (T_AQK, 6, "D"), (T_AV, 3, "D"), (T_AO, 3, "D"), (T_AQM, 1, "D"),
                 (T_KV, 6, "D"), (T_BIN, 4, "D"), (T_AB, 7, "D"), (T_FOX, 12, "D")]
        for first, n, who in parts:
            for t in range(first, first + n):
                counts[who] += 1
                evac_of[t] = (who, counts[who])

        def evacuated(eng, t):
            who, n = evac_of[t]
            eng.wait_ge(evac_act if who == "A" else evac_dve, n)

        def up_view(w):
            return w.rearrange("(c p) n -> p c n", p=P)

        @block.sync
        def _(sp):
            def load(base, src, i=0):
                r = base % RING
                if base >= RING:
                    sp.wait_ge(lo_done, base + RING * i - RING + 1)
                dst = raw[:, r, :].rearrange("p (c n) -> p c n", c=src.shape[1])
                sp.dma_start(dst, src).then_inc(raw_landed[r], 16)

            def project(first, w, starts):
                v = up_view(w)
                for j, n0 in enumerate(starts):
                    load(first + j, v[:, :, n0:n0 + COLS])

            def ffn(t0, w_gate, g0, w_up, u0, w_down):
                gv, uv = up_view(w_gate), up_view(w_up)
                dv = w_down.rearrange("(s c p) n -> s p c n", c=2, p=P)
                load(t0, gv[:, :, g0:g0 + COLS])
                load(t0 + 1, uv[:, :, u0:u0 + COLS])
                g_rest, u_rest = gv[:, :, g0 + COLS:g0 + DFF], uv[:, :, u0 + COLS:u0 + DFF]
                with sp.Fori(1, STEPS) as i:
                    load(t0 - 1, g_rest[:, :, bass.ds((i - 1) * COLS, COLS)], i)
                    load(t0, u_rest[:, :, bass.ds((i - 1) * COLS, COLS)], i)
                    load(t0 + 1, w_down[bass.ds((i - 1) * COLS, COLS), :].rearrange("(c p) n -> p c n", p=P), i)
                load(t0 + RING * STEPS - 1, dv[STEPS - 1])

            def even(n, start=0, step=COLS):
                return [start + step * j for j in range(n)]

            sp.dma_start(qk[:, 0:8, :].rearrange("p (b c) t -> p b (c t)", b=NTB),
                         mem[0].rearrange("(b p) d -> p b d", p=P)).then_inc(tokens_in[0], 16)
            project(T_MEM, mem_w_kv[0], even(2))
            load(T_MEM + 2, up_view(mem_w_kv[1])[:, :, 0:COLS])
            sp.dma_start(qk[:, 8:16, :].rearrange("p (b c) t -> p b (c t)", b=NTB),
                         x[0].rearrange("(b p) d -> p b d", p=P)).then_inc(tokens_in[1], 16)
            load(T_MEM + 3, up_view(mem_w_kv[1])[:, :, COLS:2 * COLS])
            sp.dma_start(gw[:, :, 0:8], up_view(a_w_in[0])[:, :, 3072:3080]).then_inc(gw_in, 16)
            project(T_AQK, a_w_in[0], even(6 + 3 + 3) + [4 * A_WIDTH + 2 * A_HEADS])
            sp.wait_ge(tabr_ready, 1)
            sp.dma_start(tab_dram, tabr[:, :]).then_inc(tab_out, 16)
            project(T_AOUT, a_w_out[0], even(4))
            ffn(T_FF0, ffn_w_up[0], DFF, ffn_w_up[0], 0, ffn_w_down[0])
            sp.wait_ge(x_ready, 2 * NCH)
            sp.wait_ge(tab_out, 16)
            sp.dma_start(relb[:, :, 0:P],
                         bass.AP(tensor=tab_dram.tensor, offset=P, ap=[[1, P], [512, B_HEADS], [1, P]])).then_inc(relb_in, 16)
            sp.dma_start(relb[:, :, P:CAUSAL],
                         bass.AP(tensor=tab_dram.tensor, offset=0, ap=[[1, P], [512, B_HEADS], [1, 2 * P]])).then_inc(relb_in, 16)
            sp.dma_start(gw[:, :, :], up_view(fox_w_in_2[0])[:, :, 3072:3088]).then_inc(gw_in, 16)
            project(T_KV, w_kv, even(6))
            project(T_BIN, b_w_in[0], even(4))
            project(T_BOUT, b_w_out[0], even(4))
            ffn(T_FF1, ffn_w_up[1], DFF, ffn_w_up[1], 0, ffn_w_down[1])
            ffn(T_FF2, ffn_w_gate_2[0, 0], 0, ffn_w_up_2[0, 0], 0, ffn_w_down_2[0, 0])
            project(T_AB, ab_w_in_2[0], [512, 768, 0, 256, 1024, 1280, 1536])
            load(T_ABOUT, up_view(ab_w_out_2[0])[:, :, 0:COLS])
            load(T_ABOUT + 1, up_view(ab_w_out_2[0])[:, :, COLS:2 * COLS])
            sp.wait_ge(k_ready, 1)
            sp.dma_start(kswap[0:64, :], qk[64:128, 4, :]).then_inc(kswap_in, 16)
            sp.dma_start(kswap[64:128, :], qk[0:64, 4, :]).then_inc(kswap_in, 16)
            load(T_ABOUT + 2, up_view(ab_w_out_2[0])[:, :, 2 * COLS:3 * COLS])
            load(T_ABOUT + 3, up_view(ab_w_out_2[0])[:, :, 3 * COLS:4 * COLS])
            ffn(T_FF3, ffn_w_gate_2[0, 1], 0, ffn_w_up_2[0, 1], 0, ffn_w_down_2[0, 1])
            ffn(T_FF4, ffn_w_gate_2[1, 0], 0, ffn_w_up_2[1, 0], 0, ffn_w_down_2[1, 0])
            project(T_FOX, fox_w_in_2[0], even(12))
            project(T_FOXOUT, fox_w_out_2[0], even(4))
            ffn(T_FF5, ffn_w_gate_2[1, 1], 0, ffn_w_up_2[1, 1], 0, ffn_w_down_2[1, 1])
            for b in range(NTB):
                sp.wait_ge(out_sb, 2 * (b + 1))
                sp.dma_start(out[0, b * P:(b + 1) * P, :],
                             out_rows[:, b, :]).then_inc(stored, 16)
            sp.wait_ge(stored, 16 * NTB)

        @block.gpsimd
        def _(pool):
            rows = [(norm_mix_g, 0, 0, 16), (norm_ffn_g, 0, 16, 16), (kv_norm_g, 0, 32, 8), (final_g, 0, 40, 8),
                    (a_conv_w, 0, 48, 48), (a_conv_b, 0, 96, 12), (a_head_g, 0, 108, 6),
                    (norm_g_2, 1, 0, 96), (conv_ln_g_2, 1, 96, 4), (conv_ln_b_2, 1, 100, 4),
                    (ffn_conv_w[0], 2, 0, 66), (ffn_conv_b[0], 2, 66, 22),
                    (ffn_conv_w[1], 3, 0, 66), (ffn_conv_b[1], 3, 66, 22),
                    (conv_w_2, 4, 0, 124), (conv_b_2, 4, 124, 4)]
            nc.gpsimd.memset(prow[:, :, :], 0.0).then_inc(consts, 1)
            nc.gpsimd.memset(ident[:, :], 0.0).then_inc(consts, 1)
            nc.gpsimd.memset(mean_w[:, :], 1.0 / D)
            nc.gpsimd.memset(mean_c[:, :], 1.0 / (CCH * P))
            nc.gpsimd.memset(tri[:, :], 1.0)
            nc.gpsimd.memset(causal[:, :], 0.0)
            nc.gpsimd.memset(turn8[:, :], 0.0)
            nc.gpsimd.memset(zero[:, :], 0.0)
            nc.gpsimd.memset(eps[:, :], EPS)
            nc.gpsimd.memset(cum[:, :, :], 0.0)
            nc.gpsimd.memset(vaug[:, :, :, A_DH:VA], 1.0)
            nc.gpsimd.iota(dist[:, 0:P], [[-1, P]], base=0, channel_multiplier=1, allow_small_or_imprecise_dtypes=True)
            nc.gpsimd.iota(dist[:, P:CAUSAL], [[-1, 2 * P]], base=P, channel_multiplier=1,
                           allow_small_or_imprecise_dtypes=True).then_inc(consts, 1)
            pool.wait_ge(consts, 3)
            for src, tile, at, n in rows:
                dims = "abc"[:len(src.shape) - 1]
                v = src.rearrange(f"{' '.join(dims)} (r q) -> ({' '.join(dims)} r) q".replace("()", ""), q=P) if dims else \
                    src.rearrange("(r q) -> r q", q=P)
                pool.dma_start(prow[at:at + n, tile, :], v).then_inc(params_in, 16)

            def spread(vec, n):
                return bass.AP(tensor=vec.tensor, offset=vec.offset, ap=[[0, P], [1, n]])

            pool.dma_start(gate_b[:, :], spread(a_gate_b, 8)).then_inc(small_in, 16)
            pool.dma_start(fox_b[:, :], spread(fox_b_f_2, FOX_H)).then_inc(small_in, 16)
            pool.dma_start(sink[:, :], spread(swa_sinks_2, SWA_HQ)).then_inc(small_in, 16)
            pool.dma_start(tab[:, :], b_rel_bias[0]).then_inc(small_in, 16)
            nc.gpsimd.affine_select(out=ident[:, :], in_=ident[:, :], compare_op=ALU.not_equal, fill=1.0,
                                    base=0, pattern=[[-1, P]], channel_multiplier=1).then_inc(consts, 1)
            nc.gpsimd.affine_select(out=turn8[:, :], in_=turn8[:, :], compare_op=ALU.not_equal, fill=DH ** 0.5,
                                    base=1 - P, pattern=[[1, P]], channel_multiplier=1).then_inc(consts, 1)
            nc.gpsimd.affine_select(out=tri[:, 0:P], in_=tri[:, 0:P], compare_op=ALU.is_ge, fill=0.0,
                                    base=0, pattern=[[1, P]], channel_multiplier=-1).then_inc(consts, 1)
            nc.gpsimd.affine_select(out=causal[:, :].rearrange("p (a k) -> p a k", a=3)[:, 0:3:2, :],
                                    in_=causal[:, :].rearrange("p (a k) -> p a k", a=3)[:, 0:3:2, :],
                                    compare_op=ALU.is_ge, fill=NEG, base=0, pattern=[[0, 2], [-1, P]],
                                    channel_multiplier=1).then_inc(consts, 1)
            dv = dist[:, :].rearrange("p (a k) -> p a k", a=3)[:, 0:3:2, :]
            nc.gpsimd.affine_select(out=dv, in_=dv, compare_op=ALU.is_ge, fill=-NEG, base=0,
                                    pattern=[[0, 2], [-1, P]], channel_multiplier=1).then_inc(consts, 1)
            nc.gpsimd.affine_select(out=dist[:, P:2 * P], in_=dist[:, P:2 * P], compare_op=ALU.is_gt, fill=-NEG,
                                    base=0, pattern=[[1, P]], channel_multiplier=-1).then_inc(consts, 1)
            for h in range(A_HEADS):
                pool.wait_ge(ml_e, h + 1)
                ev = s_sb[:, h % 2, 0:CAUSAL].rearrange("p (a k) -> p a k", a=3)[:, 0:3:2, :]
                nc.gpsimd.affine_select(out=ev, in_=ev, compare_op=ALU.is_ge, fill=0.0, base=0,
                                        pattern=[[0, 2], [1, P]], channel_multiplier=-1).then_inc(ml_mask, 1)
            pool.wait_ge(relb_in, 32)
            for half in (0, 2):
                v = relb[CHUNK:P, :, half * P + CHUNK:(half + 1) * P]
                ins = nc.gpsimd.memset(v, NEG)
            ins.then_inc(vec_const, 1)
            pool.wait_ge(x_ready, 4 * NCH)
            nc.gpsimd.memset(apad[:, :, 0:CONV_K - 1], 0.0).then_inc(vec_const, 1)

            def alibi(n):
                if n >= 2:
                    pool.wait_ge(h_max, PAIR0["swa"] + n - 1)
                for half in range(2):
                    slope = 2.0 ** (-8.0 * (2 * n + half + 1) / SWA_HQ)
                    nc.gpsimd.tensor_scalar(swab[:, n % 2, half * CAUSAL:(half + 1) * CAUSAL], dist[:, :],
                                            -slope * DH ** 0.5, None, ALU.mult).then_inc(swab_ready, 1)

            alibi(0)
            alibi(1)
            pool.wait_ge(vec_const, 2)
            evacuated(pool, T_AB + 3)
            c = POOL_CHUNK
            for j in range(CONV_K):
                src = apad[:, c, j:j + SEQ]
                if j == 0:
                    nc.gpsimd.tensor_scalar(cv[:, c, :], src, cols(C_CW, c), cols(C_CB, c), ALU.mult, ALU.add).then_inc(cv_pool, 1)
                    continue
                pool.wait_ge(cv_pool, j)
                nc.gpsimd.tensor_scalar(pool_prod, src, cols(C_CW, CCH * j + c), None, ALU.mult).then_inc(cv_prod, 1)
                pool.wait_ge(cv_prod, j)
                nc.gpsimd.tensor_tensor(cv[:, c, :], cv[:, c, :], pool_prod, ALU.add).then_inc(cv_pool, 1)
                if j in (10, 20):
                    alibi(1 + j // 10)

        @block.scalar
        def _(act):
            def split_hi(base, i=0):
                if isinstance(i, int) and base + RING * i >= SLOTS:
                    return
                r = base % RING
                act.wait_ge(raw_landed[r], 16 * (base // RING + i) + 16)
                if base >= RING:
                    act.wait_ge(w_used, base + RING * i - RING + 1)
                nc.scalar.copy(w_hi[:, r, :], raw[:, r, :]).then_inc(hi_done, 1)

            def deviation(n):
                act.wait_ge(stat, n + 1)
                nc.scalar.activation(rstd[:, :], st[:, 0:SEQ], ACT.Sqrt, bias=eps[:, :]).then_inc(std_done, 1)

            def apply_hi(a, col, u, free):
                if free:
                    act.wait_ge(w_used, free)
                for c in range(NCH):
                    act.wait_ge(x_ready, NCH * u + c + 1)
                    nc.scalar.activation(act_hi[:, c, :], xT[:, c, :], ACT.Copy, scale=cols(col, c)).then_inc(act_hi_done, 1)

            def squares():
                for j in range(4):
                    nc.scalar.activation(nrm[:, 2 * j:2 * j + 2, :], xT[:, 2 * j:2 * j + 2, :], ACT.Square).then_inc(sq_done, 2)

            def post_squares(j, last, f):
                bank_ready(act, last, j, f)
                nc.scalar.activation(nrm[:, 2 * j:2 * j + 2, :], acc[j][:, :], ACT.Square).then_inc(sq_done, 2)

            def final_squares(u):
                for j in range(4):
                    act.wait_ge(x_ready, NCH * u + 2 * j + 2)
                    nc.scalar.activation(nrm[:, 2 * j:2 * j + 2, :], xT[:, 2 * j:2 * j + 2, :], ACT.Square).then_inc(sq_done, 2)

            def ffn(f, conv, n):
                t0 = FFN_AT[f]
                first = f == 0

                def gate(t, s, i=0):
                    split_hi(t + 2, i)
                    if isinstance(s, int) and s == 0:
                        deviation(n)
                    act.wait_ge(ff_raw, STEPS * f + s + 1)
                    if conv:
                        act.wait_ge(qk_act, ACH) if first and isinstance(s, int) else act.wait_ge(ff_act, STEPS * f + s)
                        for j in range(2):
                            w2 = par[:, bass.ds(C_FCW[f] + 2 * FCH + 2 * s + j, 1)]
                            bb = par[:, bass.ds(C_FCB[f] + 2 * s + j, 1)]
                            ins = nc.scalar.activation(gate_cv[:, j, :], gate_acc[:, j, :], ACT.Identity, bias=bb, scale=w2)
                        ins.then_inc(ff_gate, 1)
                        act.wait_ge(ff_conv, STEPS * f + s + 1)
                    if not (first and isinstance(s, int)):
                        act.wait_ge(ff_hid, STEPS * f + s)
                    nc.scalar.activation(gate_act[:, :, :], (gate_cv if conv else gate_acc)[:, :, :], ACT.Silu).then_inc(ff_act, 1)

                def up_hi(s):
                    act.wait_ge(ff_hid, STEPS * f + s + 1)
                    nc.scalar.copy(hid_hi[:, :, :], hid[:, :, :]).then_inc(ff_hi, 1)

                gate(t0, 0)
                split_hi(t0 + 3)
                up_hi(0)

                def one(i):
                    gate(t0 - 1, i, i)
                    split_hi(t0 + 2, i)
                    split_hi(t0 + 3, i)
                    act.wait_ge(w_used, t0 + 2 + RING * i)
                    up_hi(i)

                alone = t0 + FFN_SLOTS == SLOTS
                with act.Fori(1, STEPS - alone) as i:
                    one(i)
                if alone:
                    one(STEPS - 1)

            def projection(first, n, take=None, after=None):
                for t in range(first, first + n):
                    split_hi(t + 2)
                    if take:
                        take(t, t - first)
                    if after and t - first in after:
                        after[t - first]()

            def out_projection(first):
                for j in range(4):
                    split_hi(first + j + 2)
                    post_squares(j, first + 3, None)

            def exps(phase, n):
                kind, h, _ = PAIRS[phase][n]
                g = PAIR0[phase] + n
                sm = small[:, g % 2, :]
                act.wait_ge(h_max, g + 1)
                if g >= 2:
                    act.wait_ge(h_pt, g - 1)
                for half in range(2):
                    src = two[2 + g % 2][:, half * 512:] if kind[:3] in ("mem", "ban") else s_sb[:, g % 2, half * 512:]
                    for b, (lo, hi) in enumerate(cuts(kind)):
                        c = 2 * half + b
                        ins = nc.scalar.activation(p_sb[:, g % 2, half * 512 + lo:half * 512 + hi], src[:, lo:hi], ACT.Exp,
                                                   bias=sm[:, c:c + 1], scale=DH ** -0.5, accum_out=sm[:, 4 + c:5 + c])
                if kind == "swa":
                    ins = nc.scalar.activation(sm[:, 8:12], sm[:, 8:12], ACT.Exp)
                ins.then_inc(h_exp, 1)

            def pt_copy(phase, n):
                kind, _, _ = PAIRS[phase][n]
                g, w = PAIR0[phase] + n, width(kind)
                act.wait_ge(h_pt, g + 1)
                if g >= 2:
                    act.wait_ge(h_o, g - 1)
                nc.scalar.copy(pt_sb[:, g % 2, :].rearrange("p (a n) -> p a n", a=2)[:, :, 0:w],
                               two[0][:, :].rearrange("p (a n) -> p a n", a=2)[:, :, 0:w]).then_inc(h_ptc, 1)

            def o_hi(phase, n):
                g, c = PAIR0[phase] + n, PAIRS[phase][n][2]
                act.wait_ge(h_o, g + 1)
                nc.scalar.copy(act_hi[:, c, :], acc[2 + g % 2][:, 0:SEQ]).then_inc(h_ohi, 1)

            def attention(phase):
                last = len(PAIRS[phase])
                for n in range(last + 2):
                    if 1 <= n <= last:
                        pt_copy(phase, n - 1)
                    if n < last:
                        exps(phase, n)
                    if n >= 2:
                        o_hi(phase, n - 2)

            def log_sigmoid(n, k):
                act.wait_ge(gates_z, n)
                nc.scalar.activation(lf_sb[:, :, 0:k], za_sb[:, :, 0:k], ACT.Exp, scale=-1.0).then_inc(gates_e, 1)
                act.wait_ge(gates_e, 2 * n - 1)
                nc.scalar.activation(za_sb[:, :, 0:k], lf_sb[:, :, 0:k], ACT.Ln, bias=1.0).then_inc(gates_e, 1)

            split_hi(0)
            split_hi(1)
            for j in range(4):
                act.wait_ge(in_t, j + 1)
                nc.scalar.copy(act_hi[:, 2 * j:2 * j + 2, :], acc[j][:, :]).then_inc(mem_hi, 1)
            projection(T_MEM, 4)
            act.wait_ge(gw_in, 16)
            nc.scalar.copy(gw_hi[:, :, 0:8], gw[:, :, 0:8]).then_inc(gw_split, 1)
            apply_hi(0, C_MIX, 0, T_MEM + 4)
            squares()

            def take_qk(t, j):
                if j == 0:
                    deviation(0)
                else:
                    act.wait_ge(qk_act, j)
                act.wait_ge(qk_raw, j + 1)
                for m in range(2):
                    c = 2 * j + m
                    ins = nc.scalar.activation(gate_cv[:, m, :], gate_acc[:, m, :], ACT.Identity,
                                               bias=cols(C_ACB, c), scale=cols(C_ACW + 3 * 12, c))
                ins.then_inc(qk_tap, 1)
                act.wait_ge(qk_conv, j + 1)
                nc.scalar.activation(qk[:, 2 * j:2 * j + 2, :], gate_cv[:, :, :], ACT.Silu).then_inc(qk_act, 1)

            def take_o(t, j):
                act.wait_ge(pre_sig, j + 1)
                nc.scalar.activation(oT[:, 2 * j:2 * j + 2, :], gate_acc[:, :, :], ACT.Sigmoid).then_inc(evac_act, 1)

            def a_decay():
                act.wait_ge(gates_mm, 1)
                nc.scalar.activation(emm[:, :, :], emm[:, :, :], ACT.Exp, scale=-1.0).then_inc(gates_em, 1)

            projection(T_AQK, 6, take_qk, {2: lambda: log_sigmoid(1, 4)})
            projection(T_AV, 3, None, {0: a_decay})
            projection(T_AO, 3, take_o)
            projection(T_AQM, 1)
            for h in range(A_HEADS):
                act.wait_ge(ml_x, h + 1)
                nc.scalar.activation(s_sb[:, h % 2, 0:CAUSAL], p_sb[:, h % 2, 0:CAUSAL], ACT.Exp).then_inc(ml_e, 1)
            for h in range(A_HEADS):
                act.wait_ge(ml_h, h + 1)
                if h:
                    act.wait_ge(ml_ss, h)
                for b in range(NTB):
                    ins = nc.scalar.activation(work[:, 2048 + b * SEQ:2048 + b * SEQ + A_DH], hm[:, b, h * A_DH:(h + 1) * A_DH], ACT.Square,
                                               accum_out=small[:, 0, 2 * h + b:2 * h + b + 1])
                ins.then_inc(ml_ss, 1)
            act.wait_ge(ml_ss, A_HEADS)
            nc.scalar.activation(small[:, 1, 0:8], small[:, 0, 0:8], ACT.Sqrt, bias=eps[:, :], scale=1.0 / A_DH).then_inc(ml_std, 1)
            for c in range(ACH):
                act.wait_ge(ml_y, c + 1)
                nc.scalar.copy(act_hi[:, c, :], nrm[:, c, :]).then_inc(ml_yhi, 1)
            attention("a_mem")
            projection(T_AOUT, 4)
            apply_hi(1, C_FFN, 1, T_AOUT + 4)
            squares()
            ffn(0, True, 1)

            apply_hi(2, C_KV, 2, T_KV - 1)
            split_hi(T_KV + 1)
            squares()
            projection(T_KV, 6, None, {0: lambda: deviation(2)})
            apply_hi(3, C_MIX + 8, 2, T_KV + 6)
            projection(T_BIN, 4)
            attention("band")
            projection(T_BOUT, 4)
            apply_hi(4, C_FFN + 8, 3, T_BOUT + 4)
            squares()
            ffn(1, True, 3)

            final_squares(4)
            deviation(4)
            apply_hi(5, C_NG2, 5, T_FF2)
            split_hi(T_FF2 + 1)
            squares()
            ffn(2, False, 5)

            def post(n, last, f):
                for j in range(4):
                    post_squares(j, last, f)
                deviation(n)

            post(6, T_AB - 1, 2)
            apply_hi(6, C_NG2 + 16, 6, T_AB)
            split_hi(T_AB + 1)
            squares()

            def take_gate(t, j):
                if j == 0:
                    deviation(7)
                act.wait_ge(pre_sig, 3 + j + 1)
                nc.scalar.activation(csg[:, 2 * j:2 * j + 2, :], gate_acc[:, :, :], ACT.Sigmoid).then_inc(evac_act, 1)

            projection(T_AB, 2, take_gate)
            projection(T_AB + 2, 2)
            for j in range(CONV_K):
                nc.scalar.activation(diag(j), ident[:, :], ACT.Copy, scale=cols(C_CW, CCH * j + PE_CHUNK)).then_inc(diags, 1)
            projection(T_AB + 4, 3)
            act.wait_ge(cv_pe, 1)
            nc.scalar.activation(cv[:, PE_CHUNK, :], acc[0][:, 0:SEQ], ACT.Identity, bias=cols(C_CB, PE_CHUNK)).then_inc(cv_pe_out, 1)
            attention("swa")
            act.wait_ge(cv_c, 1)
            for c in range(CCH):
                nc.scalar.activation(nrm[:, c, :], cv[:, c, :], ACT.Square).then_inc(cv_sq, 1)
            act.wait_ge(cv_var, 1)
            nc.scalar.activation(rstd[:, :], st[:, SEQ:2 * SEQ], ACT.Sqrt, bias=eps[:, :]).then_inc(cv_std, 1)
            for c in range(CCH):
                act.wait_ge(cv_z, 1)
                nc.scalar.activation(nrm[:, c, :], cv[:, c, :], ACT.Silu, bias=cols(C_LNB, c),
                                     scale=cols(C_LNG, c)).then_inc(cv_silu, 1)
                act.wait_ge(cv_silu, c + 1)
                nc.scalar.copy(act_hi[:, c, :], nrm[:, c, :]).then_inc(cv_hi, 1)
            out_projection(T_ABOUT)
            deviation(8)
            apply_hi(7, C_NG2 + 32, 7, T_ABOUT + 4)
            squares()
            ffn(3, False, 9)
            post(10, T_FF4 - 1, 3)
            apply_hi(8, C_NG2 + 48, 8, T_FF4)
            split_hi(T_FF4 + 1)
            squares()
            ffn(4, False, 11)
            post(12, T_FOX - 1, 4)
            apply_hi(9, C_NG2 + 64, 9, T_FOX)
            split_hi(T_FOX + 1)
            act.wait_ge(gw_in, 32)
            nc.scalar.copy(gw_hi[:, :, :], gw[:, :, :]).then_inc(gw_split, 1)
            squares()

            projection(T_FOX, 12, None, {0: lambda: deviation(13), 2: lambda: log_sigmoid(2, FOX_H)})
            attention("fox")
            out_projection(T_FOXOUT)
            deviation(14)
            apply_hi(10, C_NG2 + 80, 10, T_FOXOUT + 4)
            squares()
            ffn(5, False, 15)
            post(16, SLOTS - 1, 5)
            for b in range(NTB):
                for q in range(2):
                    act.wait_ge(out_t, 2 * b + q + 1)
                    nc.scalar.copy(out_rows[:, b, 512 * q:512 * (q + 1)], acc[2 * b + q][:, :]).then_inc(out_sb, 1)

        @block.vector
        def _(dve):
            chain = [0]

            def step(ins):
                chain[0] += 1
                ins.then_inc(dve_step, 1)
                dve.wait_ge(dve_step, chain[0])

            def split_lo(base, i=0):
                if isinstance(i, int) and base + RING * i >= SLOTS:
                    return
                r = base % RING
                dve.wait_ge(hi_done, base + RING * i + 1)
                nc.vector.tensor_tensor(w_lo[:, r, :], raw[:, r, :], w_hi[:, r, :], ALU.subtract).then_inc(lo_done, 1)

            def deviation(n):
                dve.wait_ge(std_done, n + 1)
                nc.vector.reciprocal(rstd[:, :], rstd[:, :]).then_inc(rstd_ready, 1)
                dve.wait_ge(rstd_ready, n + 1)

            def part(a, col, c):
                dve.wait_ge(act_hi_done, NCH * a + c + 1)
                nc.vector.scalar_tensor_tensor(out=act_lo[:, c, :], in0=xT[:, c, :], scalar=cols(col, c), in1=act_hi[:, c, :],
                                               op0=ALU.mult, op1=ALU.subtract).then_inc(act_lo_done, 1)

            def parts_of(a, col):
                for c in range(NCH):
                    part(a, col, c)

            def sum_squares(n):
                dve.wait_ge(sq_done, NCH * (n + 1))
                step(nc.vector.tensor_tensor(nrm[:, 0:4, :], nrm[:, 0:4, :], nrm[:, 4:8, :], ALU.add))
                nc.vector.tensor_tensor(nrm[:, 0:2, :], nrm[:, 0:2, :], nrm[:, 2:4, :], ALU.add).then_inc(sq_sum, 1)

            def residual(j, last, f):
                bank_ready(dve, last, j, f)
                xs = xT[:, 2 * j:2 * j + 2, :].rearrange("p c t -> p (c t)")
                nc.vector.tensor_tensor(xs, acc[j][:, :], xs, ALU.add).then_inc(x_ready, 2)

            def weigh_output(n, j, col):
                dve.wait_ge(sq_done, NCH * n + 2 * j + 2)
                for c in (2 * j, 2 * j + 1):
                    ins = nc.vector.tensor_scalar(hg[:, c, :], acc[j][:, c % 2 * SEQ:(c % 2 + 1) * SEQ], cols(col, c), None, ALU.mult)
                if j == 3:
                    step(ins)

            def post(n, factor):
                deviation(n)
                for j in range(4):
                    h2, xs = hg[:, 2 * j:2 * j + 2, :], xT[:, 2 * j:2 * j + 2, :]
                    step(nc.vector.tensor_tensor(h2, h2, rstd2, ALU.mult))
                    nc.vector.scalar_tensor_tensor(out=xs, in0=h2, scalar=factor, in1=xs, op0=ALU.mult,
                                                   op1=ALU.add).then_inc(x_ready, 2)

            def ffn_post(n, col):
                for j in range(4):
                    weigh_output(n, j, col)
                post(n, 0.5)

            def ffn(f, conv, n):
                t0 = FFN_AT[f]

                def gate(t, s, i=0):
                    split_lo(t + 2, i)
                    if isinstance(s, int) and s == 0:
                        deviation(n)
                    elif conv:
                        dve.wait_ge(ff_conv, STEPS * f + s)
                    else:
                        dve.wait_ge(ff_act, STEPS * f + s)
                    dve.wait_ge(w_used, t + RING * i + 1)
                    nc.vector.tensor_tensor(gate_acc[:, :, :], pj[t % RING][:, :].rearrange("p (j t) -> p j t", j=2), rstd2,
                                            ALU.mult).then_inc(ff_raw, 1)
                    if conv:
                        dve.wait_ge(ff_gate, STEPS * f + s + 1)
                        for back in (1, 2):
                            if back == 2:
                                dve.wait_ge(ff_tap, STEPS * f + s + 1)
                            for j in range(2):
                                wt = par[:, bass.ds(C_FCW[f] + (2 - back) * FCH + 2 * s + j, 1)]
                                ins = nc.vector.scalar_tensor_tensor(
                                    out=gate_cv[:, j, back:SEQ], in0=gate_acc[:, j, 0:SEQ - back], scalar=wt,
                                    in1=gate_cv[:, j, back:SEQ], op0=ALU.mult, op1=ALU.add)
                            ins.then_inc(ff_tap if back == 1 else ff_conv, 1)

                def up(t, s, i=0):
                    if f or not isinstance(s, int):
                        dve.wait_ge(ff_hid, STEPS * f + s)
                    dve.wait_ge(w_used, t + RING * i + 1)
                    nc.vector.tensor_tensor(up_sc[:, :, :], pj[t % RING][:, :].rearrange("p (j t) -> p j t", j=2), rstd2,
                                            ALU.mult).then_inc(ff_up, 1)
                    if f or not isinstance(s, int):
                        dve.wait_ge(ff_lo, STEPS * f + s)
                    dve.wait_ge(ff_up, STEPS * f + s + 1)
                    dve.wait_ge(ff_act, STEPS * f + s + 1)
                    nc.vector.tensor_tensor(hid[:, :, :], gate_act[:, :, :], up_sc[:, :, :], ALU.mult).then_inc(ff_hid, 1)

                def hid_part(s):
                    dve.wait_ge(ff_hi, STEPS * f + s + 1)
                    nc.vector.tensor_tensor(hid_lo[:, :, :], hid[:, :, :], hid_hi[:, :, :], ALU.subtract).then_inc(ff_lo, 1)

                gate(t0, 0)
                split_lo(t0 + 3)
                up(t0 + 1, 0)
                hid_part(0)

                def one(i):
                    gate(t0 - 1, i, i)
                    split_lo(t0 + 2, i)
                    up(t0, i, i)
                    split_lo(t0 + 3, i)
                    hid_part(i)

                alone = t0 + FFN_SLOTS == SLOTS
                with dve.Fori(1, STEPS - alone) as i:
                    one(i)
                if alone:
                    one(STEPS - 1)

            def projection(first, n, take=None, after=None, before=None):
                for t in range(first, first + n):
                    split_lo(t + 2)
                    if before and t - first in before:
                        before[t - first]()
                    if take:
                        dve.wait_ge(w_used, t + 1)
                        take(t, t - first)
                    if after and t - first in after:
                        after[t - first]()

            def halves(t):
                return pj[t % RING][:, :].rearrange("p (a n) -> p a n", a=2)

            def features_out(dst):
                def take(t, j):
                    nc.vector.tensor_tensor(dst(j), halves(t), rstd2, ALU.mult).then_inc(evac_dve, 1)
                return take

            def tokens_out(dst):
                def take(t, j):
                    for b in range(NTB):
                        ins = nc.vector.tensor_scalar(dst(j)[:, b, :], halves(t)[:, b, :], rtok[:, b:b + 1], None, ALU.mult)
                    ins.then_inc(evac_dve, 1)
                return take

            def token_rstd(n):
                dve.wait_ge(tok_ps, n)
                nc.vector.tensor_copy(rtok[:, :], st[:, SEQ:SEQ + NTB]).then_inc(tok_ready, 1)
                dve.wait_ge(tok_ready, n)

            def scores(phase, n):
                kind, h, _ = PAIRS[phase][n]
                g = PAIR0[phase] + n
                sm, ps, ss = small[:, g % 2, :], two[2 + g % 2], s_sb[:, g % 2, :]
                dve.wait_ge(h_s, g + 1)
                if g >= 2:
                    dve.wait_ge(h_exp, g - 1)
                if kind.startswith("mem"):
                    step(nc.vector.tensor_reduce(sm[:, 0:4], ps[:, :].rearrange("p (a k) -> p a k", a=4), AXX, ALU.max))
                elif kind == "band":
                    for b, (lo, hi) in enumerate(cuts(kind)):
                        ins = nc.vector.tensor_reduce(sm[:, b:4:2], ps[:, :].rearrange("p (a k) -> p a k", a=2)[:, :, lo:hi],
                                                      AXX, ALU.max)
                    step(ins)
                else:
                    if kind == "swa":
                        dve.wait_ge(swab_ready, 2 * n + 2)
                    for half in range(2):
                        bias = swab[:, n % 2, half * CAUSAL:(half + 1) * CAUSAL] if kind == "swa" else causal[:, :]
                        for b, (lo, hi) in enumerate(cuts(kind)):
                            c = 2 * half + b
                            ins = nc.vector.tensor_tensor_reduce(ss[:, half * 512 + lo:half * 512 + hi],
                                                                 ps[:, half * 512 + lo:half * 512 + hi], bias[:, lo:hi],
                                                                 1.0, NEG, ALU.add, ALU.max, sm[:, c:c + 1])
                    step(ins)
                if kind == "swa":
                    sk = sink8[:, h:h + 2].rearrange("p (a b) -> p a b", b=1).to_broadcast([P, 2, 2])
                    sk1 = sink[:, h:h + 2].rearrange("p (a b) -> p a b", b=1).to_broadcast([P, 2, 2])
                    m4 = sm[:, 0:4].rearrange("p (a b) -> p a b", a=2)
                    step(nc.vector.tensor_tensor(m4, m4, sk, ALU.max))
                    step(nc.vector.tensor_scalar(sm[:, 0:4], sm[:, 0:4], -DH ** -0.5, None, ALU.mult))
                    nc.vector.tensor_tensor(sm[:, 8:12].rearrange("p (a b) -> p a b", a=2), m4, sk1, ALU.add).then_inc(h_max, 1)
                else:
                    nc.vector.tensor_scalar(sm[:, 0:4], sm[:, 0:4], -DH ** -0.5, None, ALU.mult).then_inc(h_max, 1)

            def probs(phase, n):
                kind, _, _ = PAIRS[phase][n]
                g = PAIR0[phase] + n
                sm = small[:, g % 2, :]
                dve.wait_ge(h_exp, g + 1)
                if kind == "swa":
                    step(nc.vector.tensor_tensor(sm[:, 4:8], sm[:, 4:8], sm[:, 8:12], ALU.add))
                step(nc.vector.reciprocal(sm[:, 4:8], sm[:, 4:8]))
                for half in range(2):
                    for b, (lo, hi) in enumerate(cuts(kind)):
                        p = p_sb[:, g % 2, half * 512 + lo:half * 512 + hi]
                        ins = nc.vector.tensor_scalar(p, p, sm[:, 4 + 2 * half + b:5 + 2 * half + b], None, ALU.mult)
                ins.then_inc(h_p, 1)

            def o_lo(phase, n):
                g, c = PAIR0[phase] + n, PAIRS[phase][n][2]
                dve.wait_ge(h_ohi, g + 1)
                nc.vector.tensor_tensor(act_lo[:, c, :], acc[2 + g % 2][:, 0:SEQ], act_hi[:, c, :],
                                        ALU.subtract).then_inc(h_olo, 1)

            def attention(phase, between=None):
                last = len(PAIRS[phase])
                for n in range(last + 3):
                    if 1 <= n <= last:
                        probs(phase, n - 1)
                    if n < last:
                        scores(phase, n)
                    if n >= 3:
                        o_lo(phase, n - 3)
                    if between:
                        between(n)

            def log_sigmoid(n, k, bias, zcol):
                dve.wait_ge(gates_ps, n)
                width = zcol + k
                for b in range(NTB):
                    ins = nc.vector.scalar_tensor_tensor(out=z_sb[:, b, 0:width], in0=st[:, b * width:(b + 1) * width],
                                                         scalar=rtok[:, b:b + 1], in1=bias, op0=ALU.mult, op1=ALU.add)
                step(ins)
                zk = z_sb[:, :, zcol:width]
                nc.vector.scalar_tensor_tensor(out=za_sb[:, :, 0:k], in0=zk, scalar=-1.0, in1=zk, op0=ALU.mult,
                                               op1=ALU.max).then_inc(gates_z, 1)
                dve.wait_ge(gates_e, 2 * n)
                nc.vector.scalar_tensor_tensor(out=lf_sb[:, :, 0:k], in0=z_sb[:, :, zcol:width], scalar=0.0,
                                               in1=za_sb[:, :, 0:k], op0=ALU.min, op1=ALU.subtract).then_inc(gates_lf, 1)

            dve.wait_ge(small_in, 64)
            nc.vector.tensor_scalar(sink8[:, :], sink[:, :], DH ** 0.5, None, ALU.mult)
            nc.vector.tensor_copy(tabr[:, 127:127 + REL], tab[:, ::-1])
            nc.vector.tensor_copy(tabr[:, 0:127], tab[:, REL - 1:REL].to_broadcast([B_HEADS, 127]))
            nc.vector.tensor_copy(tabr[:, 127 + REL:512], tab[:, 0:1].to_broadcast([B_HEADS, 512 - 127 - REL])).then_inc(tabr_ready, 1)
            split_lo(0)
            split_lo(1)
            for j in range(4):
                dve.wait_ge(mem_hi, j + 1)
                nc.vector.tensor_tensor(act_lo[:, 2 * j:2 * j + 2, :], acc[j][:, :].rearrange("p (c t) -> p c t", c=2),
                                        act_hi[:, 2 * j:2 * j + 2, :], ALU.subtract).then_inc(mem_lo, 1)
            dve.wait_ge(in_t, 5)
            nc.vector.tensor_copy(par[:, 0:512], pj[0][:, :])
            dve.wait_ge(in_t, 6)
            nc.vector.tensor_copy(par[:, 512:640], pj[1][:, 0:P]).then_inc(par_ready, 1)
            for j in range(4):
                dve.wait_ge(in_t, 7 + j)
                nc.vector.tensor_copy(xT[:, 2 * j:2 * j + 2, :], acc[j][:, :].rearrange("p (c t) -> p c t", c=2)).then_inc(x_ready, 2)

            def take_mem(t, j):
                dst = mv[:, j // 2, :, :] if j % 2 else mk[:, j // 2, :, :]
                nc.vector.tensor_copy(dst, pj[t % RING][:, :].rearrange("p (a n) -> p a n", a=2)).then_inc(evac_dve, 1)

            projection(T_MEM, 4, take_mem)
            dve.wait_ge(gw_split, 1)
            nc.vector.tensor_tensor(gw_lo[:, :, 0:8], gw[:, :, 0:8], gw_hi[:, :, 0:8], ALU.subtract).then_inc(gw_split, 1)
            dve.wait_ge(par_ready, 1)
            parts_of(0, C_MIX)
            sum_squares(0)

            def take_qk(t, j):
                if j == 0:
                    deviation(0)
                else:
                    dve.wait_ge(qk_conv, j)
                nc.vector.tensor_tensor(gate_acc[:, :, :], halves(t), rstd2, ALU.mult).then_inc(qk_raw, 1)
                dve.wait_ge(qk_raw, j + 1)
                dve.sem_inc(evac_dve, 1)
                dve.wait_ge(qk_tap, j + 1)
                for back in (1, 2, 3):
                    for m in range(2):
                        c = 2 * j + m
                        ins = nc.vector.scalar_tensor_tensor(
                            out=gate_cv[:, m, back:SEQ], in0=gate_acc[:, m, 0:SEQ - back],
                            scalar=cols(C_ACW + (3 - back) * 12, c), in1=gate_cv[:, m, back:SEQ], op0=ALU.mult, op1=ALU.add)
                    if back < 3:
                        step(ins)
                ins.then_inc(qk_conv, 1)

            def take_v(t, j):
                at, left = j * COLS, COLS
                while left:
                    h, e = at // A_DH, at % A_DH
                    n = min(left, A_DH - e)
                    off = at - j * COLS
                    for b in range(NTB):
                        ins = nc.vector.tensor_scalar(vaug[:, b, h, e:e + n], halves(t)[:, b, off:off + n], rtok[:, b:b + 1],
                                                      None, ALU.mult)
                    at, left = at + n, left - n
                ins.then_inc(evac_dve, 1)

            def before_sigmoid(k0):
                def take(t, j):
                    if j or not k0:
                        dve.wait_ge(evac_act, k0 + j) if k0 + j else dve.wait_ge(qk_conv, ACH)
                    nc.vector.tensor_tensor(gate_acc[:, :, :], halves(t), rstd2, ALU.mult).then_inc(pre_sig, 1)
                    dve.wait_ge(pre_sig, k0 + j + 1)
                    dve.sem_inc(evac_dve, 1)
                return take

            def a_logs():
                dve.wait_ge(gates_c, 1)
                fv = st[:, 64:72].rearrange("p (b h) -> p b h", b=2)
                nc.vector.tensor_copy(c_sb[:, :, 0:4], fv)
                nc.vector.tensor_tensor(a_tok[:, :, :], z_sb[:, :, 0:4], fv, ALU.subtract).then_inc(gates_a, 1)

            def a_running():
                dve.wait_ge(gates_t, 1)
                step(nc.vector.tensor_scalar(cum[:, 0, P:], st[0:A_HEADS, SEQ:2 * SEQ], 0.0, None, ALU.max))
                for k in range(8):
                    s, d, back = k % 2, (k + 1) % 2, 1 << k
                    step(nc.vector.tensor_tensor(cum[:, d, P:], cum[:, s, P:], cum[:, s, P - back:P + SEQ - back], ALU.max))
                nc.vector.tensor_scalar(rowc[0:A_HEADS, :], cum[:, 0, P:], -1.0, None, ALU.mult).then_inc(gates_m, 1)

            def a_max():
                dve.wait_ge(gates_mt, 1)
                dve.wait_ge(gates_a, 1)
                nc.vector.tensor_tensor(emm[:, :, :], c_sb[:, :, 0:4], st[:, 128:136].rearrange("p (b h) -> p b h", b=2),
                                        ALU.add).then_inc(gates_mm, 1)

            projection(T_AQK, 6, take_qk, {1: lambda: token_rstd(1), 2: lambda: log_sigmoid(1, A_HEADS, gate_b[:, :], A_HEADS),
                                           3: a_logs, 4: a_running})
            projection(T_AV, 3, take_v, {0: a_max})
            projection(T_AO, 3, before_sigmoid(0))
            projection(T_AQM, 1, features_out(lambda j: qm[:, :, :]))

            def decays(h):
                dve.wait_ge(ml_bc, h + 1)
                if h >= 2:
                    dve.wait_ge(ml_e, h - 1)
                bc = pj[h % 2]
                nc.vector.tensor_scalar(p_sb[:, h % 2, 0:SEQ], bc[:, 0:SEQ], a_tok[:, 0, h:h + 1], 0.0, ALU.add, ALU.min)
                nc.vector.tensor_scalar(p_sb[:, h % 2, SEQ:CAUSAL], bc[:, P:SEQ], a_tok[:, 1, h:h + 1], 0.0, ALU.add,
                                        ALU.min).then_inc(ml_x, 1)

            def weigh(h):
                dve.wait_ge(ml_mask, h + 1)
                dve.wait_ge(ml_s, h + 1)
                if h >= 2:
                    dve.wait_ge(ml_num, h - 1)
                nc.vector.scalar_tensor_tensor(out=pt_sb[:, h % 2, 0:CAUSAL], in0=acc[h % 2][:, 0:CAUSAL], scalar=A_DH ** -0.5,
                                               in1=s_sb[:, h % 2, 0:CAUSAL], op0=ALU.mult, op1=ALU.mult).then_inc(ml_p, 1)

            def divide(h):
                dve.wait_ge(ml_num, h + 1)
                num = acc[2 + h % 2][:, 0:2 * VA].rearrange("p (b e) -> p b e", b=2)
                den = small[:, 1, 2 * h:2 * h + 2]
                ps = num[:, :, A_DH:VA].rearrange("p b e -> p (b e)")
                step(nc.vector.scalar_tensor_tensor(out=den, in0=ps, scalar=-1.0, in1=emm[:, :, h:h + 1].rearrange("p b e -> p (b e)"),
                                                    op0=ALU.mult, op1=ALU.max))
                step(nc.vector.tensor_tensor(den, ps, den, ALU.max))
                step(nc.vector.reciprocal(den, den))
                for b in range(NTB):
                    ins = nc.vector.tensor_scalar(hm[:, b, h * A_DH:(h + 1) * A_DH], num[:, b, 0:A_DH], den[:, b:b + 1], None,
                                                  ALU.mult)
                ins.then_inc(ml_h, 1)

            dve.wait_ge(gates_em, 1)
            for n in range(A_HEADS + 2):
                if n < A_HEADS:
                    decays(n)
                if 1 <= n <= A_HEADS:
                    weigh(n - 1)
                if n >= 2:
                    divide(n - 2)
            dve.wait_ge(ml_std, 1)
            step(nc.vector.reciprocal(small[:, 1, 0:8], small[:, 1, 0:8]))
            dve.wait_ge(ml_h, A_HEADS)
            for h in range(A_HEADS):
                for b in range(NTB):
                    hs = hm[:, b, h * A_DH:(h + 1) * A_DH]
                    ins = nc.vector.tensor_scalar(hs, hs, small[:, 1, 2 * h + b:2 * h + b + 1], None, ALU.mult)
            ins.then_inc(ml_hn, 1)
            for c in range(ACH + 1):
                if c < ACH:
                    dve.wait_ge(ml_t, c + 1)
                    if c == 0:
                        dve.wait_ge(evac_act, 3)
                    nc.vector.scalar_tensor_tensor(out=nrm[:, c, :], in0=pj[c % 2][:, 0:SEQ], scalar=cols(C_AHG, c),
                                                   in1=oT[:, c, :], op0=ALU.mult, op1=ALU.mult).then_inc(ml_y, 1)
                if c >= 1:
                    dve.wait_ge(ml_yhi, c)
                    nc.vector.tensor_tensor(act_lo[:, c - 1, :], nrm[:, c - 1, :], act_hi[:, c - 1, :],
                                            ALU.subtract).then_inc(ml_ylo, 1)
            attention("a_mem")
            for j in range(4):
                split_lo(T_AOUT + j + 2)
                residual(j, T_AOUT + 3, None)
            parts_of(1, C_FFN)
            sum_squares(1)
            ffn(0, True, 1)

            def ffn_residual(f, a=None, col=None):
                last = FFN_AT[f] + FFN_SLOTS - 1
                for j in range(5):
                    if j < 4:
                        residual(j, last, f)
                    if j and a is not None:
                        part(a, col, 2 * j - 2)
                        part(a, col, 2 * j - 1)

            ffn_residual(0, 2, C_KV)
            split_lo(T_KV + 1)
            sum_squares(2)
            projection(T_KV, 3, features_out(lambda j: qk[:, 6 + 2 * j:8 + 2 * j, :]), None, {0: lambda: deviation(2)})
            token_rstd(2)
            projection(T_KV + 3, 3, tokens_out(lambda j: vtok[:, :, j * COLS:(j + 1) * COLS]))
            parts_of(3, C_MIX + 8)
            projection(T_BIN, 3, features_out(lambda j: qk[:, 2 * j:2 * j + 2, :]))
            projection(T_BIN + 3, 1, features_out(lambda j: qm[:, :, :]))
            attention("band")
            for j in range(4):
                split_lo(T_BOUT + j + 2)
                residual(j, T_BOUT + 3, None)
            parts_of(4, C_FFN + 8)
            sum_squares(3)
            ffn(1, True, 3)
            ffn_residual(1)

            deviation(4)
            for c in range(NCH):
                nc.vector.scalar_tensor_tensor(out=xT[:, c, :], in0=xT[:, c, :], scalar=cols(C_FINAL, c), in1=rstd[:, :],
                                               op0=ALU.mult, op1=ALU.mult).then_inc(x_ready, 1)
            parts_of(5, C_NG2)
            split_lo(T_FF2 + 1)
            sum_squares(5)
            ffn(2, False, 5)
            ffn_post(6, C_NG2 + 8)
            parts_of(6, C_NG2 + 16)
            split_lo(T_AB + 1)
            sum_squares(7)

            def take_u(t, j):
                if j == 0:
                    dve.wait_ge(evac_act, 5)
                    step(nc.vector.tensor_tensor(csg[:, 0:2, :], csg[:, 0:2, :], rstd2, ALU.mult))
                    step(nc.vector.tensor_tensor(csg[:, 2:4, :], csg[:, 2:4, :], rstd2, ALU.mult))
                nc.vector.tensor_tensor(apad[:, 2 * j:2 * j + 2, CONV_K - 1:], halves(t),
                                        csg[:, 2 * j:2 * j + 2, :], ALU.mult).then_inc(evac_dve, 1)

            def take_kv(t, j):
                nc.vector.tensor_tensor(qk[:, 4, :], pj[t % RING][:, 0:SEQ], rstd[:, :], ALU.mult).then_inc(k_ready, 1)
                for b in range(NTB):
                    ins = nc.vector.tensor_scalar(vtok[:, b, 0:P], pj[t % RING][:, SEQ + b * P:SEQ + (b + 1) * P],
                                                  rtok[:, b:b + 1], None, ALU.mult)
                ins.then_inc(evac_dve, 1)

            projection(T_AB, 2, before_sigmoid(3), None, {0: lambda: deviation(7)})
            token_rstd(3)
            projection(T_AB + 2, 2, take_u)
            projection(T_AB + 4, 2, features_out(lambda j: qk[:, 2 * j:2 * j + 2, :]))
            projection(T_AB + 6, 1, take_kv)
            dve.wait_ge(vec_const, 2)

            taps = [(c, j) for j in range(CONV_K) for c in range(DVE_CHUNKS)]

            def tap(c, j):
                src = apad[:, c, j:j + SEQ]
                if j == 0:
                    nc.vector.tensor_scalar(cv[:, c, :], src, cols(C_CW, c), cols(C_CB, c), ALU.mult, ALU.add).then_inc(cv_y, 1)
                else:
                    dve.wait_ge(cv_y, DVE_CHUNKS * (j - 1) + c + 1)
                    nc.vector.scalar_tensor_tensor(out=cv[:, c, :], in0=src, scalar=cols(C_CW, 4 * j + c), in1=cv[:, c, :],
                                                   op0=ALU.mult, op1=ALU.add).then_inc(cv_y, 1)

            def some_taps(n):
                for _ in range(8):
                    if taps:
                        tap(*taps.pop(0))

            for _ in range(16):
                tap(*taps.pop(0))
            attention("swa", some_taps)
            while taps:
                tap(*taps.pop(0))
            dve.wait_ge(cv_mu, 1)
            dve.wait_ge(cv_y, DVE_CHUNKS * CONV_K)
            for c in range(CCH):
                ins = nc.vector.tensor_tensor(cv[:, c, :], cv[:, c, :], st[:, 0:SEQ], ALU.subtract)
            ins.then_inc(cv_c, 1)
            dve.wait_ge(cv_std, 1)
            step(nc.vector.reciprocal(rstd[:, :], rstd[:, :]))
            dve.wait_ge(cv_c, 1)
            for c in range(CCH):
                ins = nc.vector.tensor_tensor(cv[:, c, :], cv[:, c, :], rstd[:, :], ALU.mult)
            ins.then_inc(cv_z, 1)
            for c in range(CCH):
                dve.wait_ge(cv_hi, c + 1)
                nc.vector.tensor_tensor(act_lo[:, c, :], nrm[:, c, :], act_hi[:, c, :], ALU.subtract).then_inc(cv_lo, 1)

            def out_projection(first, n, col):
                for j in range(4):
                    split_lo(first + j + 2)
                    weigh_output(n, j, col)
                post(n, 1.0)

            out_projection(T_ABOUT, 8, C_NG2 + 24)
            parts_of(7, C_NG2 + 32)
            sum_squares(9)
            ffn(3, False, 9)
            ffn_post(10, C_NG2 + 40)
            parts_of(8, C_NG2 + 48)
            split_lo(T_FF4 + 1)
            sum_squares(11)
            ffn(4, False, 11)
            ffn_post(12, C_NG2 + 56)
            parts_of(9, C_NG2 + 64)
            split_lo(T_FOX + 1)
            dve.wait_ge(gw_split, 3)
            nc.vector.tensor_tensor(gw_lo[:, :, :], gw[:, :, :], gw_hi[:, :, :], ALU.subtract).then_inc(gw_split, 1)
            sum_squares(13)

            def f_sums():
                dve.wait_ge(gates_c, 2)
                nc.vector.tensor_scalar(c_sb[:, :, :], st[:, 64:64 + NTB * FOX_H].rearrange("p (b h) -> p b h", b=2), DH ** 0.5,
                                        None, ALU.mult).then_inc(gates_a, 1)

            def f_rows():
                dve.wait_ge(gates_t, 2)
                nc.vector.tensor_scalar(rowc[:, :], st[0:FOX_H, SEQ:2 * SEQ], -1.0, None, ALU.mult).then_inc(gates_m, 1)

            projection(T_FOX, 8, features_out(lambda j: qk[:, 2 * j:2 * j + 2, :]),
                       {1: lambda: token_rstd(4), 2: lambda: log_sigmoid(2, FOX_H, fox_b[:, :], 0), 3: f_sums, 4: f_rows},
                       {0: lambda: deviation(13)})
            projection(T_FOX + 8, 4, tokens_out(lambda j: vtok[:, :, j * COLS:(j + 1) * COLS]))
            attention("fox")
            out_projection(T_FOXOUT, 14, C_NG2 + 72)
            parts_of(10, C_NG2 + 80)
            sum_squares(15)
            ffn(5, False, 15)
            ffn_post(16, C_NG2 + 88)

        @block.tensor
        def _(pe):
            def three(dst, w, a, start, stop):
                nc.tensor.matmul(dst, w[0], a[0], start=start, stop=False, skip_group_check=True)
                nc.tensor.matmul(dst, w[0], a[1], start=False, stop=False, skip_group_check=True)
                return nc.tensor.matmul(dst, w[1], a[0], start=False, stop=stop, skip_group_check=True)

            def weights(base, lo, n=P):
                r = base % RING
                return w_hi[:, r, lo:lo + n], w_lo[:, r, lo:lo + n]

            def acts(k, lo=0, n=SEQ):
                return act_hi[:, k, lo:lo + n], act_lo[:, k, lo:lo + n]

            def slot_ready(base, i=0):
                pe.wait_ge(lo_done, base + RING * i + 1)

            def feature_major(base, bank, i=0, widths=2):
                slot_ready(base, i)
                for m in range(widths):
                    for k in range(NCH):
                        ins = three(bank[:, m * SEQ:(m + 1) * SEQ], weights(base, k * COLS + m * P), acts(k),
                                    start=k == 0, stop=k == NCH - 1)
                return ins

            def token_major(base, bank, i=0, lo=0, n=COLS, at=0, ready=True):
                if ready:
                    slot_ready(base, i)
                for b in range(NTB):
                    for k in range(NCH):
                        ins = three(bank[:, at + b * n:at + (b + 1) * n], acts(k, b * P, P), weights(base, k * COLS + lo, n),
                                    start=k == 0, stop=k == NCH - 1)
                return ins

            def down(base, i=0, done=None):
                slot_ready(base, i)
                for c in range(NCH):
                    for k in range(2):
                        ins = three(acc[c // 2][:, c % 2 * SEQ:(c % 2 + 1) * SEQ], weights(base, k * D + c * P),
                                    (hid_hi[:, k, :], hid_lo[:, k, :]), start=False, stop=False)
                    if done and c % 2 and c < NCH - 1:
                        ins.then_inc(acc_done, 1)
                        done(c // 2)
                ins.then_inc(w_used, 1)

            def square_mean(n, j):
                pe.wait_ge(sq_done, NCH * n + 2 * j + 2)
                for c in (2 * j, 2 * j + 1):
                    ins = nc.tensor.matmul(st[:, 0:SEQ], mean_w[:, :], nrm[:, c, :], start=c == 0, stop=c == NCH - 1)
                if j == 3:
                    ins.then_inc(stat, 1)

            def light_mean(n):
                pe.wait_ge(sq_sum, LIGHT.index(n) + 1)
                nc.tensor.matmul(st[:, 0:SEQ], mean_w[:, :], nrm[:, 0, :], start=True, stop=False)
                nc.tensor.matmul(st[:, 0:SEQ], mean_w[:, :], nrm[:, 1, :], start=False, stop=True).then_inc(stat, 1)

            def token_rstd(n):
                pe.wait_ge(rstd_ready, n + 1)
                for b in range(NTB):
                    ins = nc.tensor.matmul(st[:, SEQ + b:SEQ + b + 1], rstd[:, b * P:(b + 1) * P], ident[:, 0:1], start=True,
                                           stop=True, skip_group_check=True)
                ins.then_inc(tok_ps, 1)

            def first_slot(base, dst, a):
                slot_ready(base)
                for m in range(2):
                    for k in range(NCH):
                        pe.wait_ge(act_hi_done, NCH * a + k + 1)
                        w, d = weights(base, k * COLS + m * P), dst[:, m * SEQ:(m + 1) * SEQ]
                        nc.tensor.matmul(d, w[0], act_hi[:, k, :], start=k == 0 and m == 0, stop=False, skip_group_check=True)
                        nc.tensor.matmul(d, w[1], act_hi[:, k, :], start=False, stop=False, skip_group_check=True)
                for m in range(2):
                    for k in range(NCH):
                        pe.wait_ge(act_lo_done, NCH * a + k + 1)
                        ins = nc.tensor.matmul(dst[:, m * SEQ:(m + 1) * SEQ], w_hi[:, base % RING, k * COLS + m * P:k * COLS + (m + 1) * P],
                                               act_lo[:, k, :], start=False, stop=k == NCH - 1, skip_group_check=True)
                return ins

            def ffn(f, a, u, n, heavy=None):
                t0 = FFN_AT[f]
                pe.wait_ge(x_ready, NCH * (u + 1))
                for j in range(4):
                    nc.tensor.matmul(acc[j][:, :], zero[:, 0:P], zero[:, :], start=True, stop=True)
                first_slot(t0, pj[t0 % RING], a).then_inc(w_used, 1)
                light_mean(n)
                feature_major(t0 + 1, pj[(t0 + 1) % RING]).then_inc(w_used, 1)
                with pe.Fori(1, STEPS) as i:
                    pe.wait_ge(ff_raw, STEPS * f + i)
                    feature_major(t0 - 1, pj[(t0 - 1) % RING], i).then_inc(w_used, 1)
                    pe.wait_ge(ff_up, STEPS * f + i)
                    feature_major(t0, pj[t0 % RING], i).then_inc(w_used, 1)
                    pe.wait_ge(ff_lo, STEPS * f + i)
                    down(t0 + 1, i)
                pe.wait_ge(ff_lo, STEPS * (f + 1))

                def done(j):
                    if heavy and j:
                        square_mean(heavy, j - 1)

                down(t0 + RING * STEPS - 1, 0, done)
                if heavy:
                    square_mean(heavy, 2)
                    square_mean(heavy, 3)

            def project(first, n, form, a=None, after=None):
                for t in range(first, first + n):
                    if t - RING in evac_of:
                        evacuated(pe, t - RING)
                    if a is not None and t == first:
                        first_slot(t, pj[t % RING], a).then_inc(w_used, 1)
                    else:
                        form(t, pj[t % RING]).then_inc(w_used, 1)
                    if after and t - first in after:
                        after[t - first]()

            def project_out(first, heavy=None):
                for j in range(4):
                    feature_major(first + j, acc[j]).then_inc(w_used, 1)
                    if heavy and j:
                        square_mean(heavy, j - 1)
                if heavy:
                    square_mean(heavy, 3)

            def head_qk(kind, h):
                rows = slice(DH * (h % 2), DH * (h % 2) + DH)
                if kind == "band":
                    return qk[rows, h // 2, :], qk[rows, 6 + h // 2, :]
                if kind == "fox":
                    return qk[rows, h // 2, :], qk[rows, 8 + h // 2, :]
                if kind == "swa":
                    keys = qk[rows, 4, :] if h // 4 == h % 2 else kswap[rows, :]
                    return qk[rows, h // 2, :], keys
                return qm[rows, h // 2, :], mk[rows, int(kind[3]), h // 2, :]

            def head_v(kind, h, b):
                if kind.startswith("mem"):
                    return mv[:, int(kind[3]), b, h * DH:(h + 1) * DH]
                if kind == "swa":
                    h = h // 4
                return vtok[:, b, h * DH:(h + 1) * DH]

            def scores(phase, n):
                kind, h0, _ = PAIRS[phase][n]
                g = PAIR0[phase] + n
                if n >= 2:
                    pe.wait_ge(h_exp, g - 1)
                for half in range(2):
                    h = h0 + half
                    q, k = head_qk(kind, h)
                    dst = two[2 + g % 2][:, half * 512:(half + 1) * 512]
                    for b, (lo, hi) in enumerate(cuts(kind)):
                        ins = nc.tensor.matmul(dst[:, lo:hi], q[:, b * P:(b + 1) * P], k[:, 0:hi - lo], start=True,
                                               stop=kind not in ("fox", "band"), skip_group_check=True)
                        if kind == "fox":
                            ins = nc.tensor.matmul(dst[:, lo:hi], ident[0:FOX_H, h:h + 1].to_broadcast([FOX_H, P]),
                                                   rowc[:, 0:hi - lo], start=False, stop=True, skip_group_check=True)
                        if kind == "band":
                            ins = nc.tensor.matmul(dst[:, lo:hi], turn8[:, :], relb[:, h, lo:hi], start=False, stop=True,
                                                   skip_group_check=True)
                ins.then_inc(h_s, 1)

            def turns(phase, n):
                kind, _, _ = PAIRS[phase][n]
                g = PAIR0[phase] + n
                pe.wait_ge(h_p, g + 1)
                if n >= 1:
                    pe.wait_ge(h_ptc, g)
                blocks = [(0, 0), (256, 128), (128, 256), (384, 384)] if kind.startswith("mem") else \
                    [(0, 0), (128, 128), (256, 256)]
                for half in range(2):
                    for src, dst in blocks:
                        ins = nc.tensor.transpose(acc[half][:, dst:dst + P],
                                                  p_sb[:, g % 2, half * 512 + src:half * 512 + src + P], ident[:, :])
                ins.then_inc(h_pt, 1)

            def values(phase, n):
                kind, h0, _ = PAIRS[phase][n]
                g = PAIR0[phase] + n
                pe.wait_ge(h_ptc, g + 1)
                if n >= 2:
                    pe.wait_ge(h_olo, g - 1)
                for half in range(2):
                    dst = acc[2 + g % 2][DH * half:DH * (half + 1), :]
                    pt = pt_sb[:, g % 2, half * 512:(half + 1) * 512]
                    nc.tensor.matmul(dst[:, 0:SEQ], head_v(kind, h0 + half, 0), pt[:, 0:SEQ], start=True, stop=False,
                                     skip_group_check=True)
                    first = 0 if kind.startswith("mem") else P
                    ins = nc.tensor.matmul(dst[:, first:SEQ], head_v(kind, h0 + half, 1), pt[:, SEQ:2 * SEQ - first],
                                           start=False, stop=True, skip_group_check=True)
                ins.then_inc(h_o, 1)

            def attention(phase):
                last = len(PAIRS[phase])
                for n in range(last + 2):
                    if n < last:
                        scores(phase, n)
                    if 1 <= n <= last:
                        turns(phase, n - 1)
                    if n >= 2:
                        values(phase, n - 2)
                pe.wait_ge(h_olo, PAIR0[phase] + last)

            def narrow(width, n):
                pe.wait_ge(tok_ready, n)
                for b in range(NTB):
                    for k in range(NCH):
                        ins = three(st[:, b * width:(b + 1) * width], acts(k, b * P, P),
                                    (gw_hi[:, k, 0:width], gw_lo[:, k, 0:width]), start=k == 0, stop=k == NCH - 1)
                ins.then_inc(gates_ps, 1)

            def cumulate(n, k):
                pe.wait_ge(gates_lf, n)
                nc.tensor.matmul(st[:, 64:64 + k], tri[:, 0:P], lf_sb[:, 0, 0:k], start=True, stop=True)
                nc.tensor.matmul(st[:, 64 + k:64 + 2 * k], tri[:, P:2 * P], lf_sb[:, 0, 0:k], start=True, stop=False)
                nc.tensor.matmul(st[:, 64 + k:64 + 2 * k], tri[:, 0:P], lf_sb[:, 1, 0:k], start=False, stop=True).then_inc(gates_c, 1)

            pe.wait_ge(consts, 9)
            pe.wait_ge(tokens_in[0], 16)
            tok = [qk[:, 0:8, :].rearrange("p (b c) t -> p b (c t)", b=NTB), qk[:, 8:16, :].rearrange("p (b c) t -> p b (c t)", b=NTB)]

            def turn_tokens(src, waits):
                for j in range(4):
                    if waits:
                        pe.wait_ge(mem_lo, j + 1)
                    for c in range(2):
                        for b in range(NTB):
                            ins = nc.tensor.transpose(acc[j][:, c * SEQ + b * P:c * SEQ + (b + 1) * P],
                                                      src[:, b, (2 * j + c) * P:(2 * j + c + 1) * P], ident[:, :])
                    ins.then_inc(in_t, 1)

            turn_tokens(tok[0], False)
            pe.wait_ge(params_in, 16 * 16)
            for n in range(PARAM_TILES):
                ins = nc.tensor.transpose(pj[n // 4][:, n % 4 * P:(n % 4 + 1) * P], prow[:, n, :], ident[:, :])
                if n in (3, 4):
                    ins.then_inc(in_t, 1)
            pe.wait_ge(tokens_in[1], 16)
            turn_tokens(tok[1], True)
            pe.wait_ge(par_ready, 1)
            for l in range(2):
                for part, form in enumerate((feature_major, token_major)):
                    t = T_MEM + 2 * l + part
                    if t >= RING:
                        evacuated(pe, t - RING)
                    form(t, pj[t % RING]).then_inc(w_used, 1)

            def a_turn():
                pe.wait_ge(gates_a, 1)
                for b in range(NTB):
                    ins = nc.tensor.transpose(st[0:A_HEADS, SEQ + b * P:SEQ + (b + 1) * P], a_tok[:, b, :], ident[:, :])
                ins.then_inc(gates_t, 1)

            def a_back():
                pe.wait_ge(gates_m, 1)
                for b in range(NTB):
                    ins = nc.tensor.matmul(st[:, 128 + 4 * b:132 + 4 * b], cum[:, 0, P + b * P:P + (b + 1) * P],
                                           ident[0:A_HEADS, 0:A_HEADS], start=True, stop=True, skip_group_check=True)
                ins.then_inc(gates_mt, 1)

            pe.wait_ge(gw_split, 2)
            project(T_AQK, 6, feature_major, 0, {0: lambda: light_mean(0), 1: lambda: token_rstd(0), 2: lambda: narrow(8, 1),
                                                 3: lambda: cumulate(1, 4), 4: a_turn})
            project(T_AV, 3, token_major, None, {0: a_back})
            project(T_AO, 3, feature_major)
            project(T_AQM, 1, feature_major)
            for t in range(T_AO + 1, T_AQM + 1):
                evacuated(pe, t)

            def spread(h):
                if h >= 2:
                    pe.wait_ge(ml_x, h - 1)
                nc.tensor.matmul(pj[h % 2][:, 0:SEQ], ident[0:A_HEADS, h:h + 1].to_broadcast([A_HEADS, P]), rowc[0:A_HEADS, :], start=True, stop=True).then_inc(ml_bc, 1)

            def keys_queries(h):
                if h >= 2:
                    pe.wait_ge(ml_p, h - 1)
                pieces = a_head_rows(h)
                for lo, n, s0, t0 in ((0, SEQ, 0, 0), (SEQ, P, P, P)):
                    for i, (c, r0, rows) in enumerate(pieces):
                        rs = slice(r0, r0 + rows)
                        ins = nc.tensor.matmul(acc[h % 2][:, lo:lo + n], qk[rs, ACH + c, s0:s0 + P], qk[rs, c, t0:t0 + n],
                                               start=i == 0, stop=i == len(pieces) - 1, skip_group_check=True)
                ins.then_inc(ml_s, 1)

            def numerator(h):
                pe.wait_ge(ml_p, h + 1)
                if h >= 2:
                    pe.wait_ge(ml_h, h - 1)
                bank = acc[2 + h % 2]
                nc.tensor.matmul(bank[:, 0:VA], pt_sb[:, h % 2, 0:P], vaug[:, 0, h, :], start=True, stop=True, skip_group_check=True)
                nc.tensor.matmul(bank[:, VA:2 * VA], pt_sb[:, h % 2, P:2 * P], vaug[:, 0, h, :], start=True, stop=False, skip_group_check=True)
                nc.tensor.matmul(bank[:, VA:2 * VA], pt_sb[:, h % 2, 2 * P:3 * P], vaug[:, 1, h, :], start=False, stop=True,
                                 skip_group_check=True).then_inc(ml_num, 1)

            pe.wait_ge(qk_act, 6)
            for n in range(A_HEADS + 1):
                if n < A_HEADS:
                    spread(n)
                    keys_queries(n)
                if n >= 1:
                    numerator(n - 1)
            pe.wait_ge(ml_hn, 1)
            for c in range(ACH):
                if c >= 2:
                    pe.wait_ge(ml_y, c - 1)
                for b in range(NTB):
                    ins = nc.tensor.transpose(pj[c % 2][:, b * P:(b + 1) * P], hm[:, b, c * P:(c + 1) * P], ident[:, :])
                ins.then_inc(ml_t, 1)
            pe.wait_ge(ml_ylo, ACH)
            attention("a_mem")
            project_out(T_AOUT)
            ffn(0, 1, 1, 1)

            project(T_KV, 3, feature_major, 2, {0: lambda: light_mean(2), 1: lambda: token_rstd(2)})
            project(T_KV + 3, 3, token_major)
            project(T_BIN, 4, feature_major, 3)
            for t in range(T_BIN + 1, T_BIN + 4):
                evacuated(pe, t)
            pe.wait_ge(vec_const, 1)
            attention("band")
            project_out(T_BOUT)
            ffn(1, 4, 3, 3, heavy=4)
            ffn(2, 5, 5, 5, heavy=6)

            def keys_values(base, bank):
                feature_major(base, bank, widths=1)
                return token_major(base, bank, lo=P, n=P, at=SEQ, ready=False)

            project(T_AB, 6, feature_major, 6, {0: lambda: light_mean(7), 1: lambda: token_rstd(7)})
            project(T_AB + 6, 1, keys_values)
            for t in range(T_AB + 4, T_AB + 7):
                evacuated(pe, t)
            pe.wait_ge(diags, CONV_K)
            pe.wait_ge(vec_const, 2)
            for j in range(CONV_K):
                ins = nc.tensor.matmul(acc[0][:, 0:SEQ], diag(j), apad[:, PE_CHUNK, j:j + SEQ], start=j == 0,
                                       stop=j == CONV_K - 1)
            ins.then_inc(cv_pe, 1)
            pe.wait_ge(cv_pe_out, 1)
            pe.wait_ge(kswap_in, 32)
            attention("swa")
            pe.wait_ge(cv_y, DVE_CHUNKS * CONV_K)
            pe.wait_ge(cv_pool, CONV_K)
            for c in range(CCH):
                ins = nc.tensor.matmul(st[:, 0:SEQ], mean_c[:, :], cv[:, c, :], start=c == 0, stop=c == CCH - 1)
            ins.then_inc(cv_mu, 1)
            for c in range(CCH):
                pe.wait_ge(cv_sq, c + 1)
                ins = nc.tensor.matmul(st[:, SEQ:2 * SEQ], mean_c[:, :], nrm[:, c, :], start=c == 0, stop=c == CCH - 1)
            ins.then_inc(cv_var, 1)
            pe.wait_ge(cv_lo, CCH)
            project_out(T_ABOUT, heavy=8)
            ffn(3, 7, 7, 9, heavy=10)
            ffn(4, 8, 8, 11, heavy=12)

            def f_turn():
                pe.wait_ge(gates_a, 2)
                for b in range(NTB):
                    ins = nc.tensor.transpose(st[0:FOX_H, SEQ + b * P:SEQ + (b + 1) * P], c_sb[:, b, :], ident[:, :])
                ins.then_inc(gates_t, 1)

            project(T_FOX, 8, feature_major, 9,
                    {0: lambda: light_mean(13), 1: lambda: token_rstd(13), 2: lambda: (pe.wait_ge(gw_split, 4), narrow(FOX_H, 4)),
                     3: lambda: cumulate(2, FOX_H), 4: f_turn})
            project(T_FOX + 8, 4, token_major)
            for t in range(T_FOX + 9, T_FOX + 12):
                evacuated(pe, t)
            pe.wait_ge(gates_m, 2)
            attention("fox")
            project_out(T_FOXOUT, heavy=14)
            ffn(5, 10, 10, 15, heavy=16)
            for b in range(NTB):
                for q in range(2):
                    pe.wait_ge(x_ready, NCH * 12)
                    for c in range(4):
                        ins = nc.tensor.transpose(acc[2 * b + q][:, c * P:(c + 1) * P], xT[:, 4 * q + c, b * P:(b + 1) * P], ident[:, :])
                    ins.then_inc(out_t, 1)


INPUTS = ["x", "mem", "norm_mix_g", "norm_ffn_g", "a_w_in", "a_gate_b", "a_conv_w", "a_conv_b", "a_head_g", "a_w_out",
          "kv_norm_g", "w_kv", "b_w_in", "b_rel_bias", "b_w_out", "mem_w_kv", "ffn_w_up", "ffn_conv_w", "ffn_conv_b",
          "ffn_w_down", "final_g", "norm_g_2", "ffn_w_gate_2", "ffn_w_up_2", "ffn_w_down_2", "ab_w_in_2", "conv_w_2",
          "conv_b_2", "conv_ln_g_2", "conv_ln_b_2", "swa_sinks_2", "ab_w_out_2", "fox_w_in_2", "fox_b_f_2", "fox_w_out_2"]


def kernel(**inputs):
    import numpy as np
    import concourse.bacc as bacc
    from concourse.bass_utils import run_bass_kernel_spmd

    nc = bacc.Bacc("TRN2", target_bir_lowering=False, num_devices=1)
    arrays, args = {}, []
    for name in INPUTS:
        a = np.ascontiguousarray(inputs[name])
        arrays[f"in_{name}"] = a
        args.append(nc.dram_tensor(f"in_{name}", a.shape, mybir.dt.from_np(a.dtype), kind="ExternalInput").ap())
    args.append(nc.dram_tensor("out_x", (1, SEQ, D), F32, kind="ExternalOutput").ap())
    build(nc, *args)
    r = run_bass_kernel_spmd(nc, [arrays], core_ids=[0])
    return r.results[0]["out_x"]
```

```python
from contextlib import ExitStack

import concourse.bass as bass
from concourse import mybir

F32 = mybir.dt.float32
F32R = mybir.dt.float32r
BF16 = mybir.dt.bfloat16
ALU = mybir.AluOpType
ACT = mybir.ActivationFunctionType
AXX = mybir.AxisListType.X

P = 128
D = 1024
NCH = D // P
SEQ = 256
NTB = SEQ // P
COLS = 256
RING = 3
SLOTW = NCH * COLS
EPS = 1e-6

DFF = 2816
STEPS = DFF // COLS
FCH = DFF // P

A_WIDTH = 768
A_HEADS = 4
A_DH = A_WIDTH // A_HEADS
A_CONV = 4
ACH = A_WIDTH // P
VA = A_DH + 1
DH = 64
B_HEADS = 12
REL = 192
MAX_REL = 128
CHUNK = 64
MEM_HEADS = 4
MCH = 2
CONV_K = 31
CCH = 4
DVE_CHUNKS = 2
PE_CHUNKS = (3, 2)
SWA_HQ = 8
FOX_H = 16
WINDOW = 128
NEG = -1e30
CAUSAL = 3 * P

T_MEM = 0
T_AQK = T_MEM + 4
T_AV = T_AQK + 6
T_AQM = T_AV + 3
T_AO = T_AQM + 1
T_AOUT = T_AO + 3
T_FF0 = T_AOUT + 4
FFN_SLOTS = 3 * STEPS
T_KV = T_FF0 + FFN_SLOTS
T_BIN = T_KV + 6
T_BOUT = T_BIN + 4
T_FF1 = T_BOUT + 4
T_FF2 = T_FF1 + FFN_SLOTS
T_AB = T_FF2 + FFN_SLOTS
T_ABOUT = T_AB + 7
T_FF3 = T_ABOUT + 4
T_FF4 = T_FF3 + FFN_SLOTS
T_FOX = T_FF4 + FFN_SLOTS
T_FOXOUT = T_FOX + 12
T_FF5 = T_FOXOUT + 4
SLOTS = T_FF5 + FFN_SLOTS
FFN_AT = [T_FF0, T_FF1, T_FF2, T_FF3, T_FF4, T_FF5]

PARAM_TILES = 5
C_MIX, C_FFN, C_KV, C_FINAL, C_ACW, C_ACB, C_AHG = 0, 16, 32, 40, 48, 96, 108
C_NG2, C_LNG, C_LNB = 128, 224, 228
C_FCW = [256, 384]
C_FCB = [256 + 66, 384 + 66]
C_CW, C_CB = 512, 636


def a_head_rows(h):
    at, left, out = h * A_DH, A_DH, []
    while left:
        n = min(left, P - at % P)
        out.append((at // P, at % P, n))
        at, left = at + n, left - n
    return out


def pairs(kind, heads, chunk):
    return [(kind, 2 * j, chunk + j) for j in range(heads // 2)]


PAIRS = {"a_mem": pairs("mem0", MEM_HEADS, 6),
         "band": pairs("band", B_HEADS, 0) + pairs("mem1", MEM_HEADS, 6),
         "swa": pairs("swa", SWA_HQ, 4),
         "fox": pairs("fox", FOX_H, 0)}
PAIR0 = {"a_mem": 0, "band": 2, "swa": 10, "fox": 14}


def width(kind):
    return 512 if kind.startswith("mem") else CAUSAL


def cuts(kind):
    return [(0, 256), (256, 512)] if kind.startswith("mem") else [(0, P), (P, CAUSAL)]


def build(nc, x, mem, norm_mix_g, norm_ffn_g, a_w_in, a_gate_b, a_conv_w, a_conv_b, a_head_g, a_w_out,
          kv_norm_g, w_kv, b_w_in, b_rel_bias, b_w_out, mem_w_kv, ffn_w_up, ffn_conv_w, ffn_conv_b,
          ffn_w_down, final_g, norm_g_2, ffn_w_gate_2, ffn_w_up_2, ffn_w_down_2, ab_w_in_2, conv_w_2,
          conv_b_2, conv_ln_g_2, conv_ln_b_2, swa_sinks_2, ab_w_out_2, fox_w_in_2, fox_b_f_2,
          fox_w_out_2, out):
    ctx = ExitStack()
    with ctx:
        def sb(name, shape, dt=F32):
            return ctx.enter_context(nc.sbuf_tensor(name, shape, dt))

        def sem(name):
            return ctx.enter_context(nc.semaphore(name))

        raw = sb("raw", [P, RING, SLOTW])
        w_hi = sb("w_hi", [P, RING, SLOTW], F32R)
        w_lo = sb("w_lo", [P, RING, SLOTW], F32R)
        xT = sb("xT", [P, NCH, SEQ])
        act_hi = sb("act_hi", [P, NCH, SEQ], F32R)
        act_lo = sb("act_lo", [P, NCH, SEQ], F32R)
        nrm = sb("nrm", [P, NCH, SEQ])
        rstd = sb("rstd", [P, SEQ])
        rstd2 = rstd[:, :].rearrange("p (a t) -> p a t", a=1).to_broadcast([P, 2, SEQ])
        work = sb("work", [P, 5 * 2 * SEQ])
        gate_acc, gate_act, hid, gate_cv, up_sc = (
            work[:, j * 2 * SEQ:(j + 1) * 2 * SEQ].rearrange("p (m t) -> p m t", m=2) for j in range(5))
        rtok = sb("rtok", [P, NTB])
        hid_hi = sb("hid_hi", [P, 2, SEQ], F32R)
        hid_lo = sb("hid_lo", [P, 2, SEQ], F32R)
        qk = sb("qk", [P, 16, SEQ])
        vals = sb("vals", [P, NTB * D])
        qm = sb("qm", [P, MCH, SEQ])
        mk = sb("mk", [P, 2, MCH, SEQ])
        mv = sb("mv", [P, 2, NTB, MCH * P])
        p_sb = sb("p_sb", [P, 2, 2 * 512])
        ident = sb("ident", [P, P])
        mean_w = sb("mean_w", [P, P])
        mean_c = sb("mean_c", [P, P])
        turn8 = sb("turn8", [P, P])
        tri = sb("tri", [P, 2 * P])
        causal = sb("causal", [P, CAUSAL])
        dist = sb("dist", [P, CAUSAL])
        fetch = sb("fetch", [P, 1])
        eps = sb("eps", [P, 1])
        zero = sb("zero", [P, 512], BF16)
        par = sb("par", [P, PARAM_TILES * P])
        gate_b = sb("gate_b", [P, 2 * A_HEADS])
        fox_b = sb("fox_b", [P, FOX_H])
        sink = sb("sink", [P, SWA_HQ])
        sink8 = sb("sink8", [P, SWA_HQ])
        gw = sb("gw", [P, NCH, FOX_H])
        gw_hi = sb("gw_hi", [P, NCH, FOX_H], F32R)
        gw_lo = sb("gw_lo", [P, NCH, FOX_H], F32R)
        z_sb = sb("z_sb", [P, NTB, FOX_H])
        za_sb = sb("za_sb", [P, NTB, FOX_H])
        lf_sb = sb("lf_sb", [P, NTB, FOX_H])
        c_sb = sb("c_sb", [P, NTB, FOX_H])
        rowc = sb("rowc", [FOX_H, SEQ])
        rowf = sb("rowf", [FOX_H, 2, SEQ], F32R)
        pick = sb("pick", [FOX_H, FOX_H], F32R)
        cum = sb("cum", [A_HEADS, 2, P + SEQ])
        a_tok = sb("a_tok", [P, NTB, A_HEADS])
        emm = sb("emm", [P, NTB, A_HEADS])
        small = sb("small", [P, 2, 12])
        swab = sb("swab", [P, 2, 2 * CAUSAL])
        tab = sb("tab", [B_HEADS, REL])
        tabr = sb("tabr", [B_HEADS, 512])
        with nc.sbuf_tensor("aux", [P, B_HEADS * CAUSAL], F32) as aux:
            pass
        fox_parts = sb("fox_parts", [P, 2, NCH, SEQ], F32R)
        tab_dram = nc.dram_tensor("tab_dram", [B_HEADS, 512], F32, kind="Internal").ap()

        oT = aux[:, 0:ACH * SEQ].rearrange("p (c t) -> p c t", c=ACH)
        hm = aux[:, ACH * SEQ:ACH * SEQ + NTB * A_WIDTH].rearrange("p (b f) -> p b f", b=NTB)
        relb = aux[:, :].rearrange("p (h k) -> p h k", h=B_HEADS)
        PADW = CONV_K - 1 + SEQ
        apad = aux[:, 0:CCH * PADW].rearrange("p (c t) -> p c t", c=CCH)
        cv = aux[:, CCH * PADW:CCH * PADW + CCH * SEQ].rearrange("p (c t) -> p c t", c=CCH)
        csg = aux[:, CCH * (PADW + SEQ):CCH * (PADW + 2 * SEQ)].rearrange("p (c t) -> p c t", c=CCH)
        prow = aux[:, 0:PARAM_TILES * P].rearrange("p (n q) -> p n q", n=PARAM_TILES)
        kswap = work[:, 2048:2048 + SEQ]
        hg = qk[:, 0:NCH, :]
        out_rows = qk[:, 8:16, :].rearrange("p (b c) t -> p b (c t)", b=NTB)
        s_sb = nrm[:, :, :].rearrange("p (g c) t -> p g (c t)", g=2)
        pt_sb = work[:, 0:2048].rearrange("p (g n) -> p g n", g=2)
        DIAG_QK = 11 * SEQ // P
        diag_qk = qk[:, 5:16, :].rearrange("p c (a q) -> p (c a) q", a=2)
        diag_aux = aux[:, CCH * (PADW + 2 * SEQ):CCH * (PADW + 2 * SEQ) + (CONV_K - DIAG_QK) * P].rearrange(
            "p (n q) -> p n q", q=P)

        fox_hi, fox_lo = fox_parts[:, 0, :, :], fox_parts[:, 1, :, :]

        def out_parts(kind, c):
            if kind == "fox":
                return fox_hi[:, c, :], fox_lo[:, c, :]
            if kind == "mem0":
                return hid_hi[:, c - ACH, :], hid_lo[:, c - ACH, :]
            return act_hi[:, c, :], act_lo[:, c, :]

        def diag(j):
            return diag_qk[:, j, :] if j < DIAG_QK else diag_aux[:, j - DIAG_QK, :]

        vaug = vals[:, 0:NTB * A_HEADS * VA].rearrange("p (b h e) -> p b h e", b=NTB, h=A_HEADS)
        vtok = vals[:, :].rearrange("p (b f) -> p b f", b=NTB)

        two = [ctx.enter_context(nc.psum_tensor(f"two{j}", [P, 1024], F32)) for j in range(4)]
        bank = [two[j // 2][:, j % 2 * 512:(j % 2 + 1) * 512] for j in range(8)]
        acc, pj, st = bank[0:4], bank[4:7], bank[7]

        place, before = {}, {}
        for phase, ways in (("a_mem", (0, 1)), ("band", (0, 1, 2, 3) * 2), ("swa", (1, 2, 3, 1)), ("fox", (0, 1, 0, 1, 0, 1, 2, 3))):
            for n, way in enumerate(ways):
                earlier = [k for k in range(n) if ways[k] == way]
                place[PAIR0[phase] + n] = two[way]
                before[PAIR0[phase] + n] = PAIR0[phase] + earlier[-1] + 1 if earlier else 0

        raw_landed = [sem(f"raw_landed{r}") for r in range(RING)]
        hi_done = sem("hi_done")
        lo_done = sem("lo_done")
        w_used = sem("w_used")
        evac_act = sem("evac_act")
        evac_dve = sem("evac_dve")
        ident_ready = sem("ident_ready")
        prow_clear = sem("prow_clear")
        params_in = sem("params_in")
        tokens_in = [sem("mem_in"), sem("x_in")]
        small_in = sem("small_in")
        gw_in = sem("gw_in")
        consts = sem("consts")
        vec_const = sem("vec_const")
        in_t = sem("in_t")
        mem_hi = sem("mem_hi")
        mem_lo = sem("mem_lo")
        par_ready = sem("par_ready")
        x_ready = sem("x_ready")
        sq_done = sem("sq_done")
        stat = sem("stat")
        sq_sum = sem("sq_sum")
        rstd_ready = sem("rstd_ready")
        rstd_spread = sem("rstd_spread")
        tok_ps = sem("tok_ps")
        tok_ready = sem("tok_ready")
        acc_done = sem("acc_done")
        gate_open = sem("gate_open")
        pre_sig = sem("pre_sig")
        hg_done = sem("hg_done")
        std_done = sem("std_done")
        act_hi_done = sem("act_hi_done")
        act_lo_done = sem("act_lo_done")
        ff_raw = sem("ff_raw")
        ff_up = sem("ff_up")
        ff_gate = sem("ff_gate")
        ff_tap = sem("ff_tap")
        ff_conv = sem("ff_conv")
        ff_act = sem("ff_act")
        ff_hid = sem("ff_hid")
        ff_hi = sem("ff_hi")
        ff_lo = sem("ff_lo")
        qk_raw = sem("qk_raw")
        qk_tap = sem("qk_tap")
        qk_conv = sem("qk_conv")
        qk_act = sem("qk_act")
        h_s = sem("h_s")
        h_max = sem("h_max")
        h_exp = sem("h_exp")
        h_p = sem("h_p")
        h_pt = sem("h_pt")
        h_ptc = sem("h_ptc")
        h_o = sem("h_o")
        h_ohi = sem("h_ohi")
        h_olo = sem("h_olo")
        dve_step = sem("dve_step")
        gates_ps = sem("gates_ps")
        gw_split = sem("gw_split")
        gates_z = sem("gates_z")
        gates_e = sem("gates_e")
        gates_lf = sem("gates_lf")
        gates_c = sem("gates_c")
        gates_a = sem("gates_a")
        gates_t = sem("gates_t")
        gates_m = sem("gates_m")
        gates_mt = sem("gates_mt")
        gates_mm = sem("gates_mm")
        gates_em = sem("gates_em")
        ml_bc = sem("ml_bc")
        ml_x = sem("ml_x")
        ml_e = sem("ml_e")
        ml_mask = sem("ml_mask")
        ml_s = sem("ml_s")
        ml_p = sem("ml_p")
        ml_num = sem("ml_num")
        ml_h = sem("ml_h")
        ml_ss = sem("ml_ss")
        ml_std = sem("ml_std")
        ml_hn = sem("ml_hn")
        ml_t = sem("ml_t")
        ml_y = sem("ml_y")
        ml_yhi = sem("ml_yhi")
        ml_ylo = sem("ml_ylo")
        tabr_ready = sem("tabr_ready")
        tab_out = sem("tab_out")
        relb_in = sem("relb_in")
        kswap_in = sem("kswap_in")
        k_ready = sem("k_ready")
        cv_y = sem("cv_y")
        cv_mu = sem("cv_mu")
        cv_c = sem("cv_c")
        cv_sq = sem("cv_sq")
        cv_var = sem("cv_var")
        cv_std = sem("cv_std")
        cv_z = sem("cv_z")
        cv_silu = sem("cv_silu")
        cv_hi = sem("cv_hi")
        cv_lo = sem("cv_lo")
        swab_ready = sem("swab_ready")
        diags = sem("diags")
        cv_tap = sem("cv_tap")
        cv_pe = sem("cv_pe")
        cv_pe_out = sem("cv_pe_out")
        out_t = sem("out_t")
        out_sb = sem("out_sb")
        stored = sem("stored")

        block = ctx.enter_context(nc.Block())

        def cols(c0, c=0, n=1):
            return par[:, c0 + c:c0 + c + n]

        LIGHT = [0, 1, 2, 3, 5, 7, 9, 11, 13, 15]
        HEAVY = [4, 6, 8, 10, 12, 14, 16]

        def bank_ready(eng, last, j, f):
            if f is None:
                eng.wait_ge(w_used, last - 3 + j + 1)
            elif j < 3:
                eng.wait_ge(acc_done, 3 * f + j + 1)
            else:
                eng.wait_ge(w_used, last + 1)

        evac_of = {}
        counts = {"A": 0, "D": 0}
        parts = [(T_MEM, 4, "D"), (T_AQK, 6, "D"), (T_AV, 3, "D"), (T_AQM, 1, "D"), (T_AO, 3, "D"),
                 (T_KV, 6, "D"), (T_BIN, 4, "D"), (T_AB, 7, "D"), (T_FOX, 12, "D")]
        for first, n, who in parts:
            for t in range(first, first + n):
                counts[who] += 1
                evac_of[t] = (who, counts[who])

        def evacuated(eng, t):
            who, n = evac_of[t]
            eng.wait_ge(evac_act if who == "A" else evac_dve, n)

        def up_view(w):
            return w.rearrange("(c p) n -> p c n", p=P)

        @block.sync
        def _(sp):
            def load(base, src, i=0):
                r = base % RING
                if base >= RING:
                    sp.wait_ge(lo_done, base + RING * i - RING + 1)
                dst = raw[:, r, :].rearrange("p (c n) -> p c n", c=src.shape[1])
                sp.dma_start(dst, src).then_inc(raw_landed[r], 16)

            def project(first, w, starts):
                v = up_view(w)
                for j, n0 in enumerate(starts):
                    load(first + j, v[:, :, n0:n0 + COLS])

            def ffn(t0, w_gate, g0, w_up, u0, w_down):
                gv, uv = up_view(w_gate), up_view(w_up)
                dv = w_down.rearrange("(s c p) n -> s p c n", c=2, p=P)
                load(t0, gv[:, :, g0:g0 + COLS])
                load(t0 + 1, uv[:, :, u0:u0 + COLS])
                g_rest, u_rest = gv[:, :, g0 + COLS:g0 + DFF], uv[:, :, u0 + COLS:u0 + DFF]
                with sp.Fori(1, STEPS) as i:
                    load(t0 - 1, g_rest[:, :, bass.ds((i - 1) * COLS, COLS)], i)
                    load(t0, u_rest[:, :, bass.ds((i - 1) * COLS, COLS)], i)
                    load(t0 + 1, w_down[bass.ds((i - 1) * COLS, COLS), :].rearrange("(c p) n -> p c n", p=P), i)
                load(t0 + RING * STEPS - 1, dv[STEPS - 1])

            def even(n, start=0, step=COLS):
                return [start + step * j for j in range(n)]

            sp.dma_start(qk[:, 0:8, :].rearrange("p (b c) t -> p b (c t)", b=NTB),
                         mem[0].rearrange("(b p) d -> p b d", p=P)).then_inc(tokens_in[0], 16)
            project(T_MEM, mem_w_kv[0], even(2))
            load(T_MEM + 2, up_view(mem_w_kv[1])[:, :, 0:COLS])
            sp.dma_start(qk[:, 8:16, :].rearrange("p (b c) t -> p b (c t)", b=NTB),
                         x[0].rearrange("(b p) d -> p b d", p=P)).then_inc(tokens_in[1], 16)
            load(T_MEM + 3, up_view(mem_w_kv[1])[:, :, COLS:2 * COLS])
            sp.dma_start(gw[:, :, 0:8], up_view(a_w_in[0])[:, :, 3072:3080]).then_inc(gw_in, 16)
            project(T_AQK, a_w_in[0], even(6 + 3) + [4 * A_WIDTH + 2 * A_HEADS] + even(3, 3 * A_WIDTH))
            sp.wait_ge(tabr_ready, 1)
            sp.dma_start(tab_dram, tabr[:, :]).then_inc(tab_out, 16)
            project(T_AOUT, a_w_out[0], even(4))
            ffn(T_FF0, ffn_w_up[0], DFF, ffn_w_up[0], 0, ffn_w_down[0])
            sp.wait_ge(x_ready, 2 * NCH)
            sp.wait_ge(tab_out, 16)
            sp.dma_start(relb[:, :, 0:P],
                         bass.AP(tensor=tab_dram.tensor, offset=P, ap=[[1, P], [512, B_HEADS], [1, P]])).then_inc(relb_in, 16)
            sp.dma_start(relb[:, :, P:CAUSAL],
                         bass.AP(tensor=tab_dram.tensor, offset=0, ap=[[1, P], [512, B_HEADS], [1, 2 * P]])).then_inc(relb_in, 16)
            sp.dma_start(gw[:, :, :], up_view(fox_w_in_2[0])[:, :, 3072:3088]).then_inc(gw_in, 16)
            project(T_KV, w_kv, even(6))
            project(T_BIN, b_w_in[0], even(4))
            project(T_BOUT, b_w_out[0], even(4))
            ffn(T_FF1, ffn_w_up[1], DFF, ffn_w_up[1], 0, ffn_w_down[1])
            ffn(T_FF2, ffn_w_gate_2[0, 0], 0, ffn_w_up_2[0, 0], 0, ffn_w_down_2[0, 0])
            project(T_AB, ab_w_in_2[0], [512, 768, 0, 256, 1024, 1280, 1536])
            load(T_ABOUT, up_view(ab_w_out_2[0])[:, :, 0:COLS])
            load(T_ABOUT + 1, up_view(ab_w_out_2[0])[:, :, COLS:2 * COLS])
            sp.wait_ge(k_ready, 1)
            sp.dma_start(kswap[0:64, :], qk[64:128, 4, :]).then_inc(kswap_in, 16)
            sp.dma_start(kswap[64:128, :], qk[0:64, 4, :]).then_inc(kswap_in, 16)
            load(T_ABOUT + 2, up_view(ab_w_out_2[0])[:, :, 2 * COLS:3 * COLS])
            load(T_ABOUT + 3, up_view(ab_w_out_2[0])[:, :, 3 * COLS:4 * COLS])
            ffn(T_FF3, ffn_w_gate_2[0, 1], 0, ffn_w_up_2[0, 1], 0, ffn_w_down_2[0, 1])
            ffn(T_FF4, ffn_w_gate_2[1, 0], 0, ffn_w_up_2[1, 0], 0, ffn_w_down_2[1, 0])
            project(T_FOX, fox_w_in_2[0], [D * part + COLS * m for m in range(4) for part in range(3)])
            project(T_FOXOUT, fox_w_out_2[0], even(4))
            ffn(T_FF5, ffn_w_gate_2[1, 1], 0, ffn_w_up_2[1, 1], 0, ffn_w_down_2[1, 1])
            for q in range(2):
                for b in range(NTB):
                    sp.wait_ge(out_sb, 2 * q + b + 1)
                    sp.dma_start(out[0, b * P:(b + 1) * P, 512 * q:512 * (q + 1)],
                                 out_rows[:, b, 512 * q:512 * (q + 1)]).then_inc(stored, 16)
            sp.wait_ge(stored, 16 * 2 * NTB)

        @block.gpsimd
        def _(pool):
            nc.gpsimd.memset(ident[:, :], 0.0).then_inc(ident_ready, 1)
            nc.gpsimd.memset(prow[:, :, :], 0.0).then_inc(prow_clear, 1)
            pool.wait_ge(ident_ready, 1)
            nc.gpsimd.affine_select(out=ident[:, :], in_=ident[:, :], compare_op=ALU.not_equal, fill=1.0,
                                    base=0, pattern=[[-1, P]], channel_multiplier=1).then_inc(ident_ready, 1)
            nc.gpsimd.memset(mean_w[:, :], 1.0 / D)
            nc.gpsimd.memset(mean_c[:, :], 1.0 / (CCH * P))
            nc.gpsimd.memset(tri[:, :], 1.0)
            nc.gpsimd.memset(causal[:, :], 0.0)
            nc.gpsimd.memset(turn8[:, :], 0.0)
            nc.gpsimd.memset(zero[:, :], 0.0)
            nc.gpsimd.memset(eps[:, :], EPS)
            nc.gpsimd.memset(cum[:, :, :], 0.0)
            nc.gpsimd.memset(vaug[:, :, :, A_DH:VA], 1.0)
            nc.gpsimd.iota(dist[:, 0:P], [[-1, P]], base=0, channel_multiplier=1, allow_small_or_imprecise_dtypes=True)
            nc.gpsimd.iota(dist[:, P:CAUSAL], [[-1, 2 * P]], base=P, channel_multiplier=1,
                           allow_small_or_imprecise_dtypes=True).then_inc(consts, 1)
            pool.wait_ge(consts, 1)

            def spread(vec, n):
                return bass.AP(tensor=vec.tensor, offset=vec.offset, ap=[[0, P], [1, n]])

            nc.gpsimd.affine_select(out=turn8[:, :], in_=turn8[:, :], compare_op=ALU.not_equal, fill=DH ** 0.5,
                                    base=1 - P, pattern=[[1, P]], channel_multiplier=1).then_inc(consts, 1)
            nc.gpsimd.affine_select(out=tri[:, 0:P], in_=tri[:, 0:P], compare_op=ALU.is_ge, fill=0.0,
                                    base=0, pattern=[[1, P]], channel_multiplier=-1).then_inc(consts, 1)
            nc.gpsimd.affine_select(out=causal[:, :].rearrange("p (a k) -> p a k", a=3)[:, 0:3:2, :],
                                    in_=causal[:, :].rearrange("p (a k) -> p a k", a=3)[:, 0:3:2, :],
                                    compare_op=ALU.is_ge, fill=NEG, base=0, pattern=[[0, 2], [-1, P]],
                                    channel_multiplier=1).then_inc(consts, 1)
            dv = dist[:, :].rearrange("p (a k) -> p a k", a=3)[:, 0:3:2, :]
            nc.gpsimd.affine_select(out=dv, in_=dv, compare_op=ALU.is_ge, fill=-NEG, base=0,
                                    pattern=[[0, 2], [-1, P]], channel_multiplier=1).then_inc(consts, 1)
            nc.gpsimd.affine_select(out=dist[:, P:2 * P], in_=dist[:, P:2 * P], compare_op=ALU.is_gt, fill=-NEG,
                                    base=0, pattern=[[1, P]], channel_multiplier=-1).then_inc(consts, 1)
            rows = [(norm_mix_g, 0, 0, 16), (norm_ffn_g, 0, 16, 16), (kv_norm_g, 0, 32, 8), (final_g, 0, 40, 8),
                    (a_conv_w, 0, 48, 48), (a_conv_b, 0, 96, 12), (a_head_g, 0, 108, 6),
                    (norm_g_2, 1, 0, 96), (conv_ln_g_2, 1, 96, 4), (conv_ln_b_2, 1, 100, 4),
                    (ffn_conv_w[0], 2, 0, 66), (ffn_conv_b[0], 2, 66, 22),
                    (ffn_conv_w[1], 3, 0, 66), (ffn_conv_b[1], 3, 66, 22),
                    (conv_w_2, 4, 0, 124), (conv_b_2, 4, 124, 4)]
            pool.wait_ge(prow_clear, 1)
            for src, tile, at, n in rows:
                dims = "abc"[:len(src.shape) - 1]
                v = src.rearrange(f"{' '.join(dims)} (r q) -> ({' '.join(dims)} r) q", q=P) if dims else \
                    src.rearrange("(r q) -> r q", q=P)
                pool.dma_start(prow[at:at + n, tile, :], v).then_inc(params_in, 16)
            pool.dma_start(gate_b[:, :], spread(a_gate_b, 8)).then_inc(small_in, 16)
            pool.dma_start(fox_b[:, :], spread(fox_b_f_2, FOX_H)).then_inc(small_in, 16)
            pool.dma_start(sink[:, :], spread(swa_sinks_2, SWA_HQ)).then_inc(small_in, 16)
            pool.dma_start(tab[:, :], b_rel_bias[0]).then_inc(small_in, 16)
            for h in range(A_HEADS):
                pool.wait_ge(ml_e, h + 1)
                ev = s_sb[:, h % 2, 0:CAUSAL].rearrange("p (a k) -> p a k", a=3)[:, 0:3:2, :]
                nc.gpsimd.affine_select(out=ev, in_=ev, compare_op=ALU.is_ge, fill=0.0, base=0,
                                        pattern=[[0, 2], [1, P]], channel_multiplier=-1).then_inc(ml_mask, 1)
            pool.wait_ge(relb_in, 32)
            for half in (0, 2):
                v = relb[CHUNK:P, :, half * P + CHUNK:(half + 1) * P]
                ins = nc.gpsimd.memset(v, NEG)
            ins.then_inc(vec_const, 1)
            pool.wait_ge(x_ready, 4 * NCH)
            nc.gpsimd.memset(apad[:, :, 0:CONV_K - 1], 0.0).then_inc(vec_const, 1)

            def alibi(n):
                if n >= 2:
                    pool.wait_ge(h_max, PAIR0["swa"] + n - 1)
                for half in range(2):
                    slope = 2.0 ** (-8.0 * (2 * n + half + 1) / SWA_HQ)
                    nc.gpsimd.tensor_scalar(swab[:, n % 2, half * CAUSAL:(half + 1) * CAUSAL], dist[:, :],
                                            -slope * DH ** 0.5, None, ALU.mult).then_inc(swab_ready, 1)

            pool.wait_ge(x_ready, 7 * NCH)
            for i, c in enumerate(PE_CHUNKS):
                for j in range(CONV_K):
                    if i:
                        pool.wait_ge(cv_tap, j + 1) if j < CONV_K - 1 else pool.wait_ge(cv_pe, 1)
                    nc.gpsimd.tensor_scalar(diag(j), ident[:, :], cols(C_CW, CCH * j + c), None, ALU.mult).then_inc(diags, 1)
                alibi(2 * i)
                alibi(2 * i + 1)

        @block.scalar
        def _(act):
            def split_hi(base, i=0):
                if isinstance(i, int) and base + RING * i >= SLOTS:
                    return
                r = base % RING
                act.wait_ge(raw_landed[r], 16 * (base // RING + i) + 16)
                if base >= RING:
                    act.wait_ge(w_used, base + RING * i - RING + 1)
                nc.scalar.copy(w_hi[:, r, :], raw[:, r, :]).then_inc(hi_done, 1)

            def deviation(n):
                act.wait_ge(stat, n + 1)
                if n in LIGHT:
                    nc.scalar.activation(rstd[:, :], st[:, 0:SEQ], ACT.Sqrt, bias=eps[:, :]).then_inc(std_done, 1)
                else:
                    nc.scalar.activation(rtok[:, :], st[:, SEQ:SEQ + NTB], ACT.Sqrt, bias=eps[:, :]).then_inc(std_done, 1)

            def fetch_sqrt():
                nc.scalar.activation(fetch[:, :], eps[:, :], ACT.Sqrt)

            def apply_hi(a, col, u, free):
                if free:
                    act.wait_ge(w_used, free)
                for c in range(NCH):
                    act.wait_ge(x_ready, NCH * u + c + 1)
                    nc.scalar.activation(act_hi[:, c, :], xT[:, c, :], ACT.Copy, scale=cols(col, c)).then_inc(act_hi_done, 1)

            def squares():
                for j in range(4):
                    nc.scalar.activation(nrm[:, 2 * j:2 * j + 2, :], xT[:, 2 * j:2 * j + 2, :], ACT.Square).then_inc(sq_done, 2)

            def post_squares(j, last, f):
                if j == 0:
                    fetch_sqrt()
                bank_ready(act, last, j, f)
                nc.scalar.activation(nrm[:, 2 * j:2 * j + 2, :], acc[j][:, :], ACT.Square).then_inc(sq_done, 2)

            def final_squares(u):
                fetch_sqrt()
                for j in range(4):
                    act.wait_ge(x_ready, NCH * u + 2 * j + 2)
                    nc.scalar.activation(nrm[:, 2 * j:2 * j + 2, :], xT[:, 2 * j:2 * j + 2, :], ACT.Square).then_inc(sq_done, 2)

            def ffn(f, conv, n):
                t0 = FFN_AT[f]
                first = f == 0

                def gate(t, s, i=0):
                    split_hi(t + 2, i)
                    if isinstance(s, int) and s == 0:
                        deviation(n)
                    act.wait_ge(ff_raw, STEPS * f + s + 1)
                    if conv:
                        act.wait_ge(qk_act, ACH) if first and isinstance(s, int) else act.wait_ge(ff_act, STEPS * f + s)
                        for j in range(2):
                            w2 = par[:, bass.ds(C_FCW[f] + 2 * FCH + 2 * s + j, 1)]
                            bb = par[:, bass.ds(C_FCB[f] + 2 * s + j, 1)]
                            ins = nc.scalar.activation(gate_cv[:, j, :], gate_acc[:, j, :], ACT.Identity, bias=bb, scale=w2)
                        ins.then_inc(ff_gate, 1)
                    split_hi(t + 3, i)
                    if conv:
                        act.wait_ge(ff_conv, STEPS * f + s + 1)
                    if not (first and isinstance(s, int)):
                        act.wait_ge(ff_hid, STEPS * f + s)
                    nc.scalar.activation(gate_act[:, :, :], (gate_cv if conv else gate_acc)[:, :, :], ACT.Silu).then_inc(ff_act, 1)

                def up_hi(s):
                    act.wait_ge(ff_hid, STEPS * f + s + 1)
                    nc.scalar.copy(hid_hi[:, :, :], hid[:, :, :]).then_inc(ff_hi, 1)

                gate(t0, 0)
                up_hi(0)

                def one(i):
                    gate(t0 - 1, i, i)
                    split_hi(t0 + 3, i)
                    act.wait_ge(w_used, t0 + 2 + RING * i)
                    up_hi(i)

                alone = t0 + FFN_SLOTS == SLOTS
                with act.Fori(1, STEPS - alone) as i:
                    one(i)
                if alone:
                    one(STEPS - 1)

            def projection(first, n, take=None, after=None, ahead=()):
                for t in range(first, first + n):
                    if t - first not in ahead:
                        split_hi(t + 2)
                    if take:
                        take(t, t - first)
                    if after and t - first in after:
                        after[t - first]()

            def out_projection(first):
                for j in range(4):
                    split_hi(first + j + 2)
                    post_squares(j, first + 3, None)

            def exps(phase, n):
                kind, h, _ = PAIRS[phase][n]
                g = PAIR0[phase] + n
                sm = small[:, g % 2, :]
                act.wait_ge(h_max, g + 1)
                if g >= 2:
                    act.wait_ge(h_pt, g - 1)
                for half in range(2):
                    src = place[g][:, half * 512:] if kind[:3] in ("mem", "ban") else s_sb[:, g % 2, half * 512:]
                    for b, (lo, hi) in enumerate(cuts(kind)):
                        c = 2 * half + b
                        ins = nc.scalar.activation(p_sb[:, g % 2, half * 512 + lo:half * 512 + hi], src[:, lo:hi], ACT.Exp,
                                                   bias=sm[:, c:c + 1], scale=DH ** -0.5, accum_out=sm[:, 4 + c:5 + c])
                if kind == "swa":
                    ins = nc.scalar.activation(sm[:, 8:12], sm[:, 8:12], ACT.Exp)
                ins.then_inc(h_exp, 1)

            def pt_copy(phase, n):
                kind, _, _ = PAIRS[phase][n]
                g, w = PAIR0[phase] + n, width(kind)
                act.wait_ge(h_pt, g + 1)
                if g >= 2:
                    act.wait_ge(h_o, g - 1)
                nc.scalar.copy(pt_sb[:, g % 2, :].rearrange("p (a n) -> p a n", a=2)[:, :, 0:w],
                               place[g][:, :].rearrange("p (a n) -> p a n", a=2)[:, :, 0:w]).then_inc(h_ptc, 1)

            def o_hi(phase, n):
                g, (kind, _, c) = PAIR0[phase] + n, PAIRS[phase][n]
                act.wait_ge(h_o, g + 1)
                nc.scalar.copy(out_parts(kind, c)[0], place[g][:, 0:SEQ]).then_inc(h_ohi, 1)

            def attention(phase, between=None):
                last = len(PAIRS[phase])
                for n in range(last + 2):
                    if 1 <= n <= last:
                        pt_copy(phase, n - 1)
                    if n < last:
                        exps(phase, n)
                    if n >= 2:
                        o_hi(phase, n - 2)
                    if between:
                        between(n)

            def log_sigmoid(n, k):
                act.wait_ge(gates_z, n)
                nc.scalar.activation(lf_sb[:, :, 0:k], za_sb[:, :, 0:k], ACT.Exp, scale=-1.0).then_inc(gates_e, 1)
                act.wait_ge(gates_e, 2 * n - 1)
                nc.scalar.activation(za_sb[:, :, 0:k], lf_sb[:, :, 0:k], ACT.Ln, bias=1.0).then_inc(gates_e, 1)

            for j in range(4):
                act.wait_ge(in_t, j + 1)
                nc.scalar.copy(act_hi[:, 2 * j:2 * j + 2, :], acc[j][:, :]).then_inc(mem_hi, 1)
                if j == 1:
                    split_hi(0)
            split_hi(1)
            projection(T_MEM, 4)
            act.wait_ge(gw_in, 16)
            nc.scalar.copy(gw_hi[:, :, 0:8], gw[:, :, 0:8]).then_inc(gw_split, 1)
            act.wait_ge(par_ready, 1)
            apply_hi(0, C_MIX, 0, T_MEM + 4)
            squares()

            def take_qk(t, j):
                if j == 0:
                    deviation(0)
                else:
                    act.wait_ge(qk_act, j)
                act.wait_ge(qk_raw, j + 1)
                for m in range(2):
                    c = 2 * j + m
                    ins = nc.scalar.activation(gate_cv[:, m, :], gate_acc[:, m, :], ACT.Identity,
                                               bias=cols(C_ACB, c), scale=cols(C_ACW + 3 * 12, c))
                ins.then_inc(qk_tap, 1)
                split_hi(t + 3)
                act.wait_ge(qk_conv, j + 1)
                nc.scalar.activation(qk[:, 2 * j:2 * j + 2, :], gate_cv[:, :, :], ACT.Silu).then_inc(qk_act, 1)

            def a_decay():
                act.wait_ge(gates_mm, 1)
                nc.scalar.activation(emm[:, :, :], emm[:, :, :], ACT.Exp, scale=-1.0).then_inc(gates_em, 1)

            projection(T_AQK, 6, take_qk, ahead=range(1, 6))
            projection(T_AV, 3, None, {0: lambda: log_sigmoid(1, 4)}, ahead=range(1))
            projection(T_AQM, 1)
            projection(T_AO, 1)
            exps("a_mem", 0)
            projection(T_AO + 1, 1)
            exps("a_mem", 1)
            pt_copy("a_mem", 0)
            projection(T_AO + 2, 1)
            pt_copy("a_mem", 1)
            o_hi("a_mem", 0)
            o_hi("a_mem", 1)
            a_decay()
            for h in range(A_HEADS):
                act.wait_ge(ml_x, h + 1)
                nc.scalar.activation(s_sb[:, h % 2, 0:CAUSAL], p_sb[:, h % 2, 0:CAUSAL], ACT.Exp).then_inc(ml_e, 1)
            act.wait_ge(evac_dve, evac_of[T_AO + 2][1])
            nc.scalar.activation(oT, oT, ACT.Sigmoid).then_inc(gate_open, 1)
            fetch_sqrt()
            for h in range(A_HEADS):
                act.wait_ge(ml_h, h + 1)
                if h:
                    act.wait_ge(ml_ss, h)
                for b in range(NTB):
                    ins = nc.scalar.activation(work[:, 2048 + b * SEQ:2048 + b * SEQ + A_DH], hm[:, b, h * A_DH:(h + 1) * A_DH], ACT.Square,
                                               accum_out=small[:, 0, 2 * h + b:2 * h + b + 1])
                ins.then_inc(ml_ss, 1)
            act.wait_ge(ml_ss, A_HEADS)
            nc.scalar.activation(small[:, 1, 0:8], small[:, 0, 0:8], ACT.Sqrt, bias=eps[:, :], scale=1.0 / A_DH).then_inc(ml_std, 1)
            for c in range(ACH):
                act.wait_ge(ml_y, c + 1)
                nc.scalar.copy(act_hi[:, c, :], nrm[:, c, :]).then_inc(ml_yhi, 1)
            projection(T_AOUT, 4)
            apply_hi(1, C_FFN, 1, T_AOUT + 4)
            squares()
            ffn(0, True, 1)

            split_hi(T_KV + 1)
            apply_hi(2, C_KV, 2, T_KV - 1)
            squares()
            projection(T_KV, 6, None, {0: lambda: deviation(2)})
            apply_hi(3, C_MIX + 8, 2, T_KV + 6)
            projection(T_BIN, 4)
            attention("band")
            projection(T_BOUT, 4)
            apply_hi(4, C_FFN + 8, 3, T_BOUT + 4)
            squares()
            ffn(1, True, 3)

            split_hi(T_FF2 + 1)
            final_squares(4)
            deviation(4)
            apply_hi(5, C_NG2, 5, T_FF2)
            squares()
            ffn(2, False, 5)

            def post(n, last, f):
                split_hi(last + 2)
                for j in range(4):
                    post_squares(j, last, f)
                deviation(n)

            post(6, T_AB - 1, 2)
            apply_hi(6, C_NG2 + 16, 6, T_AB)
            squares()

            def take_gate(t, j):
                if j == 0:
                    deviation(7)
                act.wait_ge(pre_sig, j + 1)
                nc.scalar.activation(csg[:, 2 * j:2 * j + 2, :], up_sc[:, :, :], ACT.Sigmoid).then_inc(evac_act, 1)

            projection(T_AB, 2, take_gate)
            projection(T_AB + 2, 2)
            projection(T_AB + 4, 3)

            def conv_out(i):
                act.wait_ge(cv_pe, i + 1)
                c = PE_CHUNKS[i]
                nc.scalar.activation(cv[:, c, :], acc[i][:, 0:SEQ], ACT.Identity, bias=cols(C_CB, c)).then_inc(cv_pe_out, 1)

            def beside(n):
                if n == 2:
                    conv_out(1)
                if n == 4:
                    act.wait_ge(cv_c, 1)
                    for c in range(CCH):
                        nc.scalar.activation(nrm[:, c, :], cv[:, c, :], ACT.Square).then_inc(cv_sq, 1)
                if n == 5:
                    act.wait_ge(cv_var, 1)
                    nc.scalar.activation(rstd[:, :], acc[1][:, 0:SEQ], ACT.Sqrt, bias=eps[:, :]).then_inc(cv_std, 1)

            conv_out(0)
            attention("swa", beside)
            for c in range(CCH):
                act.wait_ge(cv_z, 1)
                nc.scalar.activation(nrm[:, c, :], cv[:, c, :], ACT.Silu, bias=cols(C_LNB, c),
                                     scale=cols(C_LNG, c)).then_inc(cv_silu, 1)
                act.wait_ge(cv_silu, c + 1)
                nc.scalar.copy(act_hi[:, c, :], nrm[:, c, :]).then_inc(cv_hi, 1)
            out_projection(T_ABOUT)
            deviation(8)
            apply_hi(7, C_NG2 + 32, 7, T_ABOUT + 4)
            squares()
            ffn(3, False, 9)
            post(10, T_FF4 - 1, 3)
            apply_hi(8, C_NG2 + 48, 8, T_FF4)
            squares()
            ffn(4, False, 11)
            post(12, T_FOX - 1, 4)
            apply_hi(9, C_NG2 + 64, 9, T_FOX)
            act.wait_ge(gw_in, 32)
            nc.scalar.copy(gw_hi[:, :, :], gw[:, :, :]).then_inc(gw_split, 1)
            squares()

            split_hi(T_FOX + 2)
            deviation(13)
            split_hi(T_FOX + 3)
            log_sigmoid(2, FOX_H)
            split_hi(T_FOX + 4)
            for m in range(1, 4):
                t, a, b = T_FOX + 3 * m, 2 * m - 2, 2 * m - 1
                split_hi(t + 2)
                exps("fox", a)
                split_hi(t + 3)
                exps("fox", b)
                pt_copy("fox", a)
                split_hi(t + 4)
                pt_copy("fox", b)
                o_hi("fox", a)
                o_hi("fox", b)
            for stage in (exps, pt_copy, o_hi):
                stage("fox", 6)
                stage("fox", 7)
            out_projection(T_FOXOUT)
            deviation(14)
            apply_hi(10, C_NG2 + 80, 10, T_FOXOUT + 4)
            squares()
            ffn(5, False, 15)
            post(16, SLOTS - 1, 5)
            for q in range(2):
                for b in range(NTB):
                    act.wait_ge(out_t, 2 * q + b + 1)
                    nc.scalar.copy(out_rows[:, b, 512 * q:512 * (q + 1)], acc[2 * b + q][:, :]).then_inc(out_sb, 1)

        @block.vector
        def _(dve):
            chain = [0]
            hg_count = [0]

            def step(ins):
                chain[0] += 1
                ins.then_inc(dve_step, 1)
                dve.wait_ge(dve_step, chain[0])

            def split_lo(base, i=0):
                if isinstance(i, int) and base + RING * i >= SLOTS:
                    return
                r = base % RING
                dve.wait_ge(hi_done, base + RING * i + 1)
                nc.vector.tensor_tensor(w_lo[:, r, :], raw[:, r, :], w_hi[:, r, :], ALU.subtract).then_inc(lo_done, 1)

            def deviation(n):
                dve.wait_ge(std_done, n + 1)
                dst = rstd[:, :] if n in LIGHT else rtok[:, :]
                nc.vector.reciprocal(dst, dst).then_inc(rstd_ready, 1)
                if n in LIGHT:
                    dve.wait_ge(rstd_ready, n + 1)
                else:
                    dve.wait_ge(rstd_spread, HEAVY.index(n) + 1)

            def part(a, col, c):
                dve.wait_ge(act_hi_done, NCH * a + c + 1)
                nc.vector.scalar_tensor_tensor(out=act_lo[:, c, :], in0=xT[:, c, :], scalar=cols(col, c), in1=act_hi[:, c, :],
                                               op0=ALU.mult, op1=ALU.subtract).then_inc(act_lo_done, 1)

            def parts_of(a, col):
                for c in range(NCH):
                    part(a, col, c)

            def sum_squares(n):
                dve.wait_ge(sq_done, NCH * (n + 1))
                step(nc.vector.tensor_tensor(nrm[:, 0:4, :], nrm[:, 0:4, :], nrm[:, 4:8, :], ALU.add))
                nc.vector.tensor_tensor(nrm[:, 0:2, :], nrm[:, 0:2, :], nrm[:, 2:4, :], ALU.add).then_inc(sq_sum, 1)

            def residual(j, last, f):
                bank_ready(dve, last, j, f)
                xs = xT[:, 2 * j:2 * j + 2, :].rearrange("p c t -> p (c t)")
                nc.vector.tensor_tensor(xs, acc[j][:, :], xs, ALU.add).then_inc(x_ready, 2)

            def weigh_output(n, j, col):
                dve.wait_ge(sq_done, NCH * n + 2 * j + 2)
                for c in (2 * j, 2 * j + 1):
                    ins = nc.vector.tensor_scalar(hg[:, c, :], acc[j][:, c % 2 * SEQ:(c % 2 + 1) * SEQ], cols(col, c), None, ALU.mult)
                if j == 3:
                    hg_count[0] += 1
                    ins.then_inc(hg_done, 1)
                    dve.wait_ge(hg_done, hg_count[0])

            def post(n, factor):
                deviation(n)
                st2 = st[:, 0:SEQ].rearrange("p (a t) -> p a t", a=1).to_broadcast([P, 2, SEQ])
                for j in range(4):
                    h2, xs = hg[:, 2 * j:2 * j + 2, :], xT[:, 2 * j:2 * j + 2, :]
                    step(nc.vector.tensor_tensor(h2, h2, st2, ALU.mult))
                    nc.vector.scalar_tensor_tensor(out=xs, in0=h2, scalar=factor, in1=xs, op0=ALU.mult,
                                                   op1=ALU.add).then_inc(x_ready, 2)

            def ffn_post(n, col, last):
                split_lo(last + 2)
                for j in range(4):
                    weigh_output(n, j, col)
                post(n, 0.5)

            def ffn(f, conv, n):
                t0 = FFN_AT[f]

                def gate(t, s, i=0):
                    split_lo(t + 2, i)
                    if isinstance(s, int) and s == 0:
                        deviation(n)
                    elif conv:
                        dve.wait_ge(ff_conv, STEPS * f + s)
                    else:
                        dve.wait_ge(ff_act, STEPS * f + s)
                    dve.wait_ge(w_used, t + RING * i + 1)
                    nc.vector.tensor_tensor(gate_acc[:, :, :], pj[t % RING][:, :].rearrange("p (j t) -> p j t", j=2), rstd2,
                                            ALU.mult).then_inc(ff_raw, 1)
                    if conv:
                        dve.wait_ge(ff_gate, STEPS * f + s + 1)
                        for back in (1, 2):
                            if back == 2:
                                dve.wait_ge(ff_tap, STEPS * f + s + 1)
                            for j in range(2):
                                wt = par[:, bass.ds(C_FCW[f] + (2 - back) * FCH + 2 * s + j, 1)]
                                ins = nc.vector.scalar_tensor_tensor(
                                    out=gate_cv[:, j, back:SEQ], in0=gate_acc[:, j, 0:SEQ - back], scalar=wt,
                                    in1=gate_cv[:, j, back:SEQ], op0=ALU.mult, op1=ALU.add)
                            ins.then_inc(ff_tap if back == 1 else ff_conv, 1)

                def up(t, s, i=0):
                    if f or not isinstance(s, int):
                        dve.wait_ge(ff_hid, STEPS * f + s)
                    dve.wait_ge(w_used, t + RING * i + 1)
                    nc.vector.tensor_tensor(up_sc[:, :, :], pj[t % RING][:, :].rearrange("p (j t) -> p j t", j=2), rstd2,
                                            ALU.mult).then_inc(ff_up, 1)
                    if f or not isinstance(s, int):
                        dve.wait_ge(ff_lo, STEPS * f + s)
                    dve.wait_ge(ff_up, STEPS * f + s + 1)
                    dve.wait_ge(ff_act, STEPS * f + s + 1)
                    nc.vector.tensor_tensor(hid[:, :, :], gate_act[:, :, :], up_sc[:, :, :], ALU.mult).then_inc(ff_hid, 1)

                def hid_part(s):
                    dve.wait_ge(ff_hi, STEPS * f + s + 1)
                    nc.vector.tensor_tensor(hid_lo[:, :, :], hid[:, :, :], hid_hi[:, :, :], ALU.subtract).then_inc(ff_lo, 1)

                gate(t0, 0)
                split_lo(t0 + 3)
                up(t0 + 1, 0)
                hid_part(0)

                def one(i):
                    gate(t0 - 1, i, i)
                    split_lo(t0 + 2, i)
                    up(t0, i, i)
                    split_lo(t0 + 3, i)
                    hid_part(i)

                alone = t0 + FFN_SLOTS == SLOTS
                with dve.Fori(1, STEPS - alone) as i:
                    one(i)
                if alone:
                    one(STEPS - 1)

            def projection(first, n, take=None, after=None, before=None):
                for t in range(first, first + n):
                    split_lo(t + 2)
                    if before and t - first in before:
                        before[t - first]()
                    if take:
                        dve.wait_ge(w_used, t + 1)
                        take(t, t - first)
                    if after and t - first in after:
                        after[t - first]()

            def halves(t):
                return pj[t % RING][:, :].rearrange("p (a n) -> p a n", a=2)

            def features_out(dst):
                def take(t, j):
                    nc.vector.tensor_tensor(dst(j), halves(t), rstd2, ALU.mult).then_inc(evac_dve, 1)
                return take

            def tokens_out(dst):
                def take(t, j):
                    for b in range(NTB):
                        ins = nc.vector.tensor_scalar(dst(j)[:, b, :], halves(t)[:, b, :], rtok[:, b:b + 1], None, ALU.mult)
                    ins.then_inc(evac_dve, 1)
                return take

            def token_rstd(n):
                dve.wait_ge(tok_ps, n)
                nc.vector.tensor_copy(rtok[:, :], st[:, SEQ:SEQ + NTB]).then_inc(tok_ready, 1)
                dve.wait_ge(tok_ready, n)

            def scores(phase, n):
                kind, h, _ = PAIRS[phase][n]
                g = PAIR0[phase] + n
                sm, ps, ss = small[:, g % 2, :], place[g], s_sb[:, g % 2, :]
                dve.wait_ge(h_s, g + 1)
                if g >= 2:
                    dve.wait_ge(h_exp, g - 1)
                if kind.startswith("mem"):
                    step(nc.vector.tensor_reduce(sm[:, 0:4], ps[:, :].rearrange("p (a k) -> p a k", a=4), AXX, ALU.max))
                elif kind == "band":
                    for b, (lo, hi) in enumerate(cuts(kind)):
                        ins = nc.vector.tensor_reduce(sm[:, b:4:2], ps[:, :].rearrange("p (a k) -> p a k", a=2)[:, :, lo:hi],
                                                      AXX, ALU.max)
                    step(ins)
                else:
                    if kind == "swa":
                        dve.wait_ge(swab_ready, 2 * n + 2)
                    for half in range(2):
                        bias = swab[:, n % 2, half * CAUSAL:(half + 1) * CAUSAL] if kind == "swa" else causal[:, :]
                        for b, (lo, hi) in enumerate(cuts(kind)):
                            c = 2 * half + b
                            ins = nc.vector.tensor_tensor_reduce(ss[:, half * 512 + lo:half * 512 + hi],
                                                                 ps[:, half * 512 + lo:half * 512 + hi], bias[:, lo:hi],
                                                                 1.0, NEG, ALU.add, ALU.max, sm[:, c:c + 1])
                    step(ins)
                if kind == "swa":
                    sk = sink8[:, h:h + 2].rearrange("p (a b) -> p a b", b=1).to_broadcast([P, 2, 2])
                    sk1 = sink[:, h:h + 2].rearrange("p (a b) -> p a b", b=1).to_broadcast([P, 2, 2])
                    m4 = sm[:, 0:4].rearrange("p (a b) -> p a b", a=2)
                    step(nc.vector.tensor_tensor(m4, m4, sk, ALU.max))
                    step(nc.vector.tensor_scalar(sm[:, 0:4], sm[:, 0:4], -DH ** -0.5, None, ALU.mult))
                    nc.vector.tensor_tensor(sm[:, 8:12].rearrange("p (a b) -> p a b", a=2), m4, sk1, ALU.add).then_inc(h_max, 1)
                else:
                    nc.vector.tensor_scalar(sm[:, 0:4], sm[:, 0:4], -DH ** -0.5, None, ALU.mult).then_inc(h_max, 1)

            def probs(phase, n):
                kind, _, _ = PAIRS[phase][n]
                g = PAIR0[phase] + n
                sm = small[:, g % 2, :]
                dve.wait_ge(h_exp, g + 1)
                if kind == "swa":
                    step(nc.vector.tensor_tensor(sm[:, 4:8], sm[:, 4:8], sm[:, 8:12], ALU.add))
                step(nc.vector.reciprocal(sm[:, 4:8], sm[:, 4:8]))
                for half in range(2):
                    for b, (lo, hi) in enumerate(cuts(kind)):
                        p = p_sb[:, g % 2, half * 512 + lo:half * 512 + hi]
                        ins = nc.vector.tensor_scalar(p, p, sm[:, 4 + 2 * half + b:5 + 2 * half + b], None, ALU.mult)
                ins.then_inc(h_p, 1)

            def o_lo(phase, n):
                g, (kind, _, c) = PAIR0[phase] + n, PAIRS[phase][n]
                hi, lo = out_parts(kind, c)
                dve.wait_ge(h_ohi, g + 1)
                nc.vector.tensor_tensor(lo, place[g][:, 0:SEQ], hi, ALU.subtract).then_inc(h_olo, 1)

            def attention(phase, between=None):
                last = len(PAIRS[phase])
                for n in range(last + 3):
                    if 1 <= n <= last:
                        probs(phase, n - 1)
                    if n >= 3:
                        o_lo(phase, n - 3)
                    if n < last:
                        scores(phase, n)
                    if between:
                        between(n)

            def log_sigmoid(n, k, bias, zcol):
                dve.wait_ge(gates_ps, n)
                width = zcol + k
                for b in range(NTB):
                    ins = nc.vector.scalar_tensor_tensor(out=z_sb[:, b, 0:width], in0=st[:, b * width:(b + 1) * width],
                                                         scalar=rtok[:, b:b + 1], in1=bias, op0=ALU.mult, op1=ALU.add)
                step(ins)
                zk = z_sb[:, :, zcol:width]
                nc.vector.scalar_tensor_tensor(out=za_sb[:, :, 0:k], in0=zk, scalar=-1.0, in1=zk, op0=ALU.mult,
                                               op1=ALU.max).then_inc(gates_z, 1)
                dve.wait_ge(gates_e, 2 * n)
                nc.vector.scalar_tensor_tensor(out=lf_sb[:, :, 0:k], in0=z_sb[:, :, zcol:width], scalar=0.0,
                                               in1=za_sb[:, :, 0:k], op0=ALU.min, op1=ALU.subtract).then_inc(gates_lf, 1)

            for j in range(4):
                dve.wait_ge(mem_hi, j + 1)
                nc.vector.tensor_tensor(act_lo[:, 2 * j:2 * j + 2, :], acc[j][:, :].rearrange("p (c t) -> p c t", c=2),
                                        act_hi[:, 2 * j:2 * j + 2, :], ALU.subtract).then_inc(mem_lo, 1)
                if j == 1:
                    split_lo(0)
            split_lo(1)

            def take_mem(t, j):
                dst = mv[:, j // 2, :, :] if j % 2 else mk[:, j // 2, :, :]
                nc.vector.tensor_copy(dst, pj[t % RING][:, :].rearrange("p (a n) -> p a n", a=2)).then_inc(evac_dve, 1)

            def take_x():
                for j in range(4):
                    dve.wait_ge(in_t, 5 + j)
                    nc.vector.tensor_copy(xT[:, 2 * j:2 * j + 2, :], acc[j][:, :].rearrange("p (c t) -> p c t", c=2)).then_inc(x_ready, 2)

            def take_params():
                dve.wait_ge(in_t, 9)
                nc.vector.tensor_copy(par[:, 0:512], st)
                dve.wait_ge(in_t, 10)
                nc.vector.tensor_copy(par[:, 512:640], acc[0][:, 0:P]).then_inc(par_ready, 1)

            projection(T_MEM, 4, take_mem, {0: take_x, 1: take_params})
            dve.wait_ge(small_in, 64)
            nc.vector.tensor_scalar(sink8[:, :], sink[:, :], DH ** 0.5, None, ALU.mult)
            nc.vector.tensor_copy(tabr[:, 127:127 + REL], tab[:, ::-1])
            nc.vector.tensor_copy(tabr[:, 0:127], tab[:, REL - 1:REL].to_broadcast([B_HEADS, 127]))
            nc.vector.tensor_copy(tabr[:, 127 + REL:512], tab[:, 0:1].to_broadcast([B_HEADS, 512 - 127 - REL])).then_inc(tabr_ready, 1)
            dve.wait_ge(gw_split, 1)
            nc.vector.tensor_tensor(gw_lo[:, :, 0:8], gw[:, :, 0:8], gw_hi[:, :, 0:8], ALU.subtract).then_inc(gw_split, 1)
            dve.wait_ge(par_ready, 1)
            parts_of(0, C_MIX)
            sum_squares(0)

            def take_qk(t, j):
                if j == 0:
                    deviation(0)
                else:
                    dve.wait_ge(qk_conv, j)
                nc.vector.tensor_tensor(gate_acc[:, :, :], halves(t), rstd2, ALU.mult).then_inc(qk_raw, 1)
                dve.wait_ge(qk_raw, j + 1)
                dve.sem_inc(evac_dve, 1)
                dve.wait_ge(qk_tap, j + 1)
                for back in (1, 2, 3):
                    for m in range(2):
                        c = 2 * j + m
                        ins = nc.vector.scalar_tensor_tensor(
                            out=gate_cv[:, m, back:SEQ], in0=gate_acc[:, m, 0:SEQ - back],
                            scalar=cols(C_ACW + (3 - back) * 12, c), in1=gate_cv[:, m, back:SEQ], op0=ALU.mult, op1=ALU.add)
                    if back < 3:
                        step(ins)
                ins.then_inc(qk_conv, 1)

            def take_v(t, j):
                at, left = j * COLS, COLS
                while left:
                    h, e = at // A_DH, at % A_DH
                    n = min(left, A_DH - e)
                    off = at - j * COLS
                    for b in range(NTB):
                        ins = nc.vector.tensor_scalar(vaug[:, b, h, e:e + n], halves(t)[:, b, off:off + n], rtok[:, b:b + 1],
                                                      None, ALU.mult)
                    at, left = at + n, left - n
                ins.then_inc(evac_dve, 1)

            def before_sigmoid(t, j):
                if j:
                    dve.wait_ge(evac_act, j)
                nc.vector.tensor_tensor(up_sc[:, :, :], halves(t), rstd2, ALU.mult).then_inc(pre_sig, 1)
                dve.wait_ge(pre_sig, j + 1)
                dve.sem_inc(evac_dve, 1)

            def a_logs():
                dve.wait_ge(gates_c, 1)
                fv = st[:, 64:72].rearrange("p (b h) -> p b h", b=2)
                nc.vector.tensor_copy(c_sb[:, :, 0:4], fv)
                nc.vector.tensor_tensor(a_tok[:, :, :], z_sb[:, :, 0:4], fv, ALU.subtract).then_inc(gates_a, 1)

            def a_running():
                dve.wait_ge(gates_t, 1)
                step(nc.vector.tensor_scalar(cum[:, 0, P:], st[0:A_HEADS, SEQ:2 * SEQ], 0.0, None, ALU.max))
                for k in range(8):
                    s, d, back = k % 2, (k + 1) % 2, 1 << k
                    step(nc.vector.tensor_tensor(cum[:, d, P:], cum[:, s, P:], cum[:, s, P - back:P + SEQ - back], ALU.max))
                nc.vector.tensor_scalar(rowc[0:A_HEADS, :], cum[:, 0, P:], -1.0, None, ALU.mult).then_inc(gates_m, 1)

            def a_max():
                dve.wait_ge(gates_mt, 1)
                dve.wait_ge(gates_a, 1)
                nc.vector.tensor_tensor(emm[:, :, :], c_sb[:, :, 0:4], st[:, 128:136].rearrange("p (b h) -> p b h", b=2),
                                        ALU.add).then_inc(gates_mm, 1)

            projection(T_AQK, 6, take_qk, {1: lambda: token_rstd(1)})
            projection(T_AV, 3, take_v, {0: lambda: log_sigmoid(1, A_HEADS, gate_b[:, :], A_HEADS), 1: a_logs})
            projection(T_AQM, 1, features_out(lambda j: qm[:, :, :]), {0: a_running})
            gate_out = features_out(lambda j: oT[:, 2 * j:2 * j + 2, :])
            split_lo(T_AO + 2)
            dve.wait_ge(w_used, T_AO + 1)
            gate_out(T_AO, 0)
            scores("a_mem", 0)
            split_lo(T_AO + 3)
            probs("a_mem", 0)
            scores("a_mem", 1)
            dve.wait_ge(w_used, T_AO + 2)
            gate_out(T_AO + 1, 1)
            probs("a_mem", 1)
            split_lo(T_AO + 4)
            a_max()
            o_lo("a_mem", 0)
            dve.wait_ge(w_used, T_AO + 3)
            gate_out(T_AO + 2, 2)
            o_lo("a_mem", 1)

            def decays(h):
                dve.wait_ge(ml_bc, h + 1)
                if h >= 2:
                    dve.wait_ge(ml_e, h - 1)
                bc = pj[h % 2]
                nc.vector.tensor_scalar(p_sb[:, h % 2, 0:SEQ], bc[:, 0:SEQ], a_tok[:, 0, h:h + 1], 0.0, ALU.add, ALU.min)
                nc.vector.tensor_scalar(p_sb[:, h % 2, SEQ:CAUSAL], bc[:, P:SEQ], a_tok[:, 1, h:h + 1], 0.0, ALU.add,
                                        ALU.min).then_inc(ml_x, 1)

            def weigh(h):
                dve.wait_ge(ml_mask, h + 1)
                dve.wait_ge(ml_s, h + 1)
                if h >= 2:
                    dve.wait_ge(ml_num, h - 1)
                nc.vector.scalar_tensor_tensor(out=pt_sb[:, h % 2, 0:CAUSAL], in0=acc[h % 2][:, 0:CAUSAL], scalar=A_DH ** -0.5,
                                               in1=s_sb[:, h % 2, 0:CAUSAL], op0=ALU.mult, op1=ALU.mult).then_inc(ml_p, 1)

            def divide(h):
                dve.wait_ge(ml_num, h + 1)
                num = acc[2 + h % 2][:, 0:2 * VA].rearrange("p (b e) -> p b e", b=2)
                den = small[:, 1, 2 * h:2 * h + 2]
                ps = num[:, :, A_DH:VA].rearrange("p b e -> p (b e)")
                step(nc.vector.scalar_tensor_tensor(out=den, in0=ps, scalar=-1.0, in1=emm[:, :, h:h + 1].rearrange("p b e -> p (b e)"),
                                                    op0=ALU.mult, op1=ALU.max))
                step(nc.vector.tensor_tensor(den, ps, den, ALU.max))
                step(nc.vector.reciprocal(den, den))
                for b in range(NTB):
                    ins = nc.vector.tensor_scalar(hm[:, b, h * A_DH:(h + 1) * A_DH], num[:, b, 0:A_DH], den[:, b:b + 1], None,
                                                  ALU.mult)
                ins.then_inc(ml_h, 1)

            dve.wait_ge(gates_em, 1)
            for n in range(A_HEADS + 2):
                if n < A_HEADS:
                    decays(n)
                if 1 <= n <= A_HEADS:
                    weigh(n - 1)
                if n >= 2:
                    divide(n - 2)
            dve.wait_ge(ml_std, 1)
            step(nc.vector.reciprocal(small[:, 1, 0:8], small[:, 1, 0:8]))
            dve.wait_ge(ml_h, A_HEADS)
            for h in range(A_HEADS):
                for b in range(NTB):
                    hs = hm[:, b, h * A_DH:(h + 1) * A_DH]
                    ins = nc.vector.tensor_scalar(hs, hs, small[:, 1, 2 * h + b:2 * h + b + 1], None, ALU.mult)
            ins.then_inc(ml_hn, 1)
            for c in range(ACH + 1):
                if c < ACH:
                    dve.wait_ge(ml_t, c + 1)
                    if c == 0:
                        dve.wait_ge(gate_open, 1)
                    nc.vector.scalar_tensor_tensor(out=nrm[:, c, :], in0=pj[c % 2][:, 0:SEQ], scalar=cols(C_AHG, c),
                                                   in1=oT[:, c, :], op0=ALU.mult, op1=ALU.mult).then_inc(ml_y, 1)
                if c >= 1:
                    dve.wait_ge(ml_yhi, c)
                    nc.vector.tensor_tensor(act_lo[:, c - 1, :], nrm[:, c - 1, :], act_hi[:, c - 1, :],
                                            ALU.subtract).then_inc(ml_ylo, 1)
            for j in range(4):
                split_lo(T_AOUT + j + 2)
                residual(j, T_AOUT + 3, None)
            parts_of(1, C_FFN)
            sum_squares(1)
            ffn(0, True, 1)

            def ffn_residual(f, a=None, col=None):
                last = FFN_AT[f] + FFN_SLOTS - 1
                for j in range(5):
                    if j < 4:
                        residual(j, last, f)
                    if j and a is not None:
                        part(a, col, 2 * j - 2)
                        part(a, col, 2 * j - 1)

            split_lo(T_KV + 1)
            ffn_residual(0, 2, C_KV)
            sum_squares(2)
            projection(T_KV, 3, features_out(lambda j: qk[:, 6 + 2 * j:8 + 2 * j, :]), None, {0: lambda: deviation(2)})
            token_rstd(2)
            projection(T_KV + 3, 3, tokens_out(lambda j: vtok[:, :, j * COLS:(j + 1) * COLS]))
            parts_of(3, C_MIX + 8)
            projection(T_BIN, 3, features_out(lambda j: qk[:, 2 * j:2 * j + 2, :]))
            projection(T_BIN + 3, 1, features_out(lambda j: qm[:, :, :]))
            attention("band")
            for j in range(4):
                split_lo(T_BOUT + j + 2)
                residual(j, T_BOUT + 3, None)
            parts_of(4, C_FFN + 8)
            sum_squares(3)
            ffn(1, True, 3)
            split_lo(T_FF2 + 1)
            ffn_residual(1)

            deviation(4)
            for c in range(NCH):
                nc.vector.scalar_tensor_tensor(out=xT[:, c, :], in0=xT[:, c, :], scalar=cols(C_FINAL, c), in1=st[:, 0:SEQ],
                                               op0=ALU.mult, op1=ALU.mult).then_inc(x_ready, 1)
            parts_of(5, C_NG2)
            sum_squares(5)
            ffn(2, False, 5)
            ffn_post(6, C_NG2 + 8, T_AB - 1)
            parts_of(6, C_NG2 + 16)
            sum_squares(7)

            def take_u(t, j):
                if j == 0:
                    dve.wait_ge(evac_act, 2)
                    step(nc.vector.tensor_tensor(csg[:, 0:2, :], csg[:, 0:2, :], rstd2, ALU.mult))
                    step(nc.vector.tensor_tensor(csg[:, 2:4, :], csg[:, 2:4, :], rstd2, ALU.mult))
                nc.vector.tensor_tensor(apad[:, 2 * j:2 * j + 2, CONV_K - 1:], halves(t),
                                        csg[:, 2 * j:2 * j + 2, :], ALU.mult).then_inc(evac_dve, 1)

            def take_kv(t, j):
                nc.vector.tensor_tensor(qk[:, 4, :], pj[t % RING][:, 0:SEQ], rstd[:, :], ALU.mult).then_inc(k_ready, 1)
                for b in range(NTB):
                    ins = nc.vector.tensor_scalar(vtok[:, b, 0:P], pj[t % RING][:, SEQ + b * P:SEQ + (b + 1) * P],
                                                  rtok[:, b:b + 1], None, ALU.mult)
                ins.then_inc(evac_dve, 1)

            projection(T_AB, 2, before_sigmoid, None, {0: lambda: deviation(7)})
            token_rstd(3)
            projection(T_AB + 2, 2, take_u)
            projection(T_AB + 4, 2, features_out(lambda j: qk[:, 2 * j:2 * j + 2, :]))
            projection(T_AB + 6, 1, take_kv)
            dve.wait_ge(vec_const, 2)

            taps = [(c, j) for j in range(CONV_K) for c in range(DVE_CHUNKS)]

            def tap(c, j):
                src = apad[:, c, j:j + SEQ]
                if j == 0:
                    nc.vector.tensor_scalar(cv[:, c, :], src, cols(C_CW, c), cols(C_CB, c), ALU.mult, ALU.add).then_inc(cv_y, 1)
                else:
                    dve.wait_ge(cv_y, DVE_CHUNKS * (j - 1) + c + 1)
                    nc.vector.scalar_tensor_tensor(out=cv[:, c, :], in0=src, scalar=cols(C_CW, 4 * j + c), in1=cv[:, c, :],
                                                   op0=ALU.mult, op1=ALU.add).then_inc(cv_y, 1)

            def some_taps(k):
                for _ in range(min(k, len(taps))):
                    tap(*taps.pop(0))

            def beside(n):
                if n < 3:
                    some_taps(6)
                if n == 3:
                    dve.wait_ge(cv_mu, 1)
                    for c in range(CCH):
                        ins = nc.vector.tensor_tensor(cv[:, c, :], cv[:, c, :], acc[0][:, 0:SEQ], ALU.subtract)
                    ins.then_inc(cv_c, 1)
                if n == 5:
                    dve.wait_ge(cv_std, 1)
                    step(nc.vector.reciprocal(rstd[:, :], rstd[:, :]))
                    dve.wait_ge(cv_c, 1)
                    for c in range(CCH):
                        ins = nc.vector.tensor_tensor(cv[:, c, :], cv[:, c, :], rstd[:, :], ALU.mult)
                    ins.then_inc(cv_z, 1)

            some_taps(len(taps) - 18)
            attention("swa", beside)
            for c in range(CCH):
                dve.wait_ge(cv_hi, c + 1)
                nc.vector.tensor_tensor(act_lo[:, c, :], nrm[:, c, :], act_hi[:, c, :], ALU.subtract).then_inc(cv_lo, 1)

            def out_projection(first, n, col):
                for j in range(4):
                    split_lo(first + j + 2)
                    weigh_output(n, j, col)
                post(n, 1.0)

            out_projection(T_ABOUT, 8, C_NG2 + 24)
            parts_of(7, C_NG2 + 32)
            sum_squares(9)
            ffn(3, False, 9)
            ffn_post(10, C_NG2 + 40, T_FF4 - 1)
            parts_of(8, C_NG2 + 48)
            sum_squares(11)
            ffn(4, False, 11)
            ffn_post(12, C_NG2 + 56, T_FOX - 1)
            parts_of(9, C_NG2 + 64)
            dve.wait_ge(gw_split, 3)
            nc.vector.tensor_tensor(gw_lo[:, :, :], gw[:, :, :], gw_hi[:, :, :], ALU.subtract).then_inc(gw_split, 1)
            sum_squares(13)

            def f_sums():
                dve.wait_ge(gates_c, 2)
                nc.vector.tensor_scalar(c_sb[:, :, :], st[:, 64:64 + NTB * FOX_H].rearrange("p (b h) -> p b h", b=2), DH ** 0.5,
                                        None, ALU.mult).then_inc(gates_a, 1)

            def f_rows():
                dve.wait_ge(gates_t, 2)
                nc.vector.tensor_copy(pick[:, :], ident[0:FOX_H, 0:FOX_H])
                step(nc.vector.tensor_scalar(rowc[:, :], st[0:FOX_H, SEQ:2 * SEQ], -1.0, None, ALU.mult))
                step(nc.vector.tensor_copy(rowf[:, 0, :], rowc[:, :]))
                nc.vector.tensor_tensor(rowf[:, 1, :], rowc[:, :], rowf[:, 0, :], ALU.subtract).then_inc(gates_m, 1)

            def take(t):
                m, part = (t - T_FOX) // 3, (t - T_FOX) % 3
                dve.wait_ge(w_used, t + 1)
                if part < 2:
                    features_out(lambda j: qk[:, 8 * part + 2 * m:8 * part + 2 * m + 2, :])(t, m)
                else:
                    tokens_out(lambda j: vtok[:, :, m * COLS:(m + 1) * COLS])(t, m)

            split_lo(T_FOX + 2)
            deviation(13)
            take(T_FOX)
            split_lo(T_FOX + 3)
            token_rstd(4)
            take(T_FOX + 1)
            log_sigmoid(2, FOX_H, fox_b[:, :], 0)
            split_lo(T_FOX + 4)
            take(T_FOX + 2)
            f_sums()
            for m in range(1, 4):
                t, a, b = T_FOX + 3 * m, 2 * m - 2, 2 * m - 1
                split_lo(t + 2)
                if m == 1:
                    f_rows()
                take(t)
                scores("fox", a)
                split_lo(t + 3)
                probs("fox", a)
                scores("fox", b)
                take(t + 1)
                probs("fox", b)
                split_lo(t + 4)
                o_lo("fox", a)
                take(t + 2)
                o_lo("fox", b)
            for stage in (scores, probs, o_lo):
                stage("fox", 6)
                stage("fox", 7)
            out_projection(T_FOXOUT, 14, C_NG2 + 72)
            parts_of(10, C_NG2 + 80)
            sum_squares(15)
            ffn(5, False, 15)
            ffn_post(16, C_NG2 + 88, SLOTS - 1)

        @block.tensor
        def _(pe):
            def three(dst, w, a, start, stop):
                nc.tensor.matmul(dst, w[0], a[0], start=start, stop=False, skip_group_check=True)
                nc.tensor.matmul(dst, w[0], a[1], start=False, stop=False, skip_group_check=True)
                return nc.tensor.matmul(dst, w[1], a[0], start=False, stop=stop, skip_group_check=True)

            def weights(base, lo, n=P):
                r = base % RING
                return w_hi[:, r, lo:lo + n], w_lo[:, r, lo:lo + n]

            def acts(k, lo=0, n=SEQ):
                return act_hi[:, k, lo:lo + n], act_lo[:, k, lo:lo + n]

            def slot_ready(base, i=0):
                pe.wait_ge(lo_done, base + RING * i + 1)

            def out_acts(k):
                return fox_hi[:, k, :], fox_lo[:, k, :]

            def late_chunks(base, bank, late, ready, between=None, source=acts):
                slot_ready(base)
                order = [k for k in range(NCH) if k not in late] + list(late)
                for k in order:
                    if k == late[0] and between:
                        between()
                    if k in late:
                        ready(k)
                    for m in range(2):
                        ins = three(bank[:, m * SEQ:(m + 1) * SEQ], weights(base, k * COLS + m * P), source(k),
                                    start=k == order[0] and m == 0, stop=k == order[-1])
                return ins

            def feature_major(base, bank, i=0, widths=2, mid=None, source=acts):
                slot_ready(base, i)
                for m in range(widths):
                    if m and mid:
                        mid()
                    for k in range(NCH):
                        ins = three(bank[:, m * SEQ:(m + 1) * SEQ], weights(base, k * COLS + m * P), source(k),
                                    start=k == 0, stop=k == NCH - 1)
                return ins

            def token_major(base, bank, i=0, lo=0, n=COLS, at=0, ready=True, mid=None):
                if ready:
                    slot_ready(base, i)
                for b in range(NTB):
                    if b and mid:
                        mid()
                    for k in range(NCH):
                        ins = three(bank[:, at + b * n:at + (b + 1) * n], acts(k, b * P, P), weights(base, k * COLS + lo, n),
                                    start=k == 0, stop=k == NCH - 1)
                return ins

            def down(base, i=0, done=None):
                slot_ready(base, i)
                for c in range(NCH):
                    for k in range(2):
                        ins = three(acc[c // 2][:, c % 2 * SEQ:(c % 2 + 1) * SEQ], weights(base, k * D + c * P),
                                    (hid_hi[:, k, :], hid_lo[:, k, :]), start=False, stop=False)
                    if done and c % 2 and c < NCH - 1:
                        ins.then_inc(acc_done, 1)
                        done(c // 2)
                ins.then_inc(w_used, 1)

            def square_mean(n, j):
                pe.wait_ge(sq_done, NCH * n + 2 * j + 2)
                for c in (2 * j, 2 * j + 1):
                    for b in range(NTB):
                        ins = nc.tensor.matmul(st[:, SEQ + b:SEQ + b + 1], nrm[:, c, b * P:(b + 1) * P], mean_w[:, 0:1],
                                               start=c == 0 and b == 0, stop=c == NCH - 1, skip_group_check=True)
                if j == 3:
                    ins.then_inc(stat, 1)
                    pe.wait_ge(rstd_ready, n + 1)
                    for b in range(NTB):
                        ins = nc.tensor.matmul(st[:, b * P:(b + 1) * P], rtok[:, b:b + 1].to_broadcast([P, P]), ident[:, :],
                                               start=True, stop=True, skip_group_check=True)
                    ins.then_inc(rstd_spread, 1)

            def light_mean(n):
                pe.wait_ge(sq_sum, LIGHT.index(n) + 1)
                nc.tensor.matmul(st[:, 0:SEQ], mean_w[:, :], nrm[:, 0, :], start=True, stop=False)
                nc.tensor.matmul(st[:, 0:SEQ], mean_w[:, :], nrm[:, 1, :], start=False, stop=True).then_inc(stat, 1)

            def token_rstd(n):
                pe.wait_ge(rstd_ready, n + 1)
                for b in range(NTB):
                    ins = nc.tensor.matmul(st[:, SEQ + b:SEQ + b + 1], rstd[:, b * P:(b + 1) * P], ident[:, 0:1], start=True,
                                           stop=True, skip_group_check=True)
                ins.then_inc(tok_ps, 1)

            def first_slot(base, dst, a):
                slot_ready(base)
                for k in range(NCH):
                    pe.wait_ge(act_hi_done, NCH * a + k + 1)
                    for m in range(2):
                        w, d = weights(base, k * COLS + m * P), dst[:, m * SEQ:(m + 1) * SEQ]
                        nc.tensor.matmul(d, w[0], act_hi[:, k, :], start=k == 0 and m == 0, stop=False, skip_group_check=True)
                        nc.tensor.matmul(d, w[1], act_hi[:, k, :], start=False, stop=False, skip_group_check=True)
                for k in range(NCH):
                    pe.wait_ge(act_lo_done, NCH * a + k + 1)
                    for m in range(2):
                        ins = nc.tensor.matmul(dst[:, m * SEQ:(m + 1) * SEQ], w_hi[:, base % RING, k * COLS + m * P:k * COLS + (m + 1) * P],
                                               act_lo[:, k, :], start=False, stop=k == NCH - 1, skip_group_check=True)
                return ins

            HG_BEFORE = {3: 2, 4: 3, 5: 5}

            def ffn(f, a, u, n, heavy=None):
                t0 = FFN_AT[f]
                def clear():
                    if f in HG_BEFORE:
                        pe.wait_ge(hg_done, HG_BEFORE[f])
                    else:
                        pe.wait_ge(x_ready, NCH * (u + 1))
                    for j in range(4):
                        nc.tensor.matmul(acc[j][:, :], zero[:, 0:P], zero[:, :], start=True, stop=True)

                if f >= 2:
                    clear()
                first_slot(t0, pj[t0 % RING], a).then_inc(w_used, 1)
                if f < 2:
                    clear()
                light_mean(n)
                feature_major(t0 + 1, pj[(t0 + 1) % RING]).then_inc(w_used, 1)
                with pe.Fori(1, STEPS) as i:
                    pe.wait_ge(ff_raw, STEPS * f + i)
                    feature_major(t0 - 1, pj[(t0 - 1) % RING], i).then_inc(w_used, 1)
                    pe.wait_ge(ff_up, STEPS * f + i)
                    feature_major(t0, pj[t0 % RING], i).then_inc(w_used, 1)
                    pe.wait_ge(ff_lo, STEPS * f + i)
                    down(t0 + 1, i)
                pe.wait_ge(ff_lo, STEPS * (f + 1))

                def done(j):
                    if heavy and j == 2:
                        square_mean(heavy, 0)

                down(t0 + RING * STEPS - 1, 0, done)
                if heavy:
                    for j in (1, 2, 3):
                        square_mean(heavy, j)

            def project(first, n, form, a=None, after=None):
                for t in range(first, first + n):
                    if t - RING in evac_of:
                        evacuated(pe, t - RING)
                    if a is not None and t == first:
                        first_slot(t, pj[t % RING], a).then_inc(w_used, 1)
                    else:
                        form(t, pj[t % RING]).then_inc(w_used, 1)
                    if after and t - first in after:
                        after[t - first]()

            def project_out(first, heavy=None, late=None, ready=None, between=None, source=acts):
                for j in range(4):
                    if late and j == 0:
                        late_chunks(first, acc[0], late, ready, between, source).then_inc(w_used, 1)
                    else:
                        feature_major(first + j, acc[j], source=source).then_inc(w_used, 1)
                    if heavy and j:
                        square_mean(heavy, j - 1)
                if heavy:
                    square_mean(heavy, 3)

            def head_qk(kind, h):
                rows = slice(DH * (h % 2), DH * (h % 2) + DH)
                if kind == "band":
                    return qk[rows, h // 2, :], qk[rows, 6 + h // 2, :]
                if kind == "fox":
                    return qk[rows, h // 2, :], qk[rows, 8 + h // 2, :]
                if kind == "swa":
                    keys = qk[rows, 4, :] if h // 4 == h % 2 else kswap[rows, :]
                    return qk[rows, h // 2, :], keys
                return qm[rows, h // 2, :], mk[rows, int(kind[3]), h // 2, :]

            def head_v(kind, h, b):
                if kind.startswith("mem"):
                    return mv[:, int(kind[3]), b, h * DH:(h + 1) * DH]
                if kind == "swa":
                    h = h // 4
                return vtok[:, b, h * DH:(h + 1) * DH]

            def scores(phase, n):
                kind, h0, _ = PAIRS[phase][n]
                g = PAIR0[phase] + n
                if before[g]:
                    pe.wait_ge(h_olo, before[g])
                for half in range(2):
                    h = h0 + half
                    q, k = head_qk(kind, h)
                    dst = place[g][:, half * 512:(half + 1) * 512]
                    for b, (lo, hi) in enumerate(cuts(kind)):
                        ins = nc.tensor.matmul(dst[:, lo:hi], q[:, b * P:(b + 1) * P], k[:, 0:hi - lo], start=True,
                                               stop=kind not in ("fox", "band"), skip_group_check=True)
                        if kind == "fox":
                            for part in range(2):
                                ins = nc.tensor.matmul(dst[:, lo:hi], pick[:, h:h + 1].to_broadcast([FOX_H, P]),
                                                       rowf[:, part, 0:hi - lo], start=False, stop=part == 1,
                                                       skip_group_check=True)
                        if kind == "band":
                            ins = nc.tensor.matmul(dst[:, lo:hi], turn8[:, :], relb[:, h, lo:hi], start=False, stop=True,
                                                   skip_group_check=True)
                ins.then_inc(h_s, 1)

            def turns(phase, n):
                kind, _, _ = PAIRS[phase][n]
                g = PAIR0[phase] + n
                pe.wait_ge(h_p, g + 1)
                blocks = [(0, 0), (256, 128), (128, 256), (384, 384)] if kind.startswith("mem") else \
                    [(0, 0), (128, 128), (256, 256)]
                for half in range(2):
                    for src, dst in blocks:
                        ins = nc.tensor.transpose(place[g][:, half * 512 + dst:half * 512 + dst + P],
                                                  p_sb[:, g % 2, half * 512 + src:half * 512 + src + P], ident[:, :])
                ins.then_inc(h_pt, 1)

            def values(phase, n):
                kind, h0, _ = PAIRS[phase][n]
                g = PAIR0[phase] + n
                pe.wait_ge(h_ptc, g + 1)
                for half in range(2):
                    dst = place[g][DH * half:DH * (half + 1), :]
                    pt = pt_sb[:, g % 2, half * 512:(half + 1) * 512]
                    nc.tensor.matmul(dst[:, 0:SEQ], head_v(kind, h0 + half, 0), pt[:, 0:SEQ], start=True, stop=False,
                                     skip_group_check=True)
                    first = 0 if kind.startswith("mem") else P
                    ins = nc.tensor.matmul(dst[:, first:SEQ], head_v(kind, h0 + half, 1), pt[:, SEQ:2 * SEQ - first],
                                           start=False, stop=True, skip_group_check=True)
                ins.then_inc(h_o, 1)

            def attention(phase, between=None):
                last = len(PAIRS[phase])
                for n in range(last + 2):
                    if n < last:
                        scores(phase, n)
                    if 1 <= n <= last:
                        turns(phase, n - 1)
                    if n >= 2:
                        values(phase, n - 2)
                    if between:
                        between(n)
                pe.wait_ge(h_olo, PAIR0[phase] + last)

            def narrow(width, n):
                pe.wait_ge(tok_ready, n)
                for b in range(NTB):
                    for k in range(NCH):
                        ins = three(st[:, b * width:(b + 1) * width], acts(k, b * P, P),
                                    (gw_hi[:, k, 0:width], gw_lo[:, k, 0:width]), start=k == 0, stop=k == NCH - 1)
                ins.then_inc(gates_ps, 1)

            def cumulate(n, k):
                pe.wait_ge(gates_lf, n)
                nc.tensor.matmul(st[:, 64:64 + k], tri[:, 0:P], lf_sb[:, 0, 0:k], start=True, stop=True)
                nc.tensor.matmul(st[:, 64 + k:64 + 2 * k], tri[:, P:2 * P], lf_sb[:, 0, 0:k], start=True, stop=False)
                nc.tensor.matmul(st[:, 64 + k:64 + 2 * k], tri[:, 0:P], lf_sb[:, 1, 0:k], start=False, stop=True).then_inc(gates_c, 1)

            def slot(t, form, mid=None, after=None):
                evacuated(pe, t - RING) if t - RING in evac_of else None
                form(t, pj[t % RING], mid=mid).then_inc(w_used, 1)
                if after:
                    after()

            pe.wait_ge(ident_ready, 2)
            tok = [qk[:, 0:8, :].rearrange("p (b c) t -> p b (c t)", b=NTB), qk[:, 8:16, :].rearrange("p (b c) t -> p b (c t)", b=NTB)]

            def turn_tokens(n):
                pe.wait_ge(tokens_in[n], 16)
                for j in range(4):
                    if n:
                        pe.wait_ge(mem_lo, j + 1)
                    for c in range(2):
                        for b in range(NTB):
                            ins = nc.tensor.transpose(acc[j][:, c * SEQ + b * P:c * SEQ + (b + 1) * P],
                                                      tok[n][:, b, (2 * j + c) * P:(2 * j + c + 1) * P], ident[:, :])
                    ins.then_inc(in_t, 1)

            def turn_params():
                pe.wait_ge(params_in, 16 * 16)
                pe.wait_ge(x_ready, 2)
                for n in range(PARAM_TILES):
                    ins = nc.tensor.transpose((st if n < 4 else acc[0])[:, n % 4 * P:(n % 4 + 1) * P], prow[:, n, :], ident[:, :])
                    if n in (3, 4):
                        ins.then_inc(in_t, 1)

            turn_tokens(0)
            pe.wait_ge(mem_lo, 4)
            project(T_MEM, 1, feature_major, None, {0: lambda: turn_tokens(1)})
            project(T_MEM + 1, 1, token_major, None, {0: turn_params})
            project(T_MEM + 2, 1, feature_major)
            project(T_MEM + 3, 1, token_major)
            pe.wait_ge(consts, 6)

            def a_turn():
                pe.wait_ge(gates_a, 1)
                for b in range(NTB):
                    ins = nc.tensor.transpose(st[0:A_HEADS, SEQ + b * P:SEQ + (b + 1) * P], a_tok[:, b, :], ident[:, :])
                ins.then_inc(gates_t, 1)

            def a_back():
                pe.wait_ge(gates_m, 1)
                for b in range(NTB):
                    ins = nc.tensor.matmul(st[:, 128 + 4 * b:132 + 4 * b], cum[:, 0, P + b * P:P + (b + 1) * P],
                                           ident[0:A_HEADS, 0:A_HEADS], start=True, stop=True, skip_group_check=True)
                ins.then_inc(gates_mt, 1)

            pe.wait_ge(gw_split, 2)
            project(T_AQK, 6, feature_major, 0, {0: lambda: light_mean(0), 1: lambda: token_rstd(0), 5: lambda: narrow(8, 1)})
            project(T_AV, 3, token_major, None, {1: lambda: cumulate(1, 4), 2: a_turn})
            project(T_AQM, 1, feature_major)
            slot(T_AO, feature_major)
            evacuated(pe, T_AQM)
            scores("a_mem", 0)
            a_back()
            slot(T_AO + 1, feature_major, lambda: scores("a_mem", 1), lambda: turns("a_mem", 0))
            slot(T_AO + 2, feature_major, lambda: (values("a_mem", 0), turns("a_mem", 1)), lambda: values("a_mem", 1))
            for t in range(T_AO, T_AO + 3):
                evacuated(pe, t)

            def spread(h):
                if h >= 2:
                    pe.wait_ge(ml_x, h - 1)
                nc.tensor.matmul(pj[h % 2][:, 0:SEQ], ident[0:A_HEADS, h:h + 1].to_broadcast([A_HEADS, P]), rowc[0:A_HEADS, :], start=True, stop=True).then_inc(ml_bc, 1)

            def keys_queries(h):
                if h >= 2:
                    pe.wait_ge(ml_p, h - 1)
                pieces = a_head_rows(h)
                for lo, n, s0, t0 in ((0, SEQ, 0, 0), (SEQ, P, P, P)):
                    for i, (c, r0, rows) in enumerate(pieces):
                        rs = slice(r0, r0 + rows)
                        ins = nc.tensor.matmul(acc[h % 2][:, lo:lo + n], qk[rs, ACH + c, s0:s0 + P], qk[rs, c, t0:t0 + n],
                                               start=i == 0, stop=i == len(pieces) - 1, skip_group_check=True)
                ins.then_inc(ml_s, 1)

            def numerator(h):
                pe.wait_ge(ml_p, h + 1)
                if h >= 2:
                    pe.wait_ge(ml_h, h - 1)
                bank = acc[2 + h % 2]
                nc.tensor.matmul(bank[:, 0:VA], pt_sb[:, h % 2, 0:P], vaug[:, 0, h, :], start=True, stop=True, skip_group_check=True)
                nc.tensor.matmul(bank[:, VA:2 * VA], pt_sb[:, h % 2, P:2 * P], vaug[:, 0, h, :], start=True, stop=False, skip_group_check=True)
                nc.tensor.matmul(bank[:, VA:2 * VA], pt_sb[:, h % 2, 2 * P:3 * P], vaug[:, 1, h, :], start=False, stop=True,
                                 skip_group_check=True).then_inc(ml_num, 1)

            pe.wait_ge(qk_act, 6)
            for n in range(A_HEADS + 1):
                if n < A_HEADS:
                    if n == 0:
                        pe.wait_ge(h_olo, 2)
                    spread(n)
                    keys_queries(n)
                if n >= 1:
                    numerator(n - 1)
            pe.wait_ge(ml_hn, 1)
            for c in range(ACH):
                if c >= 2:
                    pe.wait_ge(ml_y, c - 1)
                for b in range(NTB):
                    ins = nc.tensor.transpose(pj[c % 2][:, b * P:(b + 1) * P], hm[:, b, c * P:(c + 1) * P], ident[:, :])
                ins.then_inc(ml_t, 1)
            project_out(T_AOUT, late=range(ACH), ready=lambda c: pe.wait_ge(ml_ylo, c + 1), source=lambda k: out_parts("mem0", k) if k >= ACH else acts(k))
            ffn(0, 1, 1, 1)

            project(T_KV, 3, feature_major, 2, {0: lambda: light_mean(2), 1: lambda: token_rstd(2)})
            project(T_KV + 3, 3, token_major)
            project(T_BIN, 4, feature_major, 3)
            for t in range(T_BIN + 1, T_BIN + 4):
                evacuated(pe, t)
            pe.wait_ge(vec_const, 1)
            attention("band")
            project_out(T_BOUT)
            ffn(1, 4, 3, 3, heavy=4)
            ffn(2, 5, 4, 5, heavy=6)

            def keys_values(base, bank):
                feature_major(base, bank, widths=1)
                return token_major(base, bank, lo=P, n=P, at=SEQ, ready=False)

            project(T_AB, 6, feature_major, 6, {0: lambda: light_mean(7), 1: lambda: token_rstd(7)})
            project(T_AB + 6, 1, keys_values)

            def conv_taps(i, lo, hi):
                for j in range(lo, hi):
                    pe.wait_ge(diags, CONV_K * i + j + 1)
                    ins = nc.tensor.matmul(acc[i][:, 0:SEQ], diag(j), apad[:, PE_CHUNKS[i], j:j + SEQ], start=j == 0,
                                           stop=j == CONV_K - 1, skip_group_check=True)
                    if j < CONV_K - 1:
                        ins.then_inc(cv_tap, 1)
                    else:
                        ins.then_inc(cv_pe, 1)

            def beside(n):
                if n < 3:
                    conv_taps(1, 11 * n, min(11 * n + 11, CONV_K))
                if n == 3:
                    pe.wait_ge(cv_pe_out, 2)
                    pe.wait_ge(cv_y, DVE_CHUNKS * CONV_K)
                    for c in range(CCH):
                        ins = nc.tensor.matmul(acc[0][:, 0:SEQ], mean_c[:, :], cv[:, c, :], start=c == 0, stop=c == CCH - 1)
                    ins.then_inc(cv_mu, 1)
                if n == 4:
                    for c in range(CCH):
                        pe.wait_ge(cv_sq, c + 1)
                        ins = nc.tensor.matmul(acc[1][:, 0:SEQ], mean_c[:, :], nrm[:, c, :], start=c == 0, stop=c == CCH - 1)
                    ins.then_inc(cv_var, 1)

            evacuated(pe, T_AB + 3)
            pe.wait_ge(vec_const, 2)
            conv_taps(0, 0, CONV_K)
            for t in range(T_AB + 4, T_AB + 7):
                evacuated(pe, t)
            pe.wait_ge(kswap_in, 32)
            attention("swa", beside)
            pe.wait_ge(cv_c, 1)
            project_out(T_ABOUT, heavy=8, late=range(CCH), ready=lambda c: pe.wait_ge(cv_lo, c + 1))
            ffn(3, 7, 7, 9, heavy=10)
            ffn(4, 8, 8, 11, heavy=12)

            def f_turn():
                pe.wait_ge(gates_a, 2)
                for b in range(NTB):
                    ins = nc.tensor.transpose(st[0:FOX_H, SEQ + b * P:SEQ + (b + 1) * P], c_sb[:, b, :], ident[:, :])
                ins.then_inc(gates_t, 1)

            project(T_FOX, 1, feature_major, 9, {0: lambda: light_mean(13)})
            slot(T_FOX + 1, feature_major, lambda: token_rstd(13), lambda: (pe.wait_ge(gw_split, 4), narrow(FOX_H, 4)))
            slot(T_FOX + 2, token_major, None, lambda: cumulate(2, FOX_H))
            for m in range(1, 4):
                t, a, b = T_FOX + 3 * m, 2 * m - 2, 2 * m - 1
                slot(t, feature_major, f_turn if m == 1 else None)
                if m == 1:
                    pe.wait_ge(gates_m, 2)
                evacuated(pe, t - 1)
                scores("fox", a)
                slot(t + 1, feature_major, lambda: scores("fox", b), lambda: turns("fox", a))
                slot(t + 2, token_major, lambda: (values("fox", a), turns("fox", b)), lambda: values("fox", b))
            for t in range(T_FOX + 9, T_FOX + 12):
                evacuated(pe, t)
            scores("fox", 6)
            scores("fox", 7)
            pe.wait_ge(h_olo, PAIR0["fox"] + 6)

            def last_pairs():
                for stage in (turns, values):
                    stage("fox", 6)
                    stage("fox", 7)

            project_out(T_FOXOUT, heavy=14, late=(6, 7), ready=lambda c: pe.wait_ge(h_olo, PAIR0["fox"] + c + 1),
                        between=last_pairs, source=out_acts)
            ffn(5, 10, 10, 15, heavy=16)
            for q in range(2):
                for b in range(NTB):
                    for c in range(4):
                        pe.wait_ge(x_ready, NCH * 11 + 4 * q + c + 1)
                        ins = nc.tensor.transpose(acc[2 * b + q][:, c * P:(c + 1) * P], xT[:, 4 * q + c, b * P:(b + 1) * P], ident[:, :])
                    ins.then_inc(out_t, 1)


INPUTS = ["x", "mem", "norm_mix_g", "norm_ffn_g", "a_w_in", "a_gate_b", "a_conv_w", "a_conv_b", "a_head_g", "a_w_out",
          "kv_norm_g", "w_kv", "b_w_in", "b_rel_bias", "b_w_out", "mem_w_kv", "ffn_w_up", "ffn_conv_w", "ffn_conv_b",
          "ffn_w_down", "final_g", "norm_g_2", "ffn_w_gate_2", "ffn_w_up_2", "ffn_w_down_2", "ab_w_in_2", "conv_w_2",
          "conv_b_2", "conv_ln_g_2", "conv_ln_b_2", "swa_sinks_2", "ab_w_out_2", "fox_w_in_2", "fox_b_f_2", "fox_w_out_2"]


def kernel(**inputs):
    import numpy as np
    import concourse.bacc as bacc
    from concourse.bass_utils import run_bass_kernel_spmd

    nc = bacc.Bacc("TRN2", target_bir_lowering=False, num_devices=1)
    arrays, args = {}, []
    for name in INPUTS:
        a = np.ascontiguousarray(inputs[name])
        arrays[f"in_{name}"] = a
        args.append(nc.dram_tensor(f"in_{name}", a.shape, mybir.dt.from_np(a.dtype), kind="ExternalInput").ap())
    args.append(nc.dram_tensor("out_x", (1, SEQ, D), F32, kind="ExternalOutput").ap())
    build(nc, *args)
    r = run_bass_kernel_spmd(nc, [arrays], core_ids=[0])
    return r.results[0]["out_x"]
```
